# Optimizing a Trainium2 kernel written in Bass

```python
import jax
import jax.numpy as jnp
from jax import lax
import numpy as np
import jax, jax.numpy as jnp

D_MODEL = 1024
BATCH = 1
SEQ = 256
DEPTH = 2

GRID_W = 64
CTX_LEN = 256
N_EVEN = (DEPTH + 1) // 2
N_ODD = DEPTH // 2
D_FF = 4 * D_MODEL
N_MOD = 6
EPS = 1e-6
F32 = jnp.float32

MLA_HEADS = 8
MLA_NOPE = 64
MLA_ROPE = 32
MLA_V = 64
MLA_QK = MLA_NOPE + MLA_ROPE
MLA_Q_RANK = 3 * D_MODEL // 8
MLA_KV_RANK = D_MODEL // 4
ROPE_THETA = 10000.0
Q_BLOCK = 128

GLA_HEADS = 4
GLA_DK = 64
GLA_DV = 128
GLA_GATE_RANK = 16
GLA_GATE_NORM = 16.0
GLA_CHUNK = 64

GDN_HEADS = 8
GDN_DK = 64
GDN_DV = 128
GDN_CONV = 3
GDN_CHUNK = 64

EVEN_SPLITS = (MLA_Q_RANK, MLA_KV_RANK, MLA_ROPE,
               GLA_HEADS * GLA_DK, GLA_HEADS * GLA_DK, GLA_HEADS * GLA_DV, GLA_HEADS * GLA_DV,
               2 * GLA_GATE_RANK)
EVEN_IN = 2240
MIX_WIDTH = MLA_HEADS * MLA_V + GLA_HEADS * GLA_DV
GDN_QKV = 2 * GDN_HEADS * GDN_DK + GDN_HEADS * GDN_DV
ODD_SPLITS = (GDN_QKV, GDN_HEADS * GDN_DV, 2 * GDN_HEADS, 2 * GDN_HEADS)
ODD_IN = 3104
GDN_WIDTH = GDN_HEADS * GDN_DV


def rms_norm(x, w):
    xf = x.astype(F32)
    y = xf * lax.rsqrt(jnp.mean(xf * xf, axis=-1, keepdims=True) + EPS)
    return (y * w.astype(F32)).astype(x.dtype)

def l2norm(t):
    tf = t.astype(F32)
    return (tf * lax.rsqrt(jnp.sum(tf * tf, axis=-1, keepdims=True) + EPS)).astype(t.dtype)

def split_cols(y, sizes):
    out, start = [], 0
    for s in sizes:
        out.append(y[..., start:start + s])
        start += s
    return out

def modulate(h, shift, scale):
    return h * (1.0 + scale) + shift

def flip_seq(ts):
    return tuple(jnp.flip(t, axis=2) for t in ts)

def axial_rope_tables(n_tokens):
    rows = n_tokens // GRID_W
    row = jnp.repeat(jnp.arange(rows, dtype=F32), GRID_W)
    col = jnp.tile(jnp.arange(GRID_W, dtype=F32), rows)
    axis_dim = MLA_ROPE // 2
    inv_freq = ROPE_THETA ** (-jnp.arange(0, axis_dim, 2, dtype=F32) / axis_dim)
    ang = jnp.concatenate([row[:, None] * inv_freq, col[:, None] * inv_freq], axis=-1)
    return jnp.cos(ang), jnp.sin(ang)

def apply_axial_rope(x, cos, sin):
    shp = x.shape
    nf = MLA_ROPE // 4
    xf = x.astype(F32).reshape(shp[:-1] + (2, 2, nf))
    x1, x2 = xf[..., 0, :], xf[..., 1, :]
    cos = cos.reshape(-1, 2, nf)
    sin = sin.reshape(-1, 2, nf)
    out = jnp.stack([x1 * cos - x2 * sin, x2 * cos + x1 * sin], axis=-2)
    return out.reshape(shp).astype(x.dtype)

def mla_attend(q, k, v):
    B, H, Lq, D = q.shape
    scale = MLA_QK ** -0.5
    nb = Lq // Q_BLOCK
    qb = jnp.moveaxis(q.reshape(B, H, nb, Q_BLOCK, D), 2, 0)

    def one(qblk):
        s = jnp.einsum('bhqd,bhkd->bhqk', qblk, k).astype(F32) * scale
        p = jax.nn.softmax(s, axis=-1).astype(v.dtype)
        return jnp.einsum('bhqk,bhkv->bhqv', p, v)

    o = lax.map(one, qb)
    return jnp.moveaxis(o, 0, 2).reshape(B, H, Lq, v.shape[-1])

def gla_chunked(q, k, v, logg, s0):
    out_dtype = v.dtype
    q, k, v, logg = (t.astype(F32) for t in (q, k, v, logg))
    B, H, L, DK = q.shape
    DV = v.shape[-1]
    C = GLA_CHUNK
    n = L // C
    q = q.reshape(B, H, n, C, DK) * DK ** -0.5
    k = k.reshape(B, H, n, C, DK)
    v = v.reshape(B, H, n, C, DV)
    b = jnp.cumsum(logg.reshape(B, H, n, C, DK), axis=3)
    q_dec = q * jnp.exp(b)
    k_inv = k * jnp.exp(-b)
    k_end = k * jnp.exp(b[..., -1:, :] - b)
    g_end = jnp.exp(b[..., -1, :])
    incl = jnp.tril(jnp.ones((C, C), bool))
    a = jnp.where(incl, jnp.einsum('bhnid,bhnjd->bhnij', q_dec, k_inv), 0.0)
    o_intra = jnp.einsum('bhnij,bhnjv->bhniv', a, v)

    def step(s, xs):
        qd_c, ke_c, v_c, ge_c = xs
        o = jnp.einsum('bhcd,bhdv->bhcv', qd_c, s)
        s = s * ge_c[..., None] + jnp.einsum('bhcd,bhcv->bhdv', ke_c, v_c)
        return s, o

    xs = tuple(jnp.moveaxis(t, 2, 0) for t in (q_dec, k_end, v, g_end))
    s_fin, o_inter = lax.scan(step, s0, xs)
    o = o_intra + jnp.moveaxis(o_inter, 0, 2)
    return o.reshape(B, H, L, DV).astype(out_dtype), s_fin

def gdn_chunked(q, k, v, log_a, beta, s0):
    out_dtype = v.dtype
    q, k, v, log_a, beta = (t.astype(F32) for t in (q, k, v, log_a, beta))
    B, H, L, DK = q.shape
    DV = v.shape[-1]
    C = GDN_CHUNK
    n = L // C
    q = q.reshape(B, H, n, C, DK) * DK ** -0.5
    k = k.reshape(B, H, n, C, DK)
    v = v.reshape(B, H, n, C, DV)
    beta = beta.reshape(B, H, n, C)[..., None]
    g = jnp.cumsum(log_a.reshape(B, H, n, C), axis=-1)
    incl = jnp.tril(jnp.ones((C, C), bool))
    strict = jnp.tril(jnp.ones((C, C), bool), -1)
    diff = g[..., :, None] - g[..., None, :]
    decay = jnp.where(incl, jnp.exp(jnp.where(incl, diff, 0.0)), 0.0)
    kb = k * beta
    a_mat = jnp.where(strict, jnp.einsum('bhnid,bhnjd->bhnij', kb, k) * decay, 0.0) + jnp.eye(C, dtype=F32)
    rhs = jnp.concatenate([v * beta, kb * jnp.exp(g)[..., None]], axis=-1)
    sol = lax.linalg.triangular_solve(a_mat, rhs, left_side=True, lower=True)
    u, w = sol[..., :DV], sol[..., DV:]
    qk = jnp.einsum('bhnid,bhnjd->bhnij', q, k) * decay
    q_dec = q * jnp.exp(g)[..., None]
    k_end = k * jnp.exp(g[..., -1:] - g)[..., None]
    g_end = jnp.exp(g[..., -1])

    def step(s, xs):
        qk_c, qd_c, w_c, u_c, ke_c, ge_c = xs
        v_new = u_c - jnp.einsum('bhcd,bhdv->bhcv', w_c, s)
        o = jnp.einsum('bhcd,bhdv->bhcv', qd_c, s) + jnp.einsum('bhcs,bhsv->bhcv', qk_c, v_new)
        s = s * ge_c[..., None, None] + jnp.einsum('bhcd,bhcv->bhdv', ke_c, v_new)
        return s, o

    xs = tuple(jnp.moveaxis(t, 2, 0) for t in (qk, q_dec, w, u, k_end, g_end))
    s_fin, o = lax.scan(step, s0, xs)
    o = jnp.moveaxis(o, 0, 2).reshape(B, H, L, DV)
    return o.astype(out_dtype), s_fin

def bidir_scan(scan_fn, ctx_f, ctx_b, lat_f, lat_b, s0):
    o_cf, s_f = scan_fn(*ctx_f, s0)
    o_cb, s_b = scan_fn(*flip_seq(ctx_b), s0)
    o_lf, _ = scan_fn(*lat_f, s_f)
    o_lb, _ = scan_fn(*flip_seq(lat_b), s_b)
    return o_lf + jnp.flip(o_lb, axis=2), (o_cf, o_cb)

def even_project(y, q_norm, w_uq, kv_norm, w_ukv, gate_up, gate_bias, rope):
    cq, ckv, kpe, gq, gk, gv, gg, glow = split_cols(y, EVEN_SPLITS)
    B, L, _ = y.shape
    q = (rms_norm(cq, q_norm) @ w_uq).reshape(B, L, MLA_HEADS, MLA_QK).transpose(0, 2, 1, 3)
    q_nope, q_pe = q[..., :MLA_NOPE], q[..., MLA_NOPE:]
    kv = (rms_norm(ckv, kv_norm) @ w_ukv).reshape(B, L, MLA_HEADS, MLA_NOPE + MLA_V).transpose(0, 2, 1, 3)
    k_nope, mv = kv[..., :MLA_NOPE], kv[..., MLA_NOPE:]
    if rope is not None:
        q_pe = apply_axial_rope(q_pe, *rope)
        kpe = apply_axial_rope(kpe, *rope)
    mq = jnp.concatenate([q_nope, q_pe], axis=-1)
    mk = jnp.concatenate([k_nope, jnp.broadcast_to(kpe[:, None], (B, MLA_HEADS, L, MLA_ROPE))], axis=-1)
    glow = glow.reshape(B, L, 2, GLA_GATE_RANK)
    logit = jnp.einsum('blzr,zrk->zblk', glow, gate_up) + gate_bias[:, None, None, :]
    logg = jax.nn.log_sigmoid(logit.astype(F32)) / GLA_GATE_NORM
    logg = logg.reshape(2, B, L, GLA_HEADS, GLA_DK).transpose(0, 1, 3, 2, 4)
    heads = lambda t, d: t.reshape(B, L, -1, d).transpose(0, 2, 1, 3)
    return (mq, mk, mv, heads(gq, GLA_DK), heads(gk, GLA_DK), heads(gv, GLA_DV), gg, logg[0], logg[1])

def even_merge(att, gla, gg, o_norm, w_out):
    B, _, L, _ = att.shape
    att = att.transpose(0, 2, 1, 3).reshape(B, L, MLA_HEADS * MLA_V)
    gla = rms_norm(gla.transpose(0, 2, 1, 3), o_norm) * jax.nn.silu(gg.reshape(B, L, GLA_HEADS, GLA_DV))
    return jnp.concatenate([att, gla.reshape(B, L, GLA_HEADS * GLA_DV)], axis=-1) @ w_out

def even_mixer(a_lat, a_ctx, w_in, q_norm, w_uq, kv_norm, w_ukv, gate_up, gate_bias, o_norm, w_out, rope, need_ctx):
    mq_l, mk_l, mv_l, gq_l, gk_l, gv_l, gg_l, lf_l, lb_l = even_project(
        a_lat @ w_in, q_norm, w_uq, kv_norm, w_ukv, gate_up, gate_bias, rope)
    mq_c, mk_c, mv_c, gq_c, gk_c, gv_c, gg_c, lf_c, lb_c = even_project(
        a_ctx @ w_in, q_norm, w_uq, kv_norm, w_ukv, gate_up, gate_bias, None)
    att_l = mla_attend(mq_l, jnp.concatenate([mk_l, mk_c], axis=2), jnp.concatenate([mv_l, mv_c], axis=2))
    B = a_lat.shape[0]
    s0 = jnp.zeros((B, GLA_HEADS, GLA_DK, GLA_DV), F32)
    gla_l, (o_cf, o_cb) = bidir_scan(gla_chunked, (gq_c, gk_c, gv_c, lf_c), (gq_c, gk_c, gv_c, lb_c),
                                     (gq_l, gk_l, gv_l, lf_l), (gq_l, gk_l, gv_l, lb_l), s0)
    o_lat = even_merge(att_l, gla_l, gg_l, o_norm, w_out)
    o_ctx = None
    if need_ctx:
        att_c = mla_attend(mq_c, mk_c, mv_c)
        o_ctx = even_merge(att_c, o_cf + jnp.flip(o_cb, axis=2), gg_c, o_norm, w_out)
    return o_lat, o_ctx

def short_conv(x, w):
    ch = x.shape[-1]
    y = lax.conv_general_dilated(x, w[:, None, :], window_strides=(1,),
                                 padding=[((GDN_CONV - 1) // 2, GDN_CONV // 2)],
                                 dimension_numbers=('NWC', 'WIO', 'NWC'), feature_group_count=ch)
    return jax.nn.silu(y)

def odd_project(a, w_in, conv_w, a_log, dt_bias):
    B, L, _ = a.shape
    qkv, g, a_in, b_in = split_cols(a @ w_in, ODD_SPLITS)
    q, k, v = split_cols(short_conv(qkv, conv_w), (GDN_HEADS * GDN_DK, GDN_HEADS * GDN_DK, GDN_HEADS * GDN_DV))
    heads = lambda t, d: t.reshape(B, L, GDN_HEADS, d).transpose(0, 2, 1, 3)
    q = l2norm(heads(q, GDN_DK))
    k = l2norm(heads(k, GDN_DK))
    v = heads(v, GDN_DV)
    a_in = a_in.reshape(B, L, 2, GDN_HEADS).astype(F32)
    log_a = -jnp.exp(a_log.astype(F32)) * jax.nn.softplus(a_in + dt_bias.astype(F32))
    beta = jax.nn.sigmoid(b_in.reshape(B, L, 2, GDN_HEADS).astype(F32))
    return q, k, v, g, log_a.transpose(2, 0, 3, 1), beta.transpose(2, 0, 3, 1)

def odd_merge(o, g, o_norm, w_out):
    B, _, L, _ = o.shape
    o = rms_norm(o.transpose(0, 2, 1, 3), o_norm) * jax.nn.silu(g.reshape(B, L, GDN_HEADS, GDN_DV))
    return o.reshape(B, L, GDN_WIDTH) @ w_out

def odd_mixer(a_lat, a_ctx, w_in, conv_w, a_log, dt_bias, o_norm, w_out, need_ctx):
    lq, lk, lv, lg, lla, lbe = odd_project(a_lat, w_in, conv_w, a_log, dt_bias)
    cq, ck, cv, cg, cla, cbe = odd_project(a_ctx, w_in, conv_w, a_log, dt_bias)
    B = a_lat.shape[0]
    s0 = jnp.zeros((B, GDN_HEADS, GDN_DK, GDN_DV), F32)
    o_l, (o_cf, o_cb) = bidir_scan(gdn_chunked, (cq, ck, cv, cla[0], cbe[0]), (cq, ck, cv, cla[1], cbe[1]),
                                   (lq, lk, lv, lla[0], lbe[0]), (lq, lk, lv, lla[1], lbe[1]), s0)
    o_lat = odd_merge(o_l, lg, o_norm, w_out)
    o_ctx = None
    if need_ctx:
        o_ctx = odd_merge(o_cf + jnp.flip(o_cb, axis=2), cg, o_norm, w_out)
    return o_lat, o_ctx

def sq_relu_mlp(h, w1, w2):
    return jnp.square(jax.nn.relu(h @ w1)) @ w2

def first_inputs(seed: int = 0) -> dict:
    key = jax.random.key(seed)
    ks = iter(jax.random.split(key, 40))
    nrm = lambda shape, scale: jax.random.normal(next(ks), shape, F32) * scale
    gain = lambda shape: 1.0 + 0.05 * jax.random.normal(next(ks), shape, F32)
    d = D_MODEL
    dt = jnp.exp(jax.random.uniform(next(ks), (N_ODD, 2, GDN_HEADS), F32, np.log(1e-3), np.log(1e-1)))
    return {
        "x": nrm((BATCH, SEQ, d), 1.0),
        "c": nrm((BATCH, d), 1.0),
        "ctx": nrm((BATCH, CTX_LEN, d), 1.0),
        "c_ctx": nrm((d,), 1.0),
        "ada_w": nrm((DEPTH, d, N_MOD * d), 0.5 * d ** -0.5),
        "ada_b": nrm((DEPTH, N_MOD * d), 0.02),
        "norm1_w": gain((DEPTH, d)),
        "norm2_w": gain((DEPTH, d)),
        "mlp_w1": nrm((DEPTH, d, D_FF), d ** -0.5),
        "mlp_w2": nrm((DEPTH, D_FF, d), D_FF ** -0.5),
        "even_w_in": nrm((N_EVEN, d, EVEN_IN), d ** -0.5),
        "mla_q_norm": gain((N_EVEN, MLA_Q_RANK)),
        "mla_w_uq": nrm((N_EVEN, MLA_Q_RANK, MLA_HEADS * MLA_QK), MLA_Q_RANK ** -0.5),
        "mla_kv_norm": gain((N_EVEN, MLA_KV_RANK)),
        "mla_w_ukv": nrm((N_EVEN, MLA_KV_RANK, MLA_HEADS * (MLA_NOPE + MLA_V)), MLA_KV_RANK ** -0.5),
        "gla_gate_up": nrm((N_EVEN, 2, GLA_GATE_RANK, GLA_HEADS * GLA_DK), GLA_GATE_RANK ** -0.5),
        "gla_gate_bias": nrm((N_EVEN, 2, GLA_HEADS * GLA_DK), 0.1),
        "gla_o_norm": gain((N_EVEN, GLA_DV)),
        "even_w_out": nrm((N_EVEN, MIX_WIDTH, d), MIX_WIDTH ** -0.5),
        "gdn_w_in": nrm((N_ODD, d, ODD_IN), d ** -0.5),
        "gdn_conv_w": nrm((N_ODD, GDN_CONV, GDN_QKV), GDN_CONV ** -0.5),
        "gdn_a_log": jnp.log(jax.random.uniform(next(ks), (N_ODD, 2, GDN_HEADS), F32, 1.0, 16.0)),
        "gdn_dt_bias": dt + jnp.log(-jnp.expm1(-dt)),
        "gdn_o_norm": gain((N_ODD, GDN_DV)),
        "gdn_w_out": nrm((N_ODD, GDN_WIDTH, d), GDN_WIDTH ** -0.5),
        "final_norm": gain((d,)),
    }

def first_block(x, c, ctx, c_ctx, ada_w, ada_b, norm1_w, norm2_w, mlp_w1, mlp_w2,
              even_w_in, mla_q_norm, mla_w_uq, mla_kv_norm, mla_w_ukv, gla_gate_up, gla_gate_bias,
              gla_o_norm, even_w_out, gdn_w_in, gdn_conv_w, gdn_a_log, gdn_dt_bias, gdn_o_norm,
              gdn_w_out, final_norm):
    rope = axial_rope_tables(x.shape[1])
    h_lat, h_ctx = x, ctx
    for layer in range(DEPTH):
        need_ctx = layer < DEPTH - 1
        ml = [m[:, None, :] for m in jnp.split(jax.nn.silu(c) @ ada_w[layer] + ada_b[layer], N_MOD, axis=-1)]
        mc = jnp.split(jax.nn.silu(c_ctx) @ ada_w[layer] + ada_b[layer], N_MOD, axis=-1)
        a_lat = modulate(rms_norm(h_lat, norm1_w[layer]), ml[0], ml[1])
        a_ctx = modulate(rms_norm(h_ctx, norm1_w[layer]), mc[0], mc[1])
        i = layer // 2
        if layer % 2 == 0:
            o_lat, o_ctx = even_mixer(a_lat, a_ctx, even_w_in[i], mla_q_norm[i], mla_w_uq[i], mla_kv_norm[i],
                                      mla_w_ukv[i], gla_gate_up[i], gla_gate_bias[i], gla_o_norm[i],
                                      even_w_out[i], rope, need_ctx)
        else:
            o_lat, o_ctx = odd_mixer(a_lat, a_ctx, gdn_w_in[i], gdn_conv_w[i], gdn_a_log[i], gdn_dt_bias[i],
                                     gdn_o_norm[i], gdn_w_out[i], need_ctx)
        h_lat = h_lat + ml[2] * o_lat
        h_lat = h_lat + ml[5] * sq_relu_mlp(modulate(rms_norm(h_lat, norm2_w[layer]), ml[3], ml[4]),
                                            mlp_w1[layer], mlp_w2[layer])
        if need_ctx:
            h_ctx = h_ctx + mc[2] * o_ctx
            h_ctx = h_ctx + mc[5] * sq_relu_mlp(modulate(rms_norm(h_ctx, norm2_w[layer]), mc[3], mc[4]),
                                                mlp_w1[layer], mlp_w2[layer])
    return rms_norm(h_lat, final_norm)


D_MIX = D_MODEL
ATT_HEADS = 8
ATT_HEAD_DIM = 64
ATT_WIDTH = ATT_HEADS * ATT_HEAD_DIM
MLSTM_HEADS = 4
MLSTM_HEAD_DIM = 128
MLSTM_WIDTH = MLSTM_HEADS * MLSTM_HEAD_DIM
Q_RANK = 256
N_IDX_HEADS = 8
IDX_DIM = 64
INDEX_TOPK = 256
MLSTM_CHUNK = 64
CONV_WIDTH = 4
FFN_HIDDEN = -(-8 * D_MODEL // (3 * 256)) * 256
IN_SPLITS = (Q_RANK, ATT_WIDTH, ATT_WIDTH, IDX_DIM, N_IDX_HEADS,
             MLSTM_WIDTH, MLSTM_WIDTH, MLSTM_WIDTH, MLSTM_WIDTH, MLSTM_HEADS, MLSTM_HEADS)
IN_COLS = sum(IN_SPLITS)


def rms_norm_2(x, w):
    x32 = x.astype(jnp.float32)
    y = x32 * lax.rsqrt(jnp.mean(x32 * x32, axis=-1, keepdims=True) + EPS)
    return (y * w.astype(jnp.float32)).astype(x.dtype)

def rope(x, positions):
    d = x.shape[-1]
    inv_freq = ROPE_THETA ** (-jnp.arange(0, d, 2, dtype=jnp.float32) / d)
    ang = positions.astype(jnp.float32)[..., None] * inv_freq
    cos = jnp.cos(ang)[:, :, None, :]
    sin = jnp.sin(ang)[:, :, None, :]
    x1, x2 = jnp.split(x.astype(jnp.float32), 2, axis=-1)
    return jnp.concatenate([x1 * cos - x2 * sin, x2 * cos + x1 * sin], axis=-1).astype(x.dtype)

def causal_dwconv(x, w, b):
    ch = x.shape[-1]
    y = lax.conv_general_dilated(x, w[:, None, :].astype(x.dtype), window_strides=(1,),
                                 padding=[(CONV_WIDTH - 1, 0)],
                                 dimension_numbers=('NWC', 'WIO', 'NWC'),
                                 feature_group_count=ch)
    return y + b.astype(x.dtype)

def dsa_attention(q, k, v, q_idx, k_idx, w_idx):
    def one_seq(args):
        q_, k_, v_, qi_, ki_, wi_ = args
        seq = q_.shape[0]
        n_sel = min(INDEX_TOPK, seq // 4)
        key_pos = jnp.arange(seq)
        ki32 = ki_.astype(jnp.float32)
        scale = ATT_HEAD_DIM ** -0.5

        def block(i):
            start = i * Q_BLOCK
            t = start + jnp.arange(Q_BLOCK)
            qb = lax.dynamic_slice_in_dim(q_, start, Q_BLOCK, 0)
            qib = lax.dynamic_slice_in_dim(qi_, start, Q_BLOCK, 0).astype(jnp.float32)
            wib = lax.dynamic_slice_in_dim(wi_, start, Q_BLOCK, 0).astype(jnp.float32)
            idx_logits = jnp.einsum('thd,sd->ths', qib, ki32)
            idx_score = jnp.einsum('ths,th->ts', jax.nn.relu(idx_logits), wib)
            idx_score = jnp.where(key_pos[None, :] <= t[:, None], idx_score, -jnp.inf)
            _, sel = lax.top_k(idx_score, n_sel)
            valid = sel <= t[:, None]
            k_sel = k_[sel]
            v_sel = v_[sel]
            logits = jnp.einsum('thd,tkhd->thk', qb, k_sel).astype(jnp.float32) * scale
            logits = jnp.where(valid[:, None, :], logits, -jnp.inf)
            p = jax.nn.softmax(logits, axis=-1)
            return jnp.einsum('thk,tkhd->thd', p.astype(v_.dtype), v_sel)

        out = lax.map(block, jnp.arange(seq // Q_BLOCK))
        return out.reshape((seq,) + q_.shape[1:])

    return lax.map(one_seq, (q, k, v, q_idx, k_idx, w_idx))

def mlstm_chunkwise(q, k, v, ig, lf):
    b_, nh, seq, dk = q.shape
    dv = v.shape[-1]
    nc = seq // MLSTM_CHUNK

    def chunks(a):
        return jnp.moveaxis(a.reshape(a.shape[:2] + (nc, MLSTM_CHUNK) + a.shape[3:]), 2, 0)

    qc, kc, vc, igc, lfc = chunks(q), chunks(k), chunks(v), chunks(ig), chunks(lf)
    bc = jnp.cumsum(lfc, axis=-1)
    causal = jnp.tril(jnp.ones((MLSTM_CHUNK, MLSTM_CHUNK), dtype=bool))

    def step(carry, inp):
        c_s, n_s, m_s = carry
        q_, k_, v_, ig_, b_c = inp
        d_mat = b_c[..., :, None] - b_c[..., None, :] + ig_[..., None, :]
        d_mat = jnp.where(causal, d_mat, -jnp.inf)
        inter = b_c + m_s[..., None]
        m_row = jnp.maximum(inter, jnp.max(d_mat, axis=-1))
        w_intra = jnp.exp(d_mat - m_row[..., None])
        w_inter = jnp.exp(inter - m_row)
        s_mat = jnp.einsum('bhtd,bhsd->bhts', q_, k_) * w_intra
        num = (jnp.einsum('bhts,bhsv->bhtv', s_mat, v_)
               + w_inter[..., None] * jnp.einsum('bhtd,bhdv->bhtv', q_, c_s))
        den = jnp.sum(s_mat, axis=-1) + w_inter * jnp.einsum('bhtd,bhd->bht', q_, n_s)
        h = num / jnp.maximum(jnp.abs(den), jnp.exp(-m_row))[..., None]
        total = b_c[..., -1]
        w_log = total[..., None] - b_c + ig_
        m_new = jnp.maximum(total + m_s, jnp.max(w_log, axis=-1))
        decay = jnp.exp(total + m_s - m_new)
        w_state = jnp.exp(w_log - m_new[..., None])
        c_new = decay[..., None, None] * c_s + jnp.einsum('bhs,bhsd,bhsv->bhdv', w_state, k_, v_)
        n_new = decay[..., None] * n_s + jnp.einsum('bhs,bhsd->bhd', w_state, k_)
        return (c_new, n_new, m_new), h

    init = (jnp.zeros((b_, nh, dk, dv), jnp.float32), jnp.zeros((b_, nh, dk), jnp.float32),
            jnp.zeros((b_, nh), jnp.float32))
    _, hs = lax.scan(step, init, (qc, kc, vc, igc, bc))
    return jnp.moveaxis(hs, 0, 2).reshape(b_, nh, seq, dv)

def hybrid_mixer(h, positions, w_in, q_latent_norm, w_q_up, w_qidx_up, conv_w, conv_b,
                 b_igate, b_fgate, attn_out_norm, mlstm_out_norm, w_out):
    b_, seq, _ = h.shape
    split_pts = [int(s) for s in np.cumsum(IN_SPLITS)[:-1]]
    (cq, k_att, v_att, k_idx, w_idx,
     q_m, k_m, v_m, o_m, i_m, f_m) = jnp.split(h @ w_in, split_pts, axis=-1)

    cq = rms_norm_2(cq, q_latent_norm)
    q = rope((cq @ w_q_up).reshape(b_, seq, ATT_HEADS, ATT_HEAD_DIM), positions)
    q_idx = rope((cq @ w_qidx_up).reshape(b_, seq, N_IDX_HEADS, IDX_DIM), positions)
    k = rope(k_att.reshape(b_, seq, ATT_HEADS, ATT_HEAD_DIM), positions)
    v = v_att.reshape(b_, seq, ATT_HEADS, ATT_HEAD_DIM)
    k_idx = rope(k_idx[:, :, None, :], positions)[:, :, 0, :]
    w_idx = w_idx * (N_IDX_HEADS * IDX_DIM) ** -0.5
    att = dsa_attention(q, k, v, q_idx, k_idx, w_idx)
    att = rms_norm_2(att, attn_out_norm.reshape(ATT_HEADS, ATT_HEAD_DIM)).reshape(b_, seq, ATT_WIDTH)

    qk = jax.nn.silu(causal_dwconv(jnp.concatenate([q_m, k_m], axis=-1), conv_w, conv_b))
    q_m, k_m = jnp.split(qk, 2, axis=-1)

    def heads(a):
        return a.reshape(b_, seq, MLSTM_HEADS, MLSTM_HEAD_DIM).transpose(0, 2, 1, 3).astype(jnp.float32)

    ig = (i_m + b_igate).astype(jnp.float32).transpose(0, 2, 1)
    lf = jax.nn.log_sigmoid((f_m + b_fgate).astype(jnp.float32)).transpose(0, 2, 1)
    hm = mlstm_chunkwise(heads(q_m) * MLSTM_HEAD_DIM ** -0.5, heads(k_m), heads(v_m), ig, lf)
    hm = hm.transpose(0, 2, 1, 3).astype(h.dtype)
    hm = rms_norm_2(hm, mlstm_out_norm.reshape(MLSTM_HEADS, MLSTM_HEAD_DIM))
    hm = (jax.nn.sigmoid(o_m).reshape(b_, seq, MLSTM_HEADS, MLSTM_HEAD_DIM) * hm).reshape(b_, seq, MLSTM_WIDTH)

    return jnp.concatenate([att, hm], axis=-1) @ w_out

def swiglu(h, w_gate_up, w_down):
    g, u = jnp.split(h @ w_gate_up, 2, axis=-1)
    return (jax.nn.silu(g) * u) @ w_down

def second_inputs(seed: int = 0) -> dict:
    key = jax.random.key(seed)
    ks = jax.random.split(key, 24)
    L = DEPTH

    def nrm(k, shape, scale):
        return jax.random.normal(k, shape, jnp.float32) * scale

    def gain(k, shape):
        return 1.0 + 0.05 * jax.random.normal(k, shape, jnp.float32)

    x = nrm(ks[0], (BATCH, SEQ, D_MODEL), 1.0)
    c = nrm(ks[1], (BATCH, D_MODEL), 1.0)
    offsets = jax.random.randint(ks[2], (BATCH, 1), 0, 1024, dtype=jnp.int32)
    positions = (offsets + jnp.arange(SEQ, dtype=jnp.int32)[None, :]).astype(jnp.int32)
    b_fgate = (jnp.linspace(3.0, 6.0, MLSTM_HEADS, dtype=jnp.float32)[None, :]
               + nrm(ks[14], (L, MLSTM_HEADS), 0.1))
    return {
        "x": x,
        "c": c,
        "positions": positions,
        "w_mod": nrm(ks[3], (L, D_MODEL, 6 * D_MODEL), 0.5 * D_MODEL ** -0.5),
        "b_mod": nrm(ks[4], (L, 6 * D_MODEL), 0.01),
        "mix_norm_pre": gain(ks[5], (L, D_MODEL)),
        "mix_norm_post": gain(ks[6], (L, D_MODEL)),
        "w_in": nrm(ks[7], (L, D_MODEL, IN_COLS), D_MODEL ** -0.5),
        "q_latent_norm": gain(ks[8], (L, Q_RANK)),
        "w_q_up": nrm(ks[9], (L, Q_RANK, ATT_WIDTH), Q_RANK ** -0.5),
        "w_qidx_up": nrm(ks[10], (L, Q_RANK, N_IDX_HEADS * IDX_DIM), Q_RANK ** -0.5),
        "conv_w": nrm(ks[11], (L, CONV_WIDTH, 2 * MLSTM_WIDTH), CONV_WIDTH ** -0.5),
        "conv_b": nrm(ks[12], (L, 2 * MLSTM_WIDTH), 0.01),
        "b_igate": nrm(ks[13], (L, MLSTM_HEADS), 0.1),
        "b_fgate": b_fgate,
        "attn_out_norm": gain(ks[15], (L, ATT_WIDTH)),
        "mlstm_out_norm": gain(ks[16], (L, MLSTM_WIDTH)),
        "w_out": nrm(ks[17], (L, D_MIX, D_MODEL), D_MIX ** -0.5),
        "ffn_norm_pre": gain(ks[18], (L, D_MODEL)),
        "ffn_norm_post": gain(ks[19], (L, D_MODEL)),
        "w_gate_up": nrm(ks[20], (L, D_MODEL, 2 * FFN_HIDDEN), D_MODEL ** -0.5),
        "w_down": nrm(ks[21], (L, FFN_HIDDEN, D_MODEL), FFN_HIDDEN ** -0.5),
    }

def second_block(x, c, positions, w_mod, b_mod, mix_norm_pre, mix_norm_post, w_in, q_latent_norm,
              w_q_up, w_qidx_up, conv_w, conv_b, b_igate, b_fgate, attn_out_norm, mlstm_out_norm,
              w_out, ffn_norm_pre, ffn_norm_post, w_gate_up, w_down):
    c_act = jax.nn.silu(c)
    for l in range(DEPTH):
        mod = c_act @ w_mod[l] + b_mod[l]
        sh_m, sc_m, g_m, sh_f, sc_f, g_f = jnp.split(mod, 6, axis=-1)
        h = rms_norm_2(x, mix_norm_pre[l]) * (1.0 + sc_m[:, None, :]) + sh_m[:, None, :]
        y = hybrid_mixer(h, positions, w_in[l], q_latent_norm[l], w_q_up[l], w_qidx_up[l],
                         conv_w[l], conv_b[l], b_igate[l], b_fgate[l], attn_out_norm[l],
                         mlstm_out_norm[l], w_out[l])
        x = x + g_m[:, None, :] * rms_norm_2(y, mix_norm_post[l])
        h = rms_norm_2(x, ffn_norm_pre[l]) * (1.0 + sc_f[:, None, :]) + sh_f[:, None, :]
        y = swiglu(h, w_gate_up[l], w_down[l])
        x = x + g_f[:, None, :] * rms_norm_2(y, ffn_norm_post[l])
    return x


def setup_inputs(seed=0):
    out = dict(first_inputs(seed))
    for name, value in second_inputs(seed + 1).items():
        if name != "x":
            out[name + "_2"] = value
    return out


def reference(
    x, c, ctx, c_ctx, ada_w, ada_b, norm1_w, norm2_w, mlp_w1, mlp_w2, even_w_in, mla_q_norm,
    mla_w_uq, mla_kv_norm, mla_w_ukv, gla_gate_up, gla_gate_bias, gla_o_norm, even_w_out,
    gdn_w_in, gdn_conv_w, gdn_a_log, gdn_dt_bias, gdn_o_norm, gdn_w_out, final_norm, c_2,
    positions_2, w_mod_2, b_mod_2, mix_norm_pre_2, mix_norm_post_2, w_in_2, q_latent_norm_2,
    w_q_up_2, w_qidx_up_2, conv_w_2, conv_b_2, b_igate_2, b_fgate_2, attn_out_norm_2,
    mlstm_out_norm_2, w_out_2, ffn_norm_pre_2, ffn_norm_post_2, w_gate_up_2, w_down_2,
):
    x = first_block(
        x, c, ctx, c_ctx, ada_w, ada_b, norm1_w, norm2_w, mlp_w1, mlp_w2, even_w_in, mla_q_norm,
        mla_w_uq, mla_kv_norm, mla_w_ukv, gla_gate_up, gla_gate_bias, gla_o_norm, even_w_out,
        gdn_w_in, gdn_conv_w, gdn_a_log, gdn_dt_bias, gdn_o_norm, gdn_w_out, final_norm,
    )
    return second_block(
        x, c_2, positions_2, w_mod_2, b_mod_2, mix_norm_pre_2, mix_norm_post_2, w_in_2,
        q_latent_norm_2, w_q_up_2, w_qidx_up_2, conv_w_2, conv_b_2, b_igate_2, b_fgate_2,
        attn_out_norm_2, mlstm_out_norm_2, w_out_2, ffn_norm_pre_2, ffn_norm_post_2,
        w_gate_up_2, w_down_2,
    )


_drawn_inputs = setup_inputs


def setup_inputs(seed=0):
    import zlib

    import numpy as np

    out = dict(_drawn_inputs(seed))
    spreads = {}
    factors = {'mla_q_norm': 8.0,
     'mla_kv_norm': 5.23,
     'gla_gate_bias': 3.865,
     'gla_o_norm': 3.458,
     'gdn_o_norm': 2.942,
     'conv_b_2': 25.657,
     'b_igate_2': 64.0,
     'attn_out_norm_2': 8.026,
     'mlstm_out_norm_2': 14.235}
    for name, (base, spread) in spreads.items():
        noise = np.random.default_rng([zlib.crc32(name.encode()), seed]).standard_normal(out[name].shape)
        drawn = base * np.exp(spread * noise) if base else spread * noise
        out[name] = jnp.asarray(drawn.astype(out[name].dtype))
    for name, factor in factors.items():
        out[name] = (out[name] * factor).astype(out[name].dtype)
    return out
```

```python
import math
from contextlib import ExitStack

import numpy as np

import concourse.bass as bass
from concourse import mybir

F32 = mybir.dt.float32
F32R = mybir.dt.float32r
I32 = mybir.dt.int32
U32 = mybir.dt.uint32
ALU = mybir.AluOpType
ACT = mybir.ActivationFunctionType
AX = mybir.AxisListType
ds = bass.ds

P = 128
D = 1024
KD = D // P
TL = 256
TC = 256
TA = TL + TC
EPS = 1e-6
PANEL = 2048
PC = PANEL // KD
RAW = 3
NEG = -1e30
TAKEN = -3e38

MLA_HEADS, NOPE, ROPE, MV = 8, 64, 32, 64
QK = NOPE + ROPE
GLA_HEADS, GLA_DK, GLA_DV, CH = 4, 64, 128, 64
GDN_HEADS, GDN_DK, GDN_DV = 8, 64, 128
ATT_HEADS, ATT_D = 8, 64
ML_HEADS, ML_D = 4, 128
TOPK = 64
FFN = 2816
D_FF = 4096
N_MOD = 48
GDN_ORDER = [0, 2, 4, 6, 1, 3, 5, 7]
LEVELS = 7


def small_layout():
    items = [
        ("ident", P), ("ones", P), ("block64", P), ("tri_f", P), ("tri_b", P),
        ("gla_f", P), ("gla_b", P), ("kpe_swap", P), ("rot", P), ("chunk_start", TA),
        ("mla_q", TL), ("mla_qc", 1), ("kr_cos", TL), ("kr_sin", TL),
        ("lev_f", LEVELS * P), ("lev_b", LEVELS * P), ("causal", 2 * TL), ("invf", 1),
        ("gate_up", 4 * P), ("gate_bias", 4),
        ("cc", 2 * KD), ("c2", KD),
        ("ada_b", 2 * N_MOD), ("b_mod", 2 * N_MOD), ("norm1", 2 * KD), ("norm2", 2 * KD),
        ("q_norm", 3), ("kv_norm", 2), ("gla_o", 1), ("gdn_conv", 3 * 16), ("gdn_o", 1),
        ("final", KD), ("mix_pre", 2 * KD), ("mix_post", 2 * KD), ("q_lat", 4),
        ("conv_w", 2 * 4 * 8), ("conv_b", 2 * 8), ("attn_out", 8), ("mlstm_out", 8),
        ("ffn_pre", 2 * KD), ("ffn_post", 2 * KD),
        ("a_log", 16), ("dt_bias", 16), ("b_ig", 8), ("b_fg", 8),
    ]
    at, out = 0, {}
    for name, width in items:
        out[name] = (at, width)
        at += width
    return out, at


SMALL, SMALL_W = small_layout()


def panel_plan():
    mod = [("g", PANEL)] * (N_MOD * P // PC)
    plan = list(mod)
    plan += [("s", PANEL)] * 9 + [("s", 1536)] * 2 + [("s", PANEL), ("s", 1024)] + [("s", PANEL)] * 4
    plan += [("s", PANEL)] * 32
    plan += mod
    plan += [("s", PANEL)] * 4 + [("s", 256)] + [("s", PANEL)] * 8 + [("s", PANEL)] * 4
    plan += [("s", PANEL)] * 32
    for _ in range(2):
        plan += mod
        plan += [("s", PANEL)] * 14 + [("s", 256)] + [("s", PANEL)] + [("s", PANEL)] * 4
        plan += [("s", PANEL)] * (3 * FFN // PC)
    return plan


PLAN = panel_plan()


def shape_constants():
    c = {}
    j = np.arange(P)[:, None]
    i = np.arange(P)[None, :]
    c["ident"] = (j == i)
    c["ones"] = np.ones((P, P))
    c["block64"] = (j // 64 == i // 64)
    c["tri_f"] = (j <= i)
    c["tri_b"] = (j >= i)
    c["gla_f"] = (j <= i) & (j // CH == i // CH)
    c["gla_b"] = (j >= i) & (j // CH == i // CH)
    c["chunk_start"] = np.broadcast_to((np.arange(TA) % CH != 0)[None, :], (P, TA))
    swap = np.zeros((P, P))
    for half in (64, 96):
        for r in range(ROPE):
            axis, part, n = r // 16, (r // 8) % 2, r % 8
            swap[64 + axis * 16 + (1 - part) * 8 + n, half + r] = 1.0
    c["kpe_swap"] = swap
    rot = np.zeros((P, P))
    for h in (0, 64):
        for r in range(32):
            rot[h + 32 + r, h + r] = -1.0
            rot[h + r, h + 32 + r] = 1.0
    c["rot"] = rot
    f32 = np.float32
    row = np.repeat(np.arange(TL // 64), 64).astype(f32)
    col = np.tile(np.arange(64), TL // 64).astype(f32)
    inv = (10000.0 ** (-np.arange(0, 16, 2) / 16.0)).astype(f32)
    ang = np.stack([row[None, :] * inv[:, None], col[None, :] * inv[:, None]])
    cos = np.zeros((ROPE, TL))
    sin = np.zeros((ROPE, TL))
    for r in range(ROPE):
        axis, part, n = r // 16, (r // 8) % 2, r % 8
        cos[r] = np.cos(ang[axis, n].astype(f32))
        sin[r] = np.sin(ang[axis, n].astype(f32)) * (-1.0 if part == 0 else 1.0)
    c["mla_q"] = np.concatenate([np.ones((64, TL)), cos, sin])
    c["mla_qc"] = (np.arange(P) < 96).astype(f32)[:, None]
    c["kr_cos"] = np.concatenate([np.zeros((64, TL)), cos, cos])
    c["kr_sin"] = np.concatenate([np.zeros((64, TL)), sin, sin])
    lev = []
    for n in range(LEVELS):
        s = 1 << n
        lev.append((j // (2 * s) == i // (2 * s)) & (j // s % 2 == 0) & (i // s % 2 == 1))
    c["lev_f"] = np.concatenate(lev, axis=1)
    c["lev_b"] = np.concatenate([m.T for m in lev], axis=1)
    s = np.arange(TL)[None, :]
    c["causal"] = np.concatenate([np.where(s <= j + t * P, 0.0, NEG) for t in range(2)], axis=1)
    c["invf"] = np.tile((10000.0 ** (-np.arange(0, 64, 2) / 64.0)).astype(f32), 4)[:, None]
    return {n: np.asarray(v, f32) for n, v in c.items()}


def columns(v):
    v = np.asarray(v)
    return v.reshape(-1, P).T


def layout_small(x):
    out = np.zeros((P, SMALL_W), np.float32)

    def put(name, value):
        at, width = SMALL[name]
        assert value.shape[1] == width, (name, value.shape, width)
        out[:value.shape[0], at:at + width] = value

    for name, value in shape_constants().items():
        put(name, value)
    gate = np.zeros((64, 2, 256), np.float32)
    gate[32:48, 0] = x["gla_gate_up"][0, 0]
    gate[48:64, 1] = x["gla_gate_up"][0, 1]
    put("gate_up", gate.reshape(64, 512))
    put("gate_bias", columns(x["gla_gate_bias"][0]))
    cc = np.stack([x["c"][0].reshape(KD, P), x["c_ctx"].reshape(KD, P)], axis=1)
    put("cc", cc.reshape(2 * KD, P).T)
    put("c2", columns(x["c_2"][0]))
    for name, key in (("ada_b", "ada_b"), ("b_mod", "b_mod_2"), ("norm1", "norm1_w"), ("norm2", "norm2_w"),
                      ("q_norm", "mla_q_norm"), ("kv_norm", "mla_kv_norm"), ("gla_o", "gla_o_norm"),
                      ("gdn_conv", "gdn_conv_w"), ("gdn_o", "gdn_o_norm"), ("final", "final_norm"),
                      ("mix_pre", "mix_norm_pre_2"), ("mix_post", "mix_norm_post_2"), ("q_lat", "q_latent_norm_2"),
                      ("conv_w", "conv_w_2"), ("conv_b", "conv_b_2"), ("attn_out", "attn_out_norm_2"),
                      ("mlstm_out", "mlstm_out_norm_2"), ("ffn_pre", "ffn_norm_pre_2"),
                      ("ffn_post", "ffn_norm_post_2")):
        put(name, columns(x[key]))
    for name, row in (("a_log", x["gdn_a_log"][0][:, GDN_ORDER]), ("dt_bias", x["gdn_dt_bias"][0][:, GDN_ORDER]),
                      ("b_ig", x["b_igate_2"]), ("b_fg", x["b_fgate_2"])):
        put(name, np.broadcast_to(row.reshape(1, -1), (P, SMALL[name][1])))
    return out


def tall(w):
    n = w.shape[1] // PC
    return list(w.reshape(KD, P, n, PC).transpose(2, 1, 0, 3).reshape(n, P, PANEL))


def blocks_of(w, cols):
    k = w.shape[0] // P
    return w.reshape(k, P, cols // P, P).transpose(1, 2, 0, 3).reshape(P, -1)


def padded(a, width=PANEL):
    out = np.zeros((P, width), np.float32)
    out[:, :a.shape[1]] = a
    return out


def down_panels(w):
    n = w.shape[0] // PC
    return list(w.reshape(n, 2, P, D).transpose(0, 2, 1, 3).reshape(n, P, PANEL))


def layout_panels(x):
    out = []
    w = x["even_w_in"][0]
    cq, ckv, kpe = w[:, :384], w[:, 384:640], w[:, 640:672]
    gq, gk, gv, gg, glow = w[:, 672:928], w[:, 928:1184], w[:, 1184:1696], w[:, 1696:2208], w[:, 2208:2240]
    feat = np.concatenate([cq, ckv, np.zeros((D, 32), np.float32), glow, kpe, kpe, gq, gk, gg], axis=1)
    out += tall(x["ada_w"][0])
    out += tall(feat) + tall(gv)
    uq = x["mla_w_uq"][0].reshape(384, MLA_HEADS, QK)
    order = [NOPE + (r // 16) * 16 + (1 - (r // 8) % 2) * 8 + r % 8 for r in range(ROPE)]
    uq = np.concatenate([uq, uq[:, :, order]], axis=2).reshape(384, MLA_HEADS * P)
    out += [padded(blocks_of(uq[:, :512], 512)), padded(blocks_of(uq[:, 512:], 512))]
    ukv = x["mla_w_ukv"][0].reshape(256, MLA_HEADS, NOPE + MV)
    kk = np.concatenate([ukv[:, :, :NOPE], np.zeros((256, MLA_HEADS, 64), np.float32)], axis=2)
    vv = ukv[:, :, NOPE:].reshape(2, P, 512).transpose(1, 0, 2).reshape(P, 1024)
    out += [blocks_of(kk.reshape(256, 1024), 1024), padded(vv)]
    out += tall(x["even_w_out"][0])

    def mlp(w1, w2):
        ups, downs = tall(w1), down_panels(w2)
        order = [ups[0]]
        for n in range(len(downs)):
            order += ups[n + 1:n + 2] + [downs[n]]
        return order

    out += mlp(x["mlp_w1"][0], x["mlp_w2"][0])
    out += tall(x["ada_w"][1])
    w = x["gdn_w_in"][0]
    ab = w[:, 3072:].reshape(D, 4, GDN_HEADS)[:, :, GDN_ORDER].reshape(KD, P, 32)
    out += tall(w[:, 2048:3072]) + [padded(ab.transpose(1, 0, 2).reshape(P, 256))]
    out += tall(w[:, 1024:2048]) + tall(w[:, :1024])
    out += tall(x["gdn_w_out"][0]) + mlp(x["mlp_w1"][1], x["mlp_w2"][1])
    for l in range(2):
        out += tall(x["w_mod_2"][l])
        w = x["w_in_2"][l]
        cut = np.cumsum([0, 256, 512, 512, 64, 8, 512, 512, 512, 512, 4, 4])
        cq, ka, va, ki, wi, qm, km, vm, om, im, fm = (w[:, a:b] for a, b in zip(cut[:-1], cut[1:]))
        out += tall(np.concatenate([cq, ka, qm, km, om, ki, ki, np.zeros((D, P), np.float32)], axis=1))
        out += tall(va) + tall(vm)
        small = np.concatenate([wi, im, fm, np.zeros((D, 16), np.float32)], axis=1)
        out += [padded(small.reshape(KD, P, 32).transpose(1, 0, 2).reshape(P, 256))]
        out += [np.concatenate([blocks_of(x["w_q_up_2"][l], 512), blocks_of(x["w_qidx_up_2"][l], 512)], axis=1)]
        out += tall(x["w_out_2"][l])
        gate = tall(x["w_gate_up_2"][l][:, :FFN])
        up = tall(x["w_gate_up_2"][l][:, FFN:])
        downs = down_panels(x["w_down_2"][l])
        out += [gate[0], up[0]]
        for n in range(len(downs)):
            out += gate[n + 1:n + 2] + up[n + 1:n + 2] + [downs[n]]
    assert len(out) == len(PLAN), (len(out), len(PLAN))
    return np.stack(out)


PER_LOOP = 6


class Chain:

    def __init__(self, sem):
        self.sem, self.n = sem, 0

    def then(self, eng, ins):
        self.n += 1
        ins.then_inc(self.sem, 1)
        eng.wait_ge(self.sem, self.n)


class Program:

    def __init__(self, nc, ctx, panels, small, xin, pos, out):
        self.nc, self.ctx = nc, ctx
        self.suffix = ""
        self.panels, self.small, self.xin, self.pos, self.out = panels, small, xin, pos, out
        self.raw = self.sb("raw", [P, RAW, PANEL])
        self.wh = self.sb("w_high", [P, 2, PANEL], F32R)
        self.wl = self.sb("w_low", [P, 2, PANEL], F32R)
        self.cst = self.sb("constants", [P, SMALL_W])
        self.xT = self.sb("x_features", [P, KD, TA])
        self.mod1 = [self.sb(f"mod1_{l}", [P, N_MOD, 2]) for l in range(2)]
        self.mod2 = [self.sb(f"mod2_{l}", [P, N_MOD, 1]) for l in range(2)]
        self.ps = ctx.enter_context(nc.psum_tensor("banks", [P, 8, 512], F32))
        self.landed = [self.sem(f"panel_landed_{s}") for s in range(RAW)]
        self.gemv_used = self.sem("gemv_panel_used")
        self.w_high = self.sem("weights_high_ready")
        self.w_split = self.sem("weights_split")
        self.dve_chain = Chain(self.sem("vector_step"))
        self.act_chain = Chain(self.sem("scalar_step"))
        self.pool_chain = Chain(self.sem("gpsimd_step"))
        self.at_stream = [n for n, (kind, _) in enumerate(PLAN) if kind == "s"]
        self.ends = [None] * len(self.at_stream)
        self.n_gemv = 0
        self.m = 0
        self.split_next = {"act": 0, "dve": 0}
        self.block = None
        self.layer_m = 0
        self.streamed = 0

    def sb(self, name, shape, dt=F32, ctx=None):
        return (ctx or self.ctx).enter_context(self.nc.sbuf_tensor(name + self.suffix, shape, dt))

    def sem(self, name):
        return self.nc.alloc_semaphore(name=name + self.suffix)

    def c(self, name):
        at, width = SMALL[name]
        return self.cst[:, at:at + width]

    def take(self, count, sem, per_panel, first=0):
        ms = list(range(self.m, self.m + count))
        self.m += count
        for j, m in enumerate(ms):
            self.ends[m] = (sem, first + per_panel * (j + 1))
        return ms

    def landed_count(self, m):
        return 16 * (self.at_stream[m] // RAW + 1)

    def in_loop(self, value, m, q):
        if q is None:
            return value(m)
        return q * (value(m + PER_LOOP) - value(m)) + value(m)

    def split_act(self, act, m, q=None):
        slot, width = self.at_stream[m] % RAW, PLAN[self.at_stream[m]][1]
        act.wait_ge(self.landed[slot], self.in_loop(self.landed_count, m, q))
        if m - 2 >= self.layer_m:
            sem = self.ends[m - 2][0]
            act.wait_ge(sem, self.in_loop(lambda x: self.ends[x][1], m - 2, q))
        self.nc.scalar.activation(self.wh[:, m % 2, 0:width], self.raw[:, slot, 0:width],
                                  ACT.Copy).then_inc(self.w_high, 1)

    def split_dve(self, dve, m, q=None):
        slot, width = self.at_stream[m] % RAW, PLAN[self.at_stream[m]][1]
        dve.wait_ge(self.w_high, self.in_loop(lambda x: x + 1, m, q))
        self.nc.vector.tensor_tensor(self.wl[:, m % 2, 0:width], self.raw[:, slot, 0:width],
                                     self.wh[:, m % 2, 0:width].bitcast(F32),
                                     ALU.subtract).then_inc(self.w_split, 1)

    def split_upto(self, which, eng, m):
        while self.split_next[which] <= m:
            (self.split_act if which == "act" else self.split_dve)(eng, self.split_next[which])
            self.split_next[which] += 1

    def wait_split(self, pe, m, q=None):
        pe.wait_ge(self.w_split, self.in_loop(lambda x: x + 1, m, q))

    def product3(self, out, sh, sl, mh, ml, nk):
        for k in range(nk):
            self.nc.tensor.matmul(out, sh(k), ml(k), start=(k == 0), stop=False)
            self.nc.tensor.matmul(out, sh(k), mh(k), start=False, stop=False)
            last = self.nc.tensor.matmul(out, sl(k), mh(k), start=False, stop=(k == nk - 1))
        return last

    def stream(self, end):
        used, g, m = [], 0, 0
        for kind, _ in PLAN:
            if kind == "g":
                g += 1
                used.append((self.gemv_used, g))
            else:
                m += 1
                used.append((self.w_split, m))
        total = min(end + RAW, len(PLAN))

        @self.block.sync
        def _(sp):
            def load(n, wait, source):
                if wait:
                    sp.wait_ge(*wait)
                sp.dma_start(self.raw[:, n % RAW, :], source).then_inc(self.landed[n % RAW], 16)

            n = self.streamed
            while n < total:
                run = 0
                while n >= RAW and n + run < total and used[n + run - RAW][0] is used[n - RAW][0]:
                    run += 1
                turns = run // RAW
                if turns > 1:
                    with sp.Fori(0, turns) as q:
                        for s in range(RAW):
                            sem, value = used[n + s - RAW]
                            load(n + s, (sem, q * RAW + value),
                                 self.panels[ds(q * RAW + (n + s), 1), :, :].rearrange("a p n -> p (a n)"))
                    n += turns * RAW
                else:
                    load(n, used[n - RAW] if n >= RAW else None, self.panels[n, :, :])
                    n += 1
        self.streamed = total

    def modulation(self, name, vec, vec_ready, nv, mod, bias):
        nc, first = self.nc, self.n_gemv
        n0 = [n for n, (kind, _) in enumerate(PLAN) if kind == "g"][first]
        turns = N_MOD * P // PC // RAW
        self.n_gemv += turns * RAW
        done = self.sem(f"{name}_products")
        ready = self.sem(f"{name}_ready")
        bank = self.ps[:, 7, 0:N_MOD * nv]

        @self.block.tensor
        def _(pe):
            for w in vec_ready:
                pe.wait_ge(*w)
            with pe.Fori(0, turns) as q:
                for s in range(RAW):
                    slot = (n0 + s) % RAW
                    pe.wait_ge(self.landed[slot], q * 16 + 16 * ((n0 + s) // RAW + 1))
                    for b in range(2):
                        for k in range(KD):
                            last = nc.tensor.matmul(
                                self.ps[:, 7, ds(q * (2 * RAW * nv) + (2 * s + b) * nv, nv)],
                                self.raw[:, slot, k * PC + b * P:k * PC + (b + 1) * P], vec[:, k, :],
                                start=(k == 0), stop=(k == KD - 1))
                    last.then_inc(self.gemv_used, 1)

        @self.block.vector
        def _(dve):
            dve.wait_ge(self.gemv_used, self.n_gemv)
            b = bias.rearrange("p (j a) -> p j a", a=1).to_broadcast([P, N_MOD, nv])
            nc.vector.tensor_tensor(mod[:], bank.rearrange("p (j v) -> p j v", v=nv), b,
                                    ALU.add).then_inc(ready, 1)
        return [(ready, 1)]

    def rstd(self, tmp, name, src, src_ready, groups, n, dim, matrix, bank=0, squares=None):
        nc, g = self.nc, len(groups)
        nb = src.shape[1]
        per_bank = 512 // n
        if squares is None:
            squares = self.sb(f"{name}_squares", [P, nb, n], ctx=tmp)
        r = self.sb(f"{name}_rstd", [P, g, n], ctx=tmp)
        root = self.sb(f"{name}_root", [P, g, n], ctx=tmp)
        sq_ready, summed, ms_ready, root_ready, ready = (
            self.sem(f"{name}_{s}") for s in ("squares_ready", "summed", "mean_ready", "root_ready", "rstd_ready"))
        nbanks = (g + per_bank - 1) // per_bank
        sums = self.ps[:, bank:bank + nbanks, :].rearrange("p b n -> p (b n)")[:, 0:g * n]\
            .rearrange("p (g n) -> p g n", n=n)

        @self.block.scalar
        def _(act):
            for w in src_ready:
                act.wait_ge(*w)
            nc.scalar.activation(squares[:], src, ACT.Square).then_inc(sq_ready, 1)
            act.wait_ge(ms_ready, 1)
            nc.scalar.activation(root[:], r[:], ACT.Sqrt).then_inc(root_ready, 1)

        @self.block.tensor
        def _(pe):
            pe.wait_ge(sq_ready, 1)
            for i, blocks in enumerate(groups):
                for b in blocks:
                    last = nc.tensor.matmul(sums[:, i, :], matrix, squares[:, b, :],
                                            start=(b == blocks[0]), stop=(b == blocks[-1]))
            last.then_inc(summed, 1)

        @self.block.vector
        def _(dve):
            dve.wait_ge(summed, 1)
            nc.vector.tensor_scalar(r[:], sums, 1.0 / dim, EPS, ALU.mult, ALU.add).then_inc(ms_ready, 1)
            dve.wait_ge(root_ready, 1)
            nc.vector.reciprocal(r[:], root[:]).then_inc(ready, 1)
        return r, squares, [(ready, 1)]

    def split_blocks(self, name, a, a_ready, high, low, counts=None):
        nc = self.nc
        nb = a.shape[1]
        h_ready, ready = self.sem(f"{name}_high_ready"), self.sem(f"{name}_split_ready")

        @self.block.scalar
        def _(act):
            for k in range(nb):
                act.wait_ge(a_ready, k + 1 if counts is None else counts[k])
                nc.scalar.activation(high[:, k, :], a[:, k, :], ACT.Copy).then_inc(h_ready, 1)

        @self.block.vector
        def _(dve):
            for k in range(nb):
                dve.wait_ge(h_ready, k + 1)
                nc.vector.tensor_tensor(low[:, k, :], a[:, k, :], high[:, k, :].bitcast(F32),
                                        ALU.subtract).then_inc(ready, 1)
        return [(ready, nb)]

    def norm_modulate(self, name, weight, mod, nv, shift, scale, n, high, low, ready, bank=0, work=None):
        nc = self.nc
        with ExitStack() as tmp:
            x = self.xT[:, :, 0:n]
            r, a, r_ready = self.rstd(tmp, name, x, ready, [list(range(KD))], n, D, self.c("ones"), bank, work)
            gain = self.sb(f"{name}_gain", [P, KD, nv], ctx=tmp)
            a_ready = self.sem(f"{name}_modulated")
            half = n // nv

            @self.block.vector
            def _(dve):
                self.dve_chain.then(dve, nc.vector.scalar_tensor_tensor(
                    gain[:], mod[:, scale:scale + KD, 0:nv], 1.0, spread(weight, 2, nv), ALU.add, ALU.mult))
                for w in r_ready:
                    dve.wait_ge(*w)
                self.dve_chain.then(dve, nc.vector.tensor_tensor(a[:], x, r[:].broadcast_to([P, KD, n]), ALU.mult))
                for k in range(KD):
                    for v in range(nv):
                        part = a[:, k, v * half:(v + 1) * half]
                        last = nc.vector.tensor_scalar(part, part, gain[:, k, v:v + 1],
                                                       mod[:, shift + k, v:v + 1], ALU.mult, ALU.add)
                    last.then_inc(a_ready, 1)
            return self.split_blocks(name, a, a_ready, high, low)

    def linear(self, name, panels, per_panel, nblocks, product, evac, x_ready, engines=("dve", "act"),
               banks=(0, 1, 2, 3), after=()):
        nc, nb = self.nc, len(banks)
        done = self.sem(f"{name}_products")
        out = {e: self.sem(f"{name}_out_{e}") for e in sorted(set(engines))}
        ms = self.take(panels, done, per_panel)
        self.ends[ms[-1]] = (done, nblocks)
        who = [engines[q % len(engines)] for q in range(nblocks)]
        rank = [sum(w == who[q] for w in who[:q + 1]) for q in range(nblocks)]

        @self.block.tensor
        def _(pe):
            for w in x_ready:
                pe.wait_ge(*w)
            for q in range(nblocks):
                m = ms[q // per_panel]
                if q % per_panel == 0:
                    self.wait_split(pe, m)
                if q >= nb:
                    pe.wait_ge(out[who[q - nb]], rank[q - nb])
                product(q, m, self.ps[:, banks[q % nb], :]).then_inc(done, 1)

        def take_out(which, eng):
            for w in after:
                eng.wait_ge(*w)
            for p, m in enumerate(ms):
                self.split_upto(which, eng, min(m + 1, ms[-1]))
                for q in range(p * per_panel, min((p + 1) * per_panel, nblocks)):
                    if who[q] == which:
                        eng.wait_ge(done, q + 1)
                        evac(q, which, eng, self.ps[:, banks[q % nb], :]).then_inc(out[which], 1)

        @self.block.scalar
        def _(act):
            take_out("act", act)

        @self.block.vector
        def _(dve):
            take_out("dve", dve)
        return [(out[e], sum(w == e for w in who)) for e in out]

    def weight_block(self, m, at):
        return (self.wh[:, m % 2, at:at + P], self.wl[:, m % 2, at:at + P])

    def features(self, high, low, n, nk, offset):
        def product(q, m, bank):
            return self.product3(bank[:, 0:n],
                                 lambda k: self.wh[:, m % 2, offset(q, k):offset(q, k) + P],
                                 lambda k: self.wl[:, m % 2, offset(q, k):offset(q, k) + P],
                                 lambda k: high[:, k, 0:n], lambda k: low[:, k, 0:n], nk)
        return product

    def tokens(self, high, low, tiles, width, nk):
        def product(q, m, bank):
            t = q % tiles
            return self.product3(bank[:, 0:width],
                                 lambda k: high[:, k, t * P:(t + 1) * P], lambda k: low[:, k, t * P:(t + 1) * P],
                                 lambda k: self.wh[:, m % 2, k * width:(k + 1) * width],
                                 lambda k: self.wl[:, m % 2, k * width:(k + 1) * width], nk)
        return product

    def copy_out(self, target):
        def evac(q, which, eng, bank):
            dst = target(q)
            src = bank[:, 0:dst.shape[-1]]
            if which == "act":
                return self.nc.scalar.activation(dst, src, ACT.Copy)
            return self.nc.vector.tensor_copy(dst, src)
        return evac

    def add_gated(self, mod, gate, nv, n):
        half = n // nv

        def evac(q, which, eng, bank):
            for v in range(nv):
                x = self.xT[:, q, v * half:(v + 1) * half]
                last = self.nc.vector.scalar_tensor_tensor(
                    x, bank[:, v * half:(v + 1) * half], mod[:, gate + q, v:v + 1], x, ALU.mult, ALU.add)
            return last
        return evac

    def feed_forward(self, name, chunks, gated, n, high, low, a_ready, y, y_free):
        nc = self.nc
        ups = 2 if gated else 1
        per = PER_LOOP // (ups + 1)
        up_done, down_done, r_ready, h_ready, hh_ready, hid_ready, y_ready = (
            self.sem(f"{name}_{s}") for s in ("up_products", "down_products", "activated", "hidden_ready",
                                              "hidden_high", "hidden_split", "added"))
        first = self.m
        kinds = [("up", 0, u) for u in range(ups)]
        for c in range(chunks):
            if c + 1 < chunks:
                kinds += [("up", c + 1, u) for u in range(ups)]
            kinds += [("down", c, 0)]
        m_of = {}
        for kind, c, u in kinds:
            if kind == "up":
                m_of[kind, c, u] = self.take(1, up_done, 1, c * ups + u)[0]
            else:
                m_of[kind, c, u] = self.take(1, down_done, 4, 4 * c)[0]
        last_m = self.m - 1
        tmp = ExitStack()
        act_buf = self.sb(f"{name}_activated", [P, 2, n], ctx=tmp)
        hid = self.sb(f"{name}_hidden", [P, 2, n], ctx=tmp)
        hh = self.sb(f"{name}_hidden_h", [P, per, 2, n], F32R, ctx=tmp)
        hl = self.sb(f"{name}_hidden_l", [P, per, 2, n], F32R, ctx=tmp)
        ps = self.ps

        def at(kind, cs, q):
            return m_of[kind, cs, 0]

        def pe_up(pe, cs, q=None):
            c = cs if q is None else q * per + cs
            for u in range(ups):
                self.wait_split(pe, m_of["up", cs, u], q)
                m = m_of["up", cs, u]
                if u == 0 and cs >= 1:
                    pe.wait_ge(h_ready, c)
                for b in range(2):
                    last = self.product3(ps[:, 2 * u + b, 0:n],
                                         lambda k: self.wh[:, m % 2, k * PC + b * P:k * PC + (b + 1) * P],
                                         lambda k: self.wl[:, m % 2, k * PC + b * P:k * PC + (b + 1) * P],
                                         lambda k: high[:, k, 0:n], lambda k: low[:, k, 0:n], KD)
                last.then_inc(up_done, 1)

        def pe_down(pe, cs, q=None):
            c = cs if q is None else q * per + cs
            m = m_of["down", cs, 0]
            self.wait_split(pe, m, q)
            pe.wait_ge(hid_ready, c + 1)
            for g in range(4):
                if cs > 0 or g >= 2:
                    pe.wait_ge(y_ready, c * 4 + (g - 1))
                for o in (2 * g, 2 * g + 1):
                    last = self.product3(ps[:, 4 + o % 4, 0:n],
                                         lambda k: self.wh[:, m % 2, k * D + o * P:k * D + (o + 1) * P],
                                         lambda k: self.wl[:, m % 2, k * D + o * P:k * D + (o + 1) * P],
                                         lambda k: hh[:, cs % per, k, :], lambda k: hl[:, cs % per, k, :], 2)
                last.then_inc(down_done, 1)

        def act_up(act, cs, q=None):
            c = cs if q is None else q * per + cs
            if cs >= 1:
                act.wait_ge(h_ready, c)
            act.wait_ge(up_done, c * ups + 1)
            nc.scalar.activation(act_buf[:], ps[:, 0:2, 0:n], ACT.Silu if gated else ACT.Relu).then_inc(r_ready, 1)

        def act_high(act, cs, q=None):
            c = cs if q is None else q * per + cs
            act.wait_ge(h_ready, c + 1)
            if cs >= per:
                act.wait_ge(down_done, c * 4 + 4 * (1 - per))
            nc.scalar.activation(hh[:, cs % per], hid[:], ACT.Copy).then_inc(hh_ready, 1)

        def dve_up(dve, cs, q=None):
            c = cs if q is None else q * per + cs
            dve.wait_ge(r_ready, c + 1)
            dve.wait_ge(up_done, (c + 1) * ups)
            if cs >= 1:
                dve.wait_ge(hid_ready, c)
            if gated:
                ins = nc.vector.tensor_tensor(hid[:], act_buf[:], ps[:, 2:4, 0:n], ALU.mult)
            else:
                ins = nc.vector.scalar_tensor_tensor(hid[:], ps[:, 0:2, 0:n], 0.0, act_buf[:], ALU.max, ALU.mult)
            ins.then_inc(h_ready, 1)

        def dve_low(dve, cs, q=None):
            c = cs if q is None else q * per + cs
            dve.wait_ge(hh_ready, c + 1)
            nc.vector.tensor_tensor(hl[:, cs % per], hid[:], hh[:, cs % per].bitcast(F32),
                                    ALU.subtract).then_inc(hid_ready, 1)

        def dve_add(dve, cs, q=None):
            c = cs if q is None else q * per + cs
            for g in range(4):
                dve.wait_ge(down_done, c * 4 + (g + 1))
                src, dst = ps[:, 4 + 2 * (g % 2):6 + 2 * (g % 2), 0:n], y[:, 2 * g:2 * g + 2, 0:n]
                if cs == 0:
                    ins = nc.vector.tensor_copy(dst, src)
                else:
                    dve.wait_ge(y_ready, c * 4 + (g - 3))
                    ins = nc.vector.tensor_tensor(dst, src, dst, ALU.add)
                ins.then_inc(y_ready, 1)

        def turn(body, eng):
            for j in range(per):
                body(eng, j, None)
            with eng.Fori(0, (chunks - 1) // per - 1) as q:
                for j in range(per):
                    body(eng, per + j, q)

        assert (chunks - 1) % per == 0

        def split(which, m, q):
            def go(eng):
                (self.split_act if which == "act" else self.split_dve)(eng, m, q)
            return go

        def step(which, up, high_or_low, add):
            def body(eng, cs, q):
                for u in range(1, ups):
                    split(which, m_of["up", cs + 1, u], q)(eng)
                split(which, m_of["down", cs, 0], q)(eng)
                up(eng, cs + 1, q)
                split(which, m_of["down", cs, 0] + 1, q)(eng)
                high_or_low(eng, cs + 1, q)
                if add:
                    add(eng, cs, q)
            return body

        @self.block.tensor
        def _(pe):
            for w in a_ready:
                pe.wait_ge(*w)
            pe_up(pe, 0)

            def body(pe, cs, q):
                pe_up(pe, cs + 1, q)
                pe_down(pe, cs, q)
            turn(body, pe)
            pe_down(pe, chunks - 1)

        @self.block.scalar
        def _(act):
            self.split_upto("act", act, first + ups)
            act_up(act, 0)
            act_high(act, 0)
            turn(step("act", act_up, act_high, None), act)
            self.split_next["act"] = last_m + 1

        @self.block.vector
        def _(dve):
            for w in y_free:
                dve.wait_ge(*w)
            self.split_upto("dve", dve, first + ups)
            dve_up(dve, 0)
            dve_low(dve, 0)
            turn(step("dve", dve_up, dve_low, dve_add), dve)
            dve_add(dve, chunks - 1)
            self.split_next["dve"] = last_m + 1
        tmp.close()
        return [(y_ready, 4 * chunks)]

    def add_feed_forward(self, name, y, y_ready, mod, gate, nv, n):
        nc, ready, half = self.nc, self.sem(f"{name}_added_to_x"), n // nv

        @self.block.vector
        def _(dve):
            for w in y_ready:
                dve.wait_ge(*w)
            for k in range(KD):
                for v in range(nv):
                    x = self.xT[:, k, v * half:(v + 1) * half]
                    last = nc.vector.scalar_tensor_tensor(
                        x, y[:, k, v * half:(v + 1) * half], mod[:, gate + k, v:v + 1], x, ALU.mult, ALU.add)
            last.then_inc(ready, 1)
        return [(ready, 1)]


def tall_offset(q, k):
    return k * PC + (q % 2) * P


def whole_split(pr, scope, name, a, ready, n):
    nc = pr.nc
    high = pr.sb(f"{name}_h", [P, a.shape[1], n], F32R, ctx=scope)
    low = pr.sb(f"{name}_l", [P, a.shape[1], n], F32R, ctx=scope)
    h_ready, l_ready = pr.sem(f"{name}_high"), pr.sem(f"{name}_split")

    @pr.block.scalar
    def _(act):
        for w in ready:
            act.wait_ge(*w)
        nc.scalar.activation(high[:], a, ACT.Copy).then_inc(h_ready, 1)

    @pr.block.vector
    def _(dve):
        dve.wait_ge(h_ready, 1)
        nc.vector.tensor_tensor(low[:], a, high[:].bitcast(F32), ALU.subtract).then_inc(l_ready, 1)
    return high, low, [(l_ready, 1)]


def spread(ap, axis, n):
    shape = list(ap.shape)
    shape.insert(axis, n)
    return ap.unsqueeze(axis).broadcast_to(shape)


def even_mixer(pr, high, low, a_ready, mod, tmp_a):
    nc, ps, c = pr.nc, pr.ps, pr.c
    N = TA
    keep = ExitStack()
    pa = pr.pa
    pb = pr.pb
    gv = pr.gv
    y = pr.y

    def target(q):
        return (pa[:, q, :] if q < 6 else pb[:, q - 6, :])

    proj = pr.linear("even_in", 7, 2, 14, pr.features(high, low, N, KD, tall_offset),
                     pr.copy_out(target), a_ready)
    vals = pr.linear("even_v", 2, 4, 8, pr.tokens(high, low, 4, PC, KD),
                     pr.copy_out(lambda q: gv[:, q % 4, (q // 4) * PC:(q // 4 + 1) * PC]), proj)
    tmp_a.close()
    ready = proj + vals

    out_ready = pr.sem("gla_out_ready")
    for d in range(2):
        with ExitStack() as t:
            n = f"gla{d}"
            z = pr.sb(f"{n}_z", [P, 2, N], ctx=t)
            e = pr.sb(f"{n}_e", [P, 2, N], ctx=t)
            cum = pr.sb(f"{n}_cum", [P, 2, N], ctx=t)
            q_dec = pr.sb(f"{n}_q_dec", [P, 2, N], ctx=t)
            k_inv = pr.sb(f"{n}_k_inv", [P, 2, N], ctx=t)
            k_tok = pr.sb(f"{n}_k_tok", [P, 2, 4, P], ctx=t)
            att = pr.sb(f"{n}_att", [P, GLA_HEADS, N], ctx=t)
            states = pr.sb(f"{n}_states", [P, 2, 8, 2 * P], ctx=t)
            g_end = pr.sb(f"{n}_g_end", [P, 2, 8], ctx=t)
            (z_ready, abs_ready, e_ready, l_ready, b_ready, exp_ready, dec_ready, turned, k_ready, u_ready,
             s_ready, a_done, a_out, o_done, zeroed) = (pr.sem(f"{n}_{x}") for x in (
                 "gate_products", "abs_ready", "exp_ready", "log_ready", "cumsum_ready", "decays_ready",
                 "decayed", "turned", "k_tokens_ready", "updates_ready", "states_ready", "scores_done",
                 "scores_out", "outputs_done", "zeroed"))
            k_end = e

            def update(b, ch):
                at = (ch // 2 % 2) * 256
                return ps[:, 4 * b + 2 * (ch % 2) + ch // 4, at:at + 256]

            @pr.block.gpsimd
            def _(pool):
                for w in ready:
                    pool.wait_ge(*w)
                if d:
                    pool.wait_ge(out_ready, GLA_HEADS)
                nc.gpsimd.memset(att[:], 0.0).then_inc(zeroed, 1)
                nc.gpsimd.memset(states[:], 0.0).then_inc(zeroed, 1)

            @pr.block.tensor
            def _(pe):
                for w in ready:
                    pe.wait_ge(*w)
                if d:
                    pe.wait_ge(out_ready, GLA_HEADS)
                for b in range(2):
                    at = d * 256 + b * P
                    last = nc.tensor.matmul(ps[:, b, :], c("gate_up")[32:64, at:at + P], pa[32:64, 5, :],
                                            start=True, stop=True)
                last.then_inc(z_ready, 1)
                pe.wait_ge(dec_ready, 3)
                for h in range(GLA_HEADS):
                    rows = slice(64 * (h % 2), 64 * (h % 2) + 64)
                    for i in range(4):
                        cols = slice(i * P, (i + 1) * P)
                        last = nc.tensor.matmul(ps[:, h, cols], k_inv[rows, h // 2, cols],
                                                q_dec[rows, h // 2, cols], start=True, stop=True)
                    last.then_inc(a_done, 1)
                for b in range(2):
                    for i in range(4):
                        last = nc.tensor.transpose(ps[:, 4 + b, i * P:(i + 1) * P],
                                                   k_end[:, b, i * P:(i + 1) * P], c("ident"))
                    last.then_inc(turned, 1)
                pe.wait_ge(k_ready, 2)
                pe.wait_ge(a_out, GLA_HEADS)
                for b in range(2):
                    for ch in range(8):
                        rows = slice(64 * (ch % 2), 64 * (ch % 2) + 64)
                        last = nc.tensor.matmul(
                            update(b, ch),
                            k_tok[rows, b, ch // 2, :], gv[rows, ch // 2, b * 256:(b + 1) * 256],
                            start=True, stop=True)
                    last.then_inc(u_ready, 1)
                pe.wait_ge(s_ready, 14)
                for h in range(GLA_HEADS):
                    rows = slice(64 * (h % 2), 64 * (h % 2) + 64)
                    for i in range(4):
                        cols = slice(i * P, (i + 1) * P)
                        nc.tensor.matmul(ps[:, h, cols], gv[:, i, h * P:(h + 1) * P], att[:, h, cols],
                                         start=True, stop=False)
                        for ch in (2 * i, 2 * i + 1):
                            cc = slice(ch * CH, (ch + 1) * CH)
                            last = nc.tensor.matmul(ps[:, h, cc],
                                                    states[rows, h // 2, ch, (h % 2) * P:(h % 2 + 1) * P],
                                                    q_dec[rows, h // 2, cc], start=False, stop=(ch == 2 * i + 1))
                    last.then_inc(o_done, 1)

            @pr.block.scalar
            def _(act):
                act.wait_ge(abs_ready, 1)
                nc.scalar.activation(e[:], e[:], ACT.Exp, scale=-1.0).then_inc(e_ready, 1)
                act.wait_ge(e_ready, 1)
                nc.scalar.activation(e[:], e[:], ACT.Ln, bias=1.0).then_inc(l_ready, 1)
                act.wait_ge(b_ready, 2)
                nc.scalar.activation(q_dec[:], z[:] if d else cum[:], ACT.Exp, scale=1.0 / 16).then_inc(exp_ready, 1)
                nc.scalar.activation(k_inv[:], z[:] if d else cum[:], ACT.Exp, scale=-1.0 / 16).then_inc(exp_ready, 1)
                nc.scalar.activation(k_end[:], e[:], ACT.Exp, scale=1.0 / 16).then_inc(exp_ready, 1)
                tot = cum[:].rearrange("p b (c t) -> p b c t", t=CH)[:, :, :, CH - 1]
                nc.scalar.activation(g_end[:], tot, ACT.Exp, scale=1.0 / 16).then_inc(exp_ready, 1)
                for b in range(2):
                    act.wait_ge(turned, b + 1)
                    nc.scalar.activation(k_tok[:, b].rearrange("p i n -> p (i n)"), ps[:, 4 + b, :],
                                         ACT.Copy).then_inc(k_ready, 1)

            @pr.block.vector
            def _(dve):
                ch = pr.dve_chain
                dve.wait_ge(z_ready, 1)
                for b in range(2):
                    bias = c("gate_bias")[:, 2 * d + b:2 * d + b + 1]
                    last = nc.vector.tensor_scalar(z[:, b, :], ps[:, b, :], bias, None, ALU.add)
                ch.then(dve, last)
                nc.vector.scalar_tensor_tensor(e[:], z[:], -1.0, z[:], ALU.mult, ALU.max).then_inc(abs_ready, 1)
                dve.wait_ge(l_ready, 1)
                ch.then(dve, nc.vector.scalar_tensor_tensor(z[:], z[:], 0.0, e[:], ALU.min, ALU.subtract))
                for b in range(2):
                    last = nc.vector.tensor_tensor_scan(cum[:, b, :], c("chunk_start"), z[:, b, :], 0.0,
                                                        ALU.mult, ALU.add)
                ch.then(dve, last)
                blocks = [x.rearrange("p b (c t) -> p (b c) t", t=CH) for x in (cum[:], z[:], e[:])]
                cum_c, z_c, e_c = blocks
                tot = cum_c[:, :, CH - 1:CH].broadcast_to([P, 16, CH])
                if d == 0:
                    nc.vector.tensor_tensor(e_c, tot, cum_c, ALU.subtract).then_inc(b_ready, 2)
                else:
                    ch.then(dve, nc.vector.tensor_tensor(e[:], cum[:], z[:], ALU.subtract))
                    nc.vector.tensor_tensor(z_c, tot, e_c, ALU.subtract).then_inc(b_ready, 2)
                dve.wait_ge(exp_ready, 4)
                nc.vector.scalar_tensor_tensor(q_dec[:], pb[:, 0:2, :], GLA_DK ** -0.5, q_dec[:],
                                               ALU.mult, ALU.mult).then_inc(dec_ready, 1)
                nc.vector.tensor_tensor(k_inv[:], pb[:, 2:4, :], k_inv[:], ALU.mult).then_inc(dec_ready, 1)
                nc.vector.tensor_tensor(k_end[:], pb[:, 2:4, :], k_end[:], ALU.mult).then_inc(dec_ready, 1)
                dve.wait_ge(zeroed, 2)
                mask = c("gla_b" if d else "gla_f").bitcast(U32)
                for h in range(GLA_HEADS):
                    dve.wait_ge(a_done, h + 1)
                    nc.vector.copy_predicated(att[:, h, :].rearrange("p (i n) -> p i n", n=P),
                                              spread(mask, 1, 4),
                                              ps[:, h, :].rearrange("p (i n) -> p i n", n=P)).then_inc(a_out, 1)
                order = [7, 6, 5, 4, 3, 2, 1, 0] if d else [4, 5, 6, 7, 0, 1, 2, 3]
                for b in range(2):
                    dve.wait_ge(u_ready, b + 1)
                    for i in range(7):
                        a, z1 = order[i], order[i + 1]
                        if i:
                            dve.wait_ge(s_ready, 7 * b + i)
                        nc.vector.scalar_tensor_tensor(
                            states[:, b, z1, :], states[:, b, a, :], g_end[:, b, a:a + 1],
                            update(b, a),
                            ALU.mult, ALU.add).then_inc(s_ready, 1)
                for h in range(GLA_HEADS):
                    dve.wait_ge(o_done, h + 1)
                    if d == 0:
                        ins = nc.vector.tensor_copy(y[:, 4 + h, :], ps[:, h, :])
                    else:
                        ins = nc.vector.tensor_tensor(y[:, 4 + h, :], ps[:, h, :], y[:, 4 + h, :], ALU.add)
                    ins.then_inc(out_ready, 1)

    with ExitStack() as t:
        gla = y[:, 4:8, :]
        gla_ready = [(out_ready, 2 * GLA_HEADS)]
        gate_ready, done = pr.sem("gla_gate_ready"), pr.sem("gla_gated")
        r, _, r_ready = pr.rstd(t, "gla_norm", gla, gla_ready, [[0], [1], [2], [3]], N, GLA_DV, c("ones"))

        @pr.block.scalar
        def _(act):
            nc.scalar.activation(pb[:, 4:8, :], pb[:, 4:8, :], ACT.Silu).then_inc(gate_ready, 1)

        @pr.block.vector
        def _(dve):
            for w in r_ready:
                dve.wait_ge(*w)
            pr.dve_chain.then(dve, nc.vector.tensor_tensor(gla, gla, r[:], ALU.mult))
            dve.wait_ge(gate_ready, 1)
            nc.vector.scalar_tensor_tensor(gla, gla, c("gla_o"), pb[:, 4:8, :], ALU.mult, ALU.mult)\
                .then_inc(done, 1)
    pr.pb_scope.close()
    att_ready = mla(pr, pa, y, [(done, 1)])
    keep.close()
    return att_ready


def mla(pr, pa, y, ready):
    nc, ps, c = pr.nc, pr.ps, pr.c
    N = TA
    scope = ExitStack()
    qT = pr.sb("mla_q", [P, MLA_HEADS, N], ctx=scope)
    kT = pr.sb("mla_k", [P, MLA_HEADS, N], ctx=scope)
    v = pr.sb("mla_v", [P, 4, 512], ctx=scope)
    kr = pr.sb("mla_k_rope", [P, N], ctx=scope)
    with ExitStack() as t:
        parts = {}
        for name, blocks, norm in (("cq", (0, 3), "q_norm"), ("ckv", (3, 5), "kv_norm")):
            nb = blocks[1] - blocks[0]
            src = pa[:, blocks[0]:blocks[1], :]
            hi = pr.sb(f"{name}_h", [P, nb, N], F32R, ctx=t)
            lo = pr.sb(f"{name}_l", [P, nb, N], F32R, ctx=t)
            with ExitStack() as t2:
                r, a, r_ready = pr.rstd(t2, name, src, ready, [list(range(nb))], N, nb * P, c("ones"))
                a_ready = pr.sem(f"{name}_normed")

                @pr.block.vector
                def _(dve):
                    for w in r_ready:
                        dve.wait_ge(*w)
                    for k in range(nb):
                        nc.vector.scalar_tensor_tensor(a[:, k, :], src[:, k, :], c(norm)[:, k:k + 1], r[:, 0, :],
                                                       ALU.mult, ALU.mult).then_inc(a_ready, 1)
                parts[name] = (hi, lo, pr.split_blocks(name, a, a_ready, hi, lo))
                ready = parts[name][2]
        swapped, kr_ready, k_full = pr.sem("kpe_swapped"), pr.sem("k_rope_ready"), pr.sem("k_rope_in_place")

        @pr.block.tensor
        def _(pe):
            for w in ready:
                pe.wait_ge(*w)
            nc.tensor.matmul(ps[:, 4, 0:TL], c("kpe_swap"), pa[:, 5, 0:TL], start=True, stop=True)\
                .then_inc(swapped, 1)

        @pr.block.vector
        def _(dve):
            r = slice(64, P)
            nc.vector.tensor_copy(kr[r, TL:TA], pa[r, 5, TL:TA])
            pr.dve_chain.then(dve, nc.vector.tensor_tensor(kr[r, 0:TL], pa[r, 5, 0:TL], c("kr_cos")[r, :], ALU.mult))
            dve.wait_ge(swapped, 1)
            pr.dve_chain.then(dve, nc.vector.tensor_tensor(pa[r, 5, 0:TL], ps[r, 4, 0:TL], c("kr_sin")[r, :], ALU.mult))
            nc.vector.tensor_tensor(kr[r, 0:TL], kr[r, 0:TL], pa[r, 5, 0:TL], ALU.add).then_inc(kr_ready, 1)

        @pr.block.gpsimd
        def _(pool):
            pool.wait_ge(kr_ready, 1)
            nc.gpsimd.tensor_copy(kT[64:P, :, :], spread(kr[64:P, :], 1, MLA_HEADS)).then_inc(k_full, 1)

        def q_out(q, which, eng, bank):
            nc.vector.tensor_tensor(qT[:, q, 0:TL], bank[:, 0:TL], c("mla_q"), ALU.mult)
            return nc.vector.tensor_scalar(qT[:, q, TL:TA], bank[:, TL:TA], c("mla_qc"), None, ALU.mult)

        def k_out(q, which, eng, bank):
            if which == "act":
                return nc.scalar.activation(kT[0:64, q, :], bank[0:64, :], ACT.Copy)
            return nc.vector.tensor_copy(kT[0:64, q, :], bank[0:64, :])

        cqh, cql, cq_ready = parts["cq"]
        ckh, ckl, ck_ready = parts["ckv"]
        q_ready = pr.linear("mla_uq", 2, 4, 8, pr.features(cqh, cql, N, 3, lambda q, k: ((q % 4) * 3 + k) * P),
                            q_out, cq_ready, engines=("dve",))
        k_ready = pr.linear("mla_uk", 1, 8, 8, pr.features(ckh, ckl, N, 2, lambda q, k: (q * 2 + k) * P),
                            k_out, ck_ready + q_ready)
        v_ready = pr.linear("mla_uv", 1, 4, 4, pr.tokens(ckh, ckl, 4, 512, 2),
                            pr.copy_out(lambda q: v[:, q, :]), k_ready)
        ready = q_ready + k_ready + v_ready + [(k_full, 1)]

    tasks = [(i, h) for i in range(4) for h in range(MLA_HEADS)]
    with ExitStack() as t:
        att = pr.sb("mla_att", [P, 4, 512], ctx=t)

        def spec(n):
            i, h = tasks[n]
            lo = 0 if i < 2 else TL
            return dict(q=lambda: qT[:, h, i * P:(i + 1) * P], k=lambda: kT[:, h, lo:TA], keys=TA - lo,
                        v=lambda j: v[:, lo // P + j, h * MV:(h + 1) * MV],
                        out=att[:, i, h * MV:(h + 1) * MV])

        done = attention(pr, t, "mla", len(tasks), spec, QK ** -0.5, MV, ready)
        turned, out = pr.sem("mla_out_turned"), pr.sem("mla_out_ready")

        @pr.block.tensor
        def _(pe):
            pe.wait_ge(*done[0])
            for b in range(4):
                for i in range(4):
                    last = nc.tensor.transpose(ps[:, b, i * P:(i + 1) * P], att[:, i, b * P:(b + 1) * P], c("ident"))
                last.then_inc(turned, 1)

        @pr.block.scalar
        def _(act):
            for b in range(4):
                act.wait_ge(turned, b + 1)
                nc.scalar.activation(y[:, b, :], ps[:, b, :], ACT.Copy).then_inc(out, 1)
    scope.close()
    return [(out, 4)]


def attention(pr, scope, name, ntasks, spec, scale, width, ready, mask=None):
    nc, ps, c = pr.nc, pr.ps, pr.c
    keys = max(spec(n)["keys"] for n in range(ntasks))
    prob = pr.sb(f"{name}_prob", [P, 2, keys], ctx=scope)
    prob_t = pr.sb(f"{name}_prob_t", [P, 2, keys], ctx=scope)
    stat = pr.sb(f"{name}_stat", [P, 4, ntasks], ctx=scope)
    logit = pr.sb(f"{name}_logits", [P, 2, keys], ctx=scope) if mask else None
    s_done, m_ready, p_ready, t_done, t_out, o_done, o_out = (pr.sem(f"{name}_{x}") for x in (
        "scores_done", "max_ready", "probs_ready", "turned", "turned_out", "values_done", "values_out"))
    mx, nmx, total, inv = (stat[:, i, :] for i in range(4))

    @pr.block.tensor
    def _(pe):
        for w in ready:
            pe.wait_ge(*w)

        def scores(n):
            s = spec(n)
            if n >= 2:
                pe.wait_ge(p_ready, n - 1)
            nc.tensor.matmul(ps[:, n % 2, 0:s["keys"]], s["q"](), s["k"](), start=True, stop=True)\
                .then_inc(s_done, 1)

        for n in range(min(2, ntasks)):
            scores(n)
        for n in range(ntasks):
            s = spec(n)
            pe.wait_ge(p_ready, n + 1)
            if n >= 2:
                pe.wait_ge(t_out, n - 1)
            for j in range(s["keys"] // P):
                last = nc.tensor.transpose(ps[:, 2 + n % 2, j * P:(j + 1) * P], prob[:, n % 2, j * P:(j + 1) * P],
                                           c("ident"))
            last.then_inc(t_done, 1)
            if n + 2 < ntasks:
                scores(n + 2)
            pe.wait_ge(t_out, n + 1)
            if n >= 2:
                pe.wait_ge(o_out, n - 1)
            for j in range(s["keys"] // P):
                last = nc.tensor.matmul(ps[:, 4 + n % 2, 0:width], prob_t[:, n % 2, j * P:(j + 1) * P], s["v"](j),
                                        start=(j == 0), stop=(j == s["keys"] // P - 1))
            last.then_inc(o_done, 1)

    @pr.block.vector
    def _(dve):
        ch = pr.dve_chain
        for n in range(ntasks + 1):
            if n < ntasks:
                s = spec(n)
                w = s["keys"]
                dve.wait_ge(s_done, n + 1)
                src = ps[:, n % 2, 0:w]
                if mask:
                    if n >= 2:
                        dve.wait_ge(p_ready, n - 1)
                    src = logit[:, n % 2, 0:w]
                    ch.then(dve, nc.vector.scalar_tensor_tensor(src, ps[:, n % 2, 0:w], 1.0, mask(n), ALU.mult,
                                                                ALU.add))
                ch.then(dve, nc.vector.tensor_reduce(mx[:, n:n + 1], src, AX.X, ALU.max))
                nc.vector.tensor_scalar(nmx[:, n:n + 1], mx[:, n:n + 1], -scale, None, ALU.mult).then_inc(m_ready, 1)
            if n >= 1:
                k = n - 1
                dve.wait_ge(p_ready, k + 1)
                ch.then(dve, nc.vector.reciprocal(inv[:, k:k + 1], total[:, k:k + 1]))
                dve.wait_ge(o_done, k + 1)
                nc.vector.tensor_scalar(spec(k)["out"], ps[:, 4 + k % 2, 0:width], inv[:, k:k + 1], None,
                                        ALU.mult).then_inc(o_out, 1)

    @pr.block.scalar
    def _(act):
        for n in range(ntasks + 1):
            if n < ntasks:
                w = spec(n)["keys"]
                act.wait_ge(m_ready, n + 1)
                if n >= 2:
                    act.wait_ge(t_done, n - 1)
                src = logit[:, n % 2, 0:w] if mask else ps[:, n % 2, 0:w]
                nc.scalar.activation(prob[:, n % 2, 0:w], src, ACT.Exp, bias=nmx[:, n:n + 1], scale=scale,
                                     accum_out=total[:, n:n + 1]).then_inc(p_ready, 1)
            if n >= 1:
                k = n - 1
                w = spec(k)["keys"]
                act.wait_ge(t_done, k + 1)
                if k >= 2:
                    act.wait_ge(o_done, k - 1)
                nc.scalar.activation(prob_t[:, k % 2, 0:w], ps[:, 2 + k % 2, 0:w], ACT.Copy).then_inc(t_out, 1)

    return [(o_out, ntasks)]


def odd_mixer(pr, mod, scope, norm_w, ready):
    nc, ps, c = pr.nc, pr.ps, pr.c
    N, H = TA, GDN_HEADS
    ch = pr.dve_chain
    y = pr.sb("odd_y", [P, H, TL], ctx=scope)
    inner = ExitStack()
    gate = pr.sb("odd_gate", [P, H, TL], ctx=inner)
    kT = pr.sb("odd_kT", [P, 4, N], ctx=inner)
    qT = pr.sb("odd_qT", [P, 4, TL], ctx=inner)
    k_tok = pr.sb("odd_k_tok", [P, 4, 512], ctx=inner)
    v_tok = pr.sb("odd_v_tok", [P, 4, 1024], ctx=inner)
    ab = pr.sb("odd_ab", [P, 4, 32], ctx=inner)
    pre_scope = ExitStack()
    pre = pr.sb("odd_conv", [P, 8, N], ctx=pre_scope)
    tmp_a = ExitStack()
    high = pr.sb("a1_h", [P, KD, N], F32R, ctx=tmp_a)
    low = pr.sb("a1_l", [P, KD, N], F32R, ctx=tmp_a)
    a_ready = pr.norm_modulate("norm1_1", norm_w, mod, 2, 0, 8, N, high, low, ready, work=pre)

    g_ready = pr.linear("odd_g", 4, 2, 8, pr.features(high, low, TL, KD, tall_offset),
                        pr.copy_out(lambda q: gate[:, q, :]), a_ready)
    ab_ready = pr.linear("odd_ab_in", 1, 4, 4, pr.tokens(high, low, 4, 32, KD),
                         pr.copy_out(lambda q: ab[:, q, :]), g_ready)

    def conv_out(first):
        def evac(q, which, eng, bank):
            tap = lambda n: c("gdn_conv")[:, n * 16 + first + q:n * 16 + first + q + 1]
            src = bank[:, 0:N].rearrange("p (s t) -> p s t", s=2)
            dst = pre[:, q, :].rearrange("p (s t) -> p s t", s=2)
            ch.then(eng, nc.vector.tensor_scalar(dst, src, tap(1), None, ALU.mult))
            ch.then(eng, nc.vector.scalar_tensor_tensor(dst[:, :, 1:TL], src[:, :, 0:TL - 1], tap(0),
                                                        dst[:, :, 1:TL], ALU.mult, ALU.add))
            return nc.vector.scalar_tensor_tensor(dst[:, :, 0:TL - 1], src[:, :, 1:TL], tap(2),
                                                  dst[:, :, 0:TL - 1], ALU.mult, ALU.add)
        return evac

    v_conv = pr.linear("odd_v", 4, 2, 8, pr.features(high, low, N, KD, tall_offset), conv_out(8),
                       ab_ready, engines=("dve",))
    v_act, v_turned, v_ready = pr.sem("odd_v_activated"), pr.sem("odd_v_turned"), pr.sem("odd_v_tokens")

    @pr.block.scalar
    def _(act):
        for q in range(8):
            act.wait_ge(v_conv[0][0], q + 1)
            nc.scalar.activation(pre[:, q, :], pre[:, q, :], ACT.Silu).then_inc(v_act, 1)

    @pr.block.tensor
    def _(pe):
        for q in range(8):
            pe.wait_ge(v_act, q + 1)
            if q >= 2:
                pe.wait_ge(v_ready, q - 1)
            for i in range(4):
                last = nc.tensor.transpose(ps[:, 4 + q % 2, i * P:(i + 1) * P], pre[:, q, i * P:(i + 1) * P],
                                           c("ident"))
            last.then_inc(v_turned, 1)

    @pr.block.vector
    def _(dve):
        for q in range(8):
            dve.wait_ge(v_turned, q + 1)
            nc.vector.tensor_copy(v_tok[:, :, q * P:(q + 1) * P],
                                  ps[:, 4 + q % 2, :].rearrange("p (i n) -> p i n", n=P)).then_inc(v_ready, 1)

    qk_conv = pr.linear("odd_qk", 4, 2, 8, pr.features(high, low, N, KD, tall_offset), conv_out(0),
                        [(v_ready, 8)], engines=("dve",))
    tmp_a.close()
    qk_act = pr.sem("odd_qk_activated")

    @pr.block.scalar
    def _(act):
        act.wait_ge(*qk_conv[0])
        nc.scalar.activation(pre[:], pre[:], ACT.Silu).then_inc(qk_act, 1)

    normed = pr.sem("odd_qk_normed")
    k_turned, kt_ready = pr.sem("odd_k_turned"), pr.sem("odd_k_tokens")
    with ExitStack() as t:
        r, _, r_ready = pr.rstd(t, "odd_k", pre[:, 4:8, :], [(qk_act, 1)], [[0], [1], [2], [3]], N, 1, c("block64"))

        @pr.block.vector
        def _(dve):
            for w in r_ready:
                dve.wait_ge(*w)
            nc.vector.tensor_tensor(kT[:], pre[:, 4:8, :], r[:], ALU.mult).then_inc(normed, 1)

    with ExitStack() as t:
        r, _, r_ready = pr.rstd(t, "odd_q", pre[:, 0:4, 0:TL], [(normed, 1)], [[0], [1], [2], [3]], TL, 1,
                                c("block64"), bank=4)

        @pr.block.vector
        def _(dve):
            for w in r_ready:
                dve.wait_ge(*w)
            nc.vector.scalar_tensor_tensor(qT[:], pre[:, 0:4, 0:TL], GDN_DK ** -0.5, r[:], ALU.mult, ALU.mult)\
                .then_inc(normed, 1)

    @pr.block.tensor
    def _(pe):
        pe.wait_ge(normed, 2)
        for b in range(4):
            for i in range(4):
                last = nc.tensor.transpose(ps[:, b, i * P:(i + 1) * P], kT[:, b, i * P:(i + 1) * P], c("ident"))
            last.then_inc(k_turned, 1)

    @pr.block.vector
    def _(dve):
        for b in range(4):
            dve.wait_ge(k_turned, b + 1)
            nc.vector.tensor_copy(k_tok[:, :, b * P:(b + 1) * P],
                                  ps[:, b, :].rearrange("p (i n) -> p i n", n=P)).then_inc(kt_ready, 1)
    pre_scope.close()

    t = ExitStack()
    la = pr.sb("odd_log_a", [P, 4, 16], ctx=t)
    tmp = pr.sb("odd_gate_tmp", [P, 4, 16], ctx=t)
    beta = pr.sb("odd_beta", [P, 4, 16], ctx=t)
    rate = pr.sb("odd_rate", [P, 16], ctx=t)
    G = pr.sb("odd_g_sum", [P, 4, 16], ctx=t)
    e_g = pr.sb("odd_exp_g", [P, 4, 16], ctx=t)
    e_end = pr.sb("odd_exp_end", [P, 4, 16], ctx=t)
    e_tot = pr.sb("odd_exp_total", [P, 4, 16], ctx=t)
    decay = pr.sb("odd_state_decay", [P, 4, 2, 4], ctx=t)
    abs_ready, exp_ready, ln_ready, la_ready, g_done, g_out, eg_ready, gates = (pr.sem(f"odd_{x}") for x in (
        "abs_ready", "gate_exp", "gate_log", "log_a_ready", "decay_sums", "g_sums_out", "exp_g_ready",
        "gates_ready"))

    @pr.block.vector
    def _(dve):
        for w in ab_ready:
            dve.wait_ge(*w)
        ch.then(dve, nc.vector.tensor_tensor(la[:], ab[:, :, 0:16], spread(c("dt_bias"), 1, 4), ALU.add))
        nc.vector.scalar_tensor_tensor(tmp[:], la[:], -1.0, la[:], ALU.mult, ALU.max).then_inc(abs_ready, 1)
        dve.wait_ge(ln_ready, 1)
        ch.then(dve, nc.vector.scalar_tensor_tensor(la[:], la[:], 0.0, tmp[:], ALU.max, ALU.add))
        nc.vector.scalar_tensor_tensor(la[:], la[:], -1.0, spread(rate[:], 1, 4), ALU.mult, ALU.mult)\
            .then_inc(la_ready, 1)
        dve.wait_ge(g_done, 1)
        g = ps[:, 4, 0:64].rearrange("p (i n) -> p i n", i=4)
        total = ps[:, 4, 64:128].rearrange("p (i n) -> p i n", i=4)
        for d in range(2):
            last = nc.vector.tensor_copy(G[:, :, 8 * d:8 * d + 8],
                                         ps[:, 4, 32 * d:32 * d + 32].rearrange("p (i n) -> p i n", i=4))
        ch.then(dve, last)
        nc.vector.tensor_tensor(e_end[:], total, G[:], ALU.subtract).then_inc(g_out, 1)
        dve.wait_ge(eg_ready, 3)
        tot_v = e_tot[:].rearrange("p i (d r b) -> p i d r b", d=2, r=2)
        for r in range(2):
            rows = slice(64 * r, 64 * r + 64)
            for d in range(2):
                last = nc.vector.tensor_copy(decay[rows, :, d, :], tot_v[rows, :, d, r, :])
        last.then_inc(gates, 1)

    @pr.block.scalar
    def _(act):
        act.wait_ge(normed, 2)
        nc.scalar.activation(rate[:], c("a_log"), ACT.Exp)
        act.wait_ge(abs_ready, 1)
        nc.scalar.activation(tmp[:], tmp[:], ACT.Exp, scale=-1.0).then_inc(exp_ready, 1)
        act.wait_ge(exp_ready, 1)
        nc.scalar.activation(tmp[:], tmp[:], ACT.Ln, bias=1.0).then_inc(ln_ready, 1)
        act.wait_ge(g_out, 1)
        nc.scalar.activation(e_tot[:], ps[:, 4, 64:128].rearrange("p (i n) -> p i n", i=4), ACT.Exp)\
            .then_inc(eg_ready, 1)
        nc.scalar.activation(e_g[:], G[:], ACT.Exp).then_inc(eg_ready, 1)
        nc.scalar.activation(e_end[:], e_end[:], ACT.Exp).then_inc(eg_ready, 1)
        nc.scalar.activation(beta[:], ab[:, :, 16:32], ACT.Sigmoid).then_inc(gates, 1)

    @pr.block.tensor
    def _(pe):
        pe.wait_ge(la_ready, 1)
        for d, tri in enumerate(("tri_f", "tri_b")):
            nc.tensor.matmul(ps[:, 4, 32 * d:32 * d + 32].rearrange("p (i n) -> p i n", i=4), c(tri),
                             la[:, :, 8 * d:8 * d + 8], start=True, stop=True)
        nc.tensor.matmul(ps[:, 4, 64:128].rearrange("p (i n) -> p i n", i=4), c("ones"), la[:],
                         start=True, stop=True).then_inc(g_done, 1)

    big = lambda name: pr.sb(f"odd_{name}", [P, H, P], ctx=t)
    Dt, E, X, Y, T, Dm, QKt, e_row, v_new = (big(x) for x in ("D", "E", "X", "Y", "T", "Dm", "QKt", "e_row", "v_new"))
    q_dec = pr.sb("odd_q_dec", [P, 4, P], ctx=t)
    w_t = pr.sb("odd_w", [P, 4, P], ctx=t)
    keg = pr.sb("odd_keg", [P, H, 64], ctx=t)
    kend = pr.sb("odd_kend", [P, H, 64], ctx=t)
    S = pr.sb("odd_S", [P, 4, P], ctx=t)
    names = ("row_sums", "kk_products", "scores_products", "diffs_ready", "decay_ready", "d_ready", "level_masked",
             "t_products", "t_out", "x_products", "y_products", "x_out", "y_out", "qk_ready", "q_dec_ready",
             "keg_ready", "kend_ready", "w_products", "w_out", "u_products", "v_new_ready", "o_products", "o_out",
             "s_products", "s_ready")
    (row_done, kk_done, qk_done, diff_ready, e_ready, d_ready, dm, t_done, t_out, x_done, y_done, xo, yo,
     qk_ready, qd_ready, keg_ready, kend_ready, w_done, w_out, u_done, vn_ready, o_done, o_out, s_done,
     s_ready) = (pr.sem(f"rule_{x}") for x in names)
    half = lambda buf, a: buf[:, 4 * a:4 * a + 4, :]
    bank = lambda b, n=2: ps[:, b:b + n, :].rearrange("p b (s n) -> p (b s) n", n=P)
    steps = [(0, i) for i in (2, 3, 0, 1)] + [(1, i) for i in (3, 2, 1, 0)]
    lats = 0
    for idx, (d, i) in enumerate(steps):
        lat, fresh = i < 2, idx % 4 == 0
        cols = slice(i * P, (i + 1) * P)
        tri = c("tri_b" if d else "tri_f")
        lev = c("lev_b" if d else "lev_f").rearrange("p (l n) -> p l n", n=P)
        gs = slice(8 * d, 8 * d + 8)

        @pr.block.tensor
        def _(pe):
            if idx == 0:
                pe.wait_ge(gates, 2)
                pe.wait_ge(kt_ready, 4)
            else:
                pe.wait_ge(vn_ready, idx)
            for s in range(H):
                last = nc.tensor.matmul(ps[:, s // 4, (s % 4) * P:(s % 4 + 1) * P],
                                        la[:, i, 8 * d + s:8 * d + s + 1].broadcast_to([P, P]), tri,
                                        start=True, stop=True)
            last.then_inc(row_done, 1)
            if lats:
                pe.wait_ge(o_out, lats)
            for s in range(H):
                rows, b = slice(64 * (s // 4), 64 * (s // 4) + 64), s % 4
                last = nc.tensor.matmul(ps[:, 2 + s // 4, b * P:(b + 1) * P], kT[rows, b, cols], kT[rows, b, cols],
                                        start=True, stop=True)
            last.then_inc(kk_done, 1)
            if lat:
                for s in range(H):
                    rows, b = slice(64 * (s // 4), 64 * (s // 4) + 64), s % 4
                    last = nc.tensor.matmul(ps[:, 4 + s // 4, b * P:(b + 1) * P], kT[rows, b, cols],
                                            qT[rows, b, cols], start=True, stop=True)
                last.then_inc(qk_done, 1)

            def t_products(n, a):
                pe.wait_ge(dm, n * 2 + (14 * idx + a + 1))
                if not isinstance(n, int) or n:
                    pe.wait_ge(xo, n * 2 + (12 * idx + a - 1))
                    for s in range(4 * a, 4 * a + 4):
                        last = nc.tensor.matmul(ps[:, a, (s % 4) * P:(s % 4 + 1) * P], Dm[:, s, :], X[:, s, :],
                                                start=True, stop=True)
                else:
                    for s in range(4 * a, 4 * a + 4):
                        last = nc.tensor.matmul(ps[:, a, (s % 4) * P:(s % 4 + 1) * P], Dm[:, s, :], c("ident"),
                                                start=True, stop=True)
                last.then_inc(t_done, 1)

            def xy_products(n, a, want_x):
                pe.wait_ge(t_out, n * 2 + (12 * idx + a - 1))
                pe.wait_ge(yo, n * 2 + (14 * idx + a - 1))
                at = lambda s: slice((s % 4) * P, (s % 4 + 1) * P)
                if want_x:
                    for s in range(4 * a, 4 * a + 4):
                        last = nc.tensor.matmul(ps[:, 2 + a, at(s)], Y[:, s, :], T[:, s, :], start=True, stop=True)
                    last.then_inc(x_done, 1)
                for s in range(4 * a, 4 * a + 4):
                    last = nc.tensor.matmul(ps[:, 4 + a, at(s)], T[:, s, :], Y[:, s, :], start=True, stop=True)
                last.then_inc(y_done, 1)

            for a in range(2):
                t_products(0, a)
            with pe.Fori(1, LEVELS - 1) as n:
                for a in range(2):
                    t_products(n, a)
                for a in range(2):
                    xy_products(n, a, True)
            for a in range(2):
                t_products(LEVELS - 1, a)
            for a in range(2):
                xy_products(LEVELS - 1, a, False)
            pe.wait_ge(yo, 14 * idx + 14)
            pe.wait_ge(keg_ready, idx + 1)
            for s in range(H):
                r, b = s // 4, s % 4
                last = nc.tensor.matmul(ps[64 * r:64 * r + 64, 6, b * P:(b + 1) * P], keg[:, s, :], Y[:, s, :],
                                        start=True, stop=True)
            last.then_inc(w_done, 1)
            pe.wait_ge(w_out, idx + 1)
            pe.wait_ge(s_ready, idx + 1)
            for s in range(H):
                r, b = s // 4, s % 4
                h = GDN_ORDER[s]
                dst = ps[:, r, b * P:(b + 1) * P]
                nc.tensor.matmul(dst, Y[:, s, :], v_tok[:, i, h * P:(h + 1) * P], start=True, stop=False)
                last = nc.tensor.matmul(dst, w_t[64 * r:64 * r + 64, b, :], S[64 * r:64 * r + 64, b, :],
                                        start=False, stop=True)
            last.then_inc(u_done, 1)
            pe.wait_ge(vn_ready, idx + 1)
            if lat:
                pe.wait_ge(qk_ready, lats + 1)
                pe.wait_ge(qd_ready, lats + 1)
                for s in range(H):
                    r, b = s // 4, s % 4
                    rows = slice(64 * r, 64 * r + 64)
                    dst = ps[:, 2 + r, b * P:(b + 1) * P]
                    nc.tensor.matmul(dst, v_new[:, s, :], QKt[:, s, :], start=True, stop=False)
                    last = nc.tensor.matmul(dst, S[rows, b, :], q_dec[rows, b, :], start=False, stop=True)
                last.then_inc(o_done, 1)
            pe.wait_ge(kend_ready, idx + 1)
            for s in range(H):
                r, b = s // 4, s % 4
                last = nc.tensor.matmul(ps[64 * r:64 * r + 64, 7, b * P:(b + 1) * P], kend[:, s, :], v_new[:, s, :],
                                        start=True, stop=True)
            last.then_inc(s_done, 1)

        @pr.block.scalar
        def _(act):
            act.wait_ge(diff_ready, idx + 1)
            if lat:
                if lats:
                    act.wait_ge(qd_ready, lats)
                nc.scalar.activation(e_row[:], bank(0), ACT.Exp)
            nc.scalar.activation(E[:], E[:], ACT.Exp).then_inc(e_ready, 1)

            def t_copy(n, a):
                act.wait_ge(t_done, n * 2 + (14 * idx + a + 1))
                nc.scalar.activation(half(T, a), bank(a, 1), ACT.Copy).then_inc(t_out, 1)

            with act.Fori(1, LEVELS) as n:
                for a in range(2):
                    t_copy(n, a)
            act.wait_ge(w_done, idx + 1)
            nc.scalar.activation(w_t[:], bank(6, 1), ACT.Copy, scale=-1.0).then_inc(w_out, 1)

        @pr.block.gpsimd
        def _(pool):
            pool.wait_ge(d_ready, idx + 1)

            def mask(n, a):
                if n:
                    pool.wait_ge(t_done, 14 * idx + 2 * n + a - 1)
                    if n == 1:
                        pool.wait_ge(yo, 14 * idx + a + 1)
                elif idx:
                    pool.wait_ge(t_done, 14 * idx)
                m = lev[:, n:n + 1, :].broadcast_to([P, 4, P])
                nc.gpsimd.tensor_tensor(half(Dm, a), half(Dt, a), m, ALU.mult).then_inc(dm, 1)

            for n in range(LEVELS):
                for a in range(2):
                    mask(n, a)
            kv = k_tok[:, i, :].rearrange("p (b r n) -> p r b n", r=2, n=64)
            for r in range(2):
                if idx:
                    pool.wait_ge(w_done, idx)
                last = nc.gpsimd.tensor_tensor(keg[:, 4 * r:4 * r + 4, :], kv[:, r], spread(
                    e_g[:, i, 8 * d + 4 * r:8 * d + 4 * r + 4], 2, 64), ALU.mult)
            last.then_inc(keg_ready, 1)
            for r in range(2):
                if idx:
                    pool.wait_ge(s_done, idx)
                last = nc.gpsimd.tensor_tensor(kend[:, 4 * r:4 * r + 4, :], kv[:, r], spread(
                    e_end[:, i, 8 * d + 4 * r:8 * d + 4 * r + 4], 2, 64), ALU.mult)
            last.then_inc(kend_ready, 1)

        @pr.block.vector
        def _(dve):
            if fresh:
                if idx:
                    dve.wait_ge(s_ready, idx)
                    dve.wait_ge(s_done, idx)
                nc.vector.memset(S[:], 0.0).then_inc(s_ready, 1)
            dve.wait_ge(row_done, idx + 1)
            for s in range(H):
                last = nc.vector.tensor_scalar(E[:, s, :], ps[:, s // 4, (s % 4) * P:(s % 4 + 1) * P],
                                               G[:, i, 8 * d + s:8 * d + s + 1], 0.0, ALU.subtract, ALU.min)
            last.then_inc(diff_ready, 1)
            dve.wait_ge(kk_done, idx + 1)
            dve.wait_ge(e_ready, idx + 1)
            for s in range(H):
                last = nc.vector.scalar_tensor_tensor(Dt[:, s, :], E[:, s, :], beta[:, i, 8 * d + s:8 * d + s + 1],
                                                      ps[:, 2 + s // 4, (s % 4) * P:(s % 4 + 1) * P],
                                                      ALU.mult, ALU.mult)
            last.then_inc(d_ready, 1)
            if lat:
                dve.wait_ge(qk_done, lats + 1)
                ch.then(dve, nc.vector.tensor_tensor(QKt[:], bank(4), E[:], ALU.mult))
                nc.vector.tensor_tensor(QKt[:], QKt[:], spread(tri, 1, H), ALU.mult).then_inc(qk_ready, 1)
                for r in range(2):
                    rows = slice(64 * r, 64 * r + 64)
                    last = nc.vector.tensor_tensor(q_dec[rows, :, :], qT[rows, :, cols],
                                                   e_row[rows, 4 * r:4 * r + 4, :], ALU.mult)
                last.then_inc(qd_ready, 1)
            eye = spread(c("ident"), 1, 4)
            for a in range(2):
                dve.wait_ge(t_done, 14 * idx + a + 1)
                nc.vector.tensor_tensor(half(X, a), eye, bank(a, 1), ALU.subtract).then_inc(xo, 1)
                nc.vector.tensor_tensor(half(Y, a), eye, half(Dm, a), ALU.subtract).then_inc(yo, 1)

            def update(n, a, want_x):
                if want_x:
                    dve.wait_ge(x_done, n * 2 + (10 * idx + a - 1))
                    dve.wait_ge(xo, n * 2 + (12 * idx + a - 1))
                    nc.vector.tensor_tensor(half(X, a), half(X, a), bank(2 + a, 1), ALU.subtract).then_inc(xo, 1)
                dve.wait_ge(y_done, n * 2 + (12 * idx + a - 1))
                dve.wait_ge(yo, n * 2 + (14 * idx + a - 1))
                nc.vector.tensor_tensor(half(Y, a), half(Y, a), bank(4 + a, 1), ALU.subtract).then_inc(yo, 1)

            with dve.Fori(1, LEVELS - 1) as n:
                for a in range(2):
                    update(n, a, True)
            for a in range(2):
                update(LEVELS - 1, a, False)
            dve.wait_ge(u_done, idx + 1)
            b_row = spread(beta[:, i, gs], 2, P)
            nc.vector.tensor_tensor(v_new[:], bank(0), b_row, ALU.mult).then_inc(vn_ready, 1)
            if lat:
                dve.wait_ge(o_done, lats + 1)
                for r in range(2):
                    dst = y[:, r::2, cols]
                    if d == 0:
                        last = nc.vector.tensor_copy(dst, bank(2 + r, 1))
                    else:
                        last = nc.vector.tensor_tensor(dst, bank(2 + r, 1), dst, ALU.add)
                last.then_inc(o_out, 1)
            dve.wait_ge(s_done, idx + 1)
            if idx % 4 != 3:
                for b in range(4):
                    last = nc.vector.scalar_tensor_tensor(S[:, b, :], S[:, b, :], decay[:, i, d, b:b + 1],
                                                          ps[:, 7, b * P:(b + 1) * P], ALU.mult, ALU.add)
                last.then_inc(s_ready, 1)
        lats += lat
    t.close()

    gate_ready, done = pr.sem("odd_gate_ready"), pr.sem("odd_gated")
    with ExitStack() as t:
        r, _, r_ready = pr.rstd(t, "odd_norm", y[:], [(o_out, lats), (s_done, len(steps))], [[h] for h in range(H)], TL, GDN_DV, c("ones"))

        @pr.block.scalar
        def _(act):
            nc.scalar.activation(gate[:], gate[:], ACT.Silu).then_inc(gate_ready, 1)

        @pr.block.vector
        def _(dve):
            for w in r_ready:
                dve.wait_ge(*w)
            ch.then(dve, nc.vector.tensor_tensor(y[:], y[:], r[:], ALU.mult))
            dve.wait_ge(gate_ready, 1)
            nc.vector.scalar_tensor_tensor(y[:], y[:], c("gdn_o"), gate[:], ALU.mult, ALU.mult).then_inc(done, 1)
    inner.close()
    return y, [(done, 1)]


def rope_tables(pr, pos_in, cos, sin):
    nc, c, ch = pr.nc, pr.c, pr.dve_chain
    turn = 2.0 * math.pi
    c1 = 6.28125
    c2 = float(np.float32(np.round((turn - c1) * 2.0 ** 20) / 2.0 ** 20))
    c3 = turn - c1 - c2
    magic = 1.5 * 2.0 ** 23
    limit = 3.1415925
    angles_ready, ready = pr.sem("angles_ready"), pr.sem("rope_tables_ready")
    with ExitStack() as t:
        ang = pr.sb("rope_angle", [P, TL], ctx=t)
        k = pr.sb("rope_turns", [P, TL], ctx=t)

        @pr.block.vector
        def _(dve):
            dve.wait_ge(pos_in, 16)
            ch.then(dve, nc.vector.tensor_copy(k[:], pr.pos_sb[:]))
            ch.then(dve, nc.vector.tensor_scalar(ang[:], k[:], c("invf"), None, ALU.mult))
            for dst, quarter in ((sin, 0.0), (cos, 0.25)):
                ch.then(dve, nc.vector.tensor_scalar(k[:], ang[:], 1.0 / turn, quarter, ALU.mult, ALU.add))
                ch.then(dve, nc.vector.tensor_scalar(k[:], k[:], magic, None, ALU.add))
                ch.then(dve, nc.vector.tensor_scalar(k[:], k[:], magic, None, ALU.subtract))
                ch.then(dve, nc.vector.scalar_tensor_tensor(dst[:], k[:], -c1, ang[:], ALU.mult, ALU.add))
                ch.then(dve, nc.vector.scalar_tensor_tensor(dst[:], k[:], -c2, dst[:], ALU.mult, ALU.add))
                ch.then(dve, nc.vector.scalar_tensor_tensor(dst[:], k[:], -c3, dst[:], ALU.mult, ALU.add))
                ch.then(dve, nc.vector.tensor_scalar(dst[:], dst[:], quarter * turn, limit, ALU.add, ALU.min))
                last = nc.vector.tensor_scalar(dst[:], dst[:], -limit, None, ALU.max)
                last.then_inc(angles_ready, 1)

        @pr.block.scalar
        def _(act):
            act.wait_ge(angles_ready, 2)
            nc.scalar.activation(sin[:], sin[:], ACT.Sin).then_inc(ready, 1)
            nc.scalar.activation(cos[:], cos[:], ACT.Sin).then_inc(ready, 1)
    return [(ready, 2)]


def post_add(pr, name, y, y_ready, mod, gate, weight):
    nc, ready = pr.nc, pr.sem(f"{name}_added_to_x")
    with ExitStack() as t:
        r, _, r_ready = pr.rstd(t, name, y, y_ready, [list(range(KD))], TL, D, pr.c("ones"))
        gain = pr.sb(f"{name}_gain", [P, KD], ctx=t)

        @pr.block.vector
        def _(dve):
            for w in r_ready:
                dve.wait_ge(*w)
            nc.vector.tensor_tensor(gain[:], mod[:, gate:gate + KD, 0], weight, ALU.mult)
            pr.dve_chain.then(dve, nc.vector.tensor_tensor(y, y, r[:].broadcast_to([P, KD, TL]), ALU.mult))
            for k in range(KD):
                x = pr.xT[:, k, 0:TL]
                last = nc.vector.scalar_tensor_tensor(x, y[:, k, :], gain[:, k:k + 1], x, ALU.mult, ALU.add)
            last.then_inc(ready, 1)
    return [(ready, 1)]


def hybrid_mixer(pr, l, mod, y, cos, sin, pre_w, ready):
    nc, ps, c, ch = pr.nc, pr.ps, pr.c, pr.dve_chain
    N = TL
    CQ, KA, QM, OM, KI = 0, 2, 6, 14, 18
    inner = ExitStack()
    pj = pr.sb("mix_proj", [P, 19, N], ctx=inner)
    vt = pr.sb("mix_v", [P, 2, 512], ctx=inner)
    vm = pr.sb("mix_vm", [P, 2, 512], ctx=inner)
    sm = pr.sb("mix_small", [P, 2, 32], ctx=inner)
    qr = pr.sb("mix_q", [P, 8, N], ctx=inner)
    tmp_a = ExitStack()
    high = pr.sb("mix_a_h", [P, KD, N], F32R, ctx=tmp_a)
    low = pr.sb("mix_a_l", [P, KD, N], F32R, ctx=tmp_a)
    a_ready = pr.norm_modulate("mix_pre", pre_w, mod, 1, 0, 8, N, high, low, ready)

    def in_out(q, which, eng, bank):
        dst, src = pj[:, q, :], bank[:, 0:N]
        if which == "act":
            return nc.scalar.activation(dst, src, ACT.Copy)
        b = q - QM
        tap = lambda n: c("conv_w")[:, l * 32 + n * 8 + b:l * 32 + n * 8 + b + 1]
        bias = c("conv_b")[:, l * 8 + b:l * 8 + b + 1]
        ch.then(eng, nc.vector.tensor_scalar(dst, src, tap(3), bias, ALU.mult, ALU.add))
        for back in (1, 2, 3):
            last = nc.vector.scalar_tensor_tensor(dst[:, back:N], src[:, 0:N - back], tap(3 - back),
                                                  dst[:, back:N], ALU.mult, ALU.add)
            if back < 3:
                ch.then(eng, last)
        return last

    who = ["dve" if QM <= q < QM + 8 else "act" for q in range(19)]
    in_ready = pr.linear("mix_in", 10, 2, 19, pr.features(high, low, N, KD, tall_offset), in_out, a_ready,
                         engines=who)
    vals = lambda dst: pr.copy_out(lambda q: dst[:, q % 2, (q // 2) * PC:(q // 2 + 1) * PC])
    vt_ready = pr.linear("mix_v_in", 2, 2, 4, pr.tokens(high, low, 2, PC, KD), vals(vt), in_ready)
    vm_ready = pr.linear("mix_vm_in", 2, 2, 4, pr.tokens(high, low, 2, PC, KD), vals(vm), vt_ready)
    sm_ready = pr.linear("mix_small_in", 1, 2, 2, pr.tokens(high, low, 2, 32, KD),
                         pr.copy_out(lambda q: sm[:, q, :]), vm_ready)
    tmp_a.close()
    proj_ready = in_ready + vt_ready + vm_ready + sm_ready

    with ExitStack() as t:
        src = pj[:, CQ:CQ + 2, :]
        r, a, r_ready = pr.rstd(t, "mix_cq", src, proj_ready, [[0, 1]], N, 2 * P, c("ones"))
        hi = pr.sb("mix_cq_h", [P, 2, N], F32R, ctx=t)
        lo = pr.sb("mix_cq_l", [P, 2, N], F32R, ctx=t)
        a_ready = pr.sem("mix_cq_normed")

        @pr.block.vector
        def _(dve):
            for w in r_ready:
                dve.wait_ge(*w)
            for k in range(2):
                nc.vector.scalar_tensor_tensor(a[:, k, :], src[:, k, :], c("q_lat")[:, 2 * l + k:2 * l + k + 1],
                                               r[:, 0, :], ALU.mult, ALU.mult).then_inc(a_ready, 1)
        cq_ready = pr.split_blocks("mix_cq", a, a_ready, hi, lo)
        q_ready = pr.linear("mix_q_up", 1, 8, 8, pr.features(hi, lo, N, 2, lambda q, k: (q * 2 + k) * P),
                            pr.copy_out(lambda q: qr[:, q, :]), cq_ready)

    rotated, rope_ready, qk_act = pr.sem("mix_rotated"), pr.sem("mix_rope_ready"), pr.sem("mix_qk_activated")
    flat = lambda x: x.rearrange("p b n -> p (b n)")
    with ExitStack() as t:
        rot = pr.sb("mix_rot", [P, 13, N], ctx=t)

        @pr.block.tensor
        def _(pe):
            for w in q_ready:
                pe.wait_ge(*w)
            srcs = [pj[:, KA:KA + 2, :], pj[:, KA + 2:KA + 4, :]] + [qr[:, 2 * i:2 * i + 2, :] for i in range(4)]
            for i, src in enumerate(srcs):
                nc.tensor.matmul(ps[:, i, :], c("rot"), flat(src), start=True, stop=True)
            nc.tensor.matmul(ps[:, 6, 0:N], c("rot"), pj[:, KI, :], start=True, stop=True).then_inc(rotated, 1)

        @pr.block.vector
        def _(dve):
            dve.wait_ge(rotated, 1)
            for w in proj_ready:
                dve.wait_ge(*w)
            for w in q_ready:
                dve.wait_ge(*w)
            allb = ps[:, 0:7, :].rearrange("p b n -> p (b n)")[:, 0:13 * N].rearrange("p (b n) -> p b n", n=N)
            ch.then(dve, nc.vector.tensor_tensor(rot[:], allb, spread(sin[:], 1, 13), ALU.mult))
            parts = ((pj[:, KA:KA + 4, :], 0, 4), (qr[:], 4, 8), (pj[:, KI:KI + 1, :], 12, 1))
            for x, at, n in parts:
                ch.then(dve, nc.vector.tensor_tensor(x, x, spread(cos[:], 1, n), ALU.mult))
                nc.vector.tensor_tensor(x, x, rot[:, at:at + n, :], ALU.add).then_inc(rope_ready, 1)

        @pr.block.scalar
        def _(act):
            for w in proj_ready:
                act.wait_ge(*w)
            nc.scalar.activation(pj[:, QM:QM + 8, :], pj[:, QM:QM + 8, :], ACT.Silu).then_inc(qk_act, 1)
            nc.scalar.activation(pj[:, OM:OM + 4, :], pj[:, OM:OM + 4, :], ACT.Sigmoid).then_inc(qk_act, 1)

    t = ExitStack()
    att = pr.sb("mix_att", [P, 2, 512], ctx=t)
    hm = pr.sb("mix_hm", [P, 2, 512], ctx=t)
    amask = pr.sb("mix_mask", [P, 2, N], ctx=t)
    causal = c("causal").rearrange("p (i n) -> p i n", i=2)
    i_done, i_relu, i_added, mask_ready = (pr.sem(f"index_{x}") for x in (
        "products", "relu_out", "added", "mask_ready"))
    with ExitStack() as t2:
        relu = pr.sb("index_relu", [P, 2, N], ctx=t2)
        score = pr.sb("index_score", [P, 2, N], ctx=t2)
        work = pr.sb("index_work", [P, 2, N], ctx=t2)
        top = pr.sb("index_top", [P, 8], ctx=t2)
        w_idx = pr.sb("index_weight", [P, 2, 8], ctx=t2)
        tasks = [(i, h) for i in range(2) for h in range(8)]

        @pr.block.tensor
        def _(pe):
            pe.wait_ge(rope_ready, 3)
            for n, (i, h) in enumerate(tasks):
                rows = slice(64 * (h % 2), 64 * (h % 2) + 64)
                if n >= 4:
                    pe.wait_ge(i_relu, n - 3)
                nc.tensor.matmul(ps[:, n % 4, 0:(i + 1) * P], qr[rows, 4 + h // 2, i * P:(i + 1) * P],
                                 pj[rows, KI, 0:(i + 1) * P], start=True, stop=True).then_inc(i_done, 1)

        @pr.block.scalar
        def _(act):
            act.wait_ge(rope_ready, 3)
            for n, (i, h) in enumerate(tasks):
                w = (i + 1) * P
                act.wait_ge(i_done, n + 1)
                if n >= 2:
                    act.wait_ge(i_added, n - 1)
                nc.scalar.activation(relu[:, n % 2, 0:w], ps[:, n % 4, 0:w], ACT.Relu).then_inc(i_relu, 1)

        @pr.block.vector
        def _(dve):
            ch.then(dve, nc.vector.tensor_scalar(w_idx[:], sm[:, :, 0:8], (8 * 64) ** -0.5, None, ALU.mult))
            for n, (i, h) in enumerate(tasks):
                w = (i + 1) * P
                dve.wait_ge(i_relu, n + 1)
                if h:
                    dve.wait_ge(i_added, n)
                nc.vector.scalar_tensor_tensor(score[:, i, 0:w], relu[:, n % 2, 0:w], w_idx[:, i, h:h + 1],
                                               score[:, i, 0:w] if h else causal[:, i, 0:w],
                                               ALU.mult, ALU.add).then_inc(i_added, 1)
            dve.wait_ge(i_added, len(tasks))
            for i in range(2):
                w = (i + 1) * P
                src = score
                for _ in range(TOPK // 8):
                    ch.then(dve, nc.vector.max(top[:], src[:, i, 0:w]))
                    ch.then(dve, nc.vector.match_replace(work[:, i, 0:w], top[:], src[:, i, 0:w], TAKEN))
                    src = work
                ch.then(dve, nc.vector.tensor_scalar(work[:, i, 0:w], work[:, i, 0:w], -2e38, -NEG, ALU.is_lt,
                                                     ALU.mult))
                nc.vector.scalar_tensor_tensor(amask[:, i, 0:w], work[:, i, 0:w], NEG, causal[:, i, 0:w],
                                               ALU.add, ALU.min).then_inc(mask_ready, 1)

    with ExitStack() as t2:
        def spec(n):
            i, h = n // 8, n % 8
            rows = slice(64 * (h % 2), 64 * (h % 2) + 64)
            return dict(q=lambda: qr[rows, h // 2, i * P:(i + 1) * P], k=lambda: pj[rows, KA + h // 2, 0:(i + 1) * P],
                        keys=(i + 1) * P, v=lambda j: vt[:, j, h * 64:(h + 1) * 64],
                        out=att[:, i, h * 64:(h + 1) * 64])

        def mask(n):
            return amask[:, n // 8, 0:(n // 8 + 1) * P]

        att_done = attention(pr, t2, "mix_att", 16, spec, ATT_D ** -0.5, 64, [(mask_ready, 2)], mask=mask)

    with ExitStack() as t2:
        gates = pr.sb("ml_gates", [P, 6, 2, 4], ctx=t2)
        ig, lf, nlf, tmp, M, B = (gates[:, k] for k in range(6))
        stats = pr.sb("ml_stats", [P, 4, 2, 4], ctx=t2)
        nM, den, em, inv = (stats[:, k] for k in range(4))
        W = pr.sb("ml_weights", [P, 2, 4, N], ctx=t2)
        S = pr.sb("ml_scores", [P, 2, 4, N], ctx=t2)
        St = pr.sb("ml_scores_t", [P, 3, 512], ctx=t2)
        (abs_ready, exp_ready, ln_ready, f_ready, c_done, m_ready, w_ready, s_done, smat, turned, t_out, b_ready,
         em_ready, inv_ready, n_done, hm_ready) = (pr.sem(f"ml_{x}") for x in (
             "abs_ready", "exp_ready", "log_ready", "gates_ready", "row_sums", "max_ready", "weights_ready",
             "scores_done", "weighted", "turned", "turned_out", "m_ready", "floor_ready", "inverse_ready",
             "numerators", "h_ready"))
        free = att_done

        @pr.block.vector
        def _(dve):
            for w in free:
                dve.wait_ge(*w)
            b = lambda name: spread(c(name)[:, 4 * l:4 * l + 4], 1, 2)
            nc.vector.tensor_tensor(ig, sm[:, :, 8:12], b("b_ig"), ALU.add)
            ch.then(dve, nc.vector.tensor_tensor(lf, sm[:, :, 12:16], b("b_fg"), ALU.add))
            nc.vector.scalar_tensor_tensor(tmp, lf, -1.0, lf, ALU.mult, ALU.max).then_inc(abs_ready, 1)
            dve.wait_ge(ln_ready, 1)
            ch.then(dve, nc.vector.scalar_tensor_tensor(lf, lf, 0.0, tmp, ALU.min, ALU.subtract))
            nc.vector.tensor_scalar(nlf, lf, -1.0, None, ALU.mult).then_inc(f_ready, 1)
            dve.wait_ge(c_done, 1)
            row = ps[:, 0:2, :].rearrange("p b (h n) -> p (b h) n", n=N)
            for i in range(2):
                w = (i + 1) * P
                ch.then(dve, nc.vector.tensor_tensor(W[:, i, :, 0:w], row[:, :, 0:w], spread(causal[:, i, 0:w], 1, 4),
                                                     ALU.add))
                ch.then(dve, nc.vector.tensor_reduce(M[:, i], W[:, i, :, 0:w], AX.X, ALU.max))
            ch.then(dve, nc.vector.tensor_scalar(M, M, 0.0, None, ALU.max))
            nc.vector.tensor_scalar(nM, M, -1.0, None, ALU.mult).then_inc(m_ready, 1)
            nc.vector.tensor_tensor(B, M, ps[:, 7, 0:8].rearrange("p (i h) -> p i h", i=2), ALU.add)\
                .then_inc(b_ready, 1)
            for i in range(2):
                w = (i + 1) * P
                dve.wait_ge(s_done, i + 1)
                for h in range(ML_HEADS):
                    dve.wait_ge(w_ready, 4 * i + h + 1)
                    nc.vector.scalar_tensor_tensor(
                        S[:, i, h, 0:w], ps[:, 2 + 2 * i + h // 2, (h % 2) * N:(h % 2) * N + w], ML_D ** -0.5,
                        W[:, i, h, 0:w], ALU.mult, ALU.mult, accum_out=den[:, i, h:h + 1]).then_inc(smat, 1)
            dve.wait_ge(smat, 8)
            ch.then(dve, nc.vector.scalar_tensor_tensor(den, den, -1.0, den, ALU.mult, ALU.max))
            dve.wait_ge(em_ready, 1)
            ch.then(dve, nc.vector.tensor_tensor(den, den, em, ALU.max))
            ch.then(dve, nc.vector.reciprocal(inv, den))
            for i in range(2):
                dve.wait_ge(n_done, i + 1)
                nc.vector.tensor_tensor(hm[:, i, :].rearrange("p (h n) -> p h n", h=4),
                                        ps[:, i, :].rearrange("p (h n) -> p h n", h=4),
                                        spread(inv[:, i], 2, P), ALU.mult).then_inc(hm_ready, 1)

        @pr.block.scalar
        def _(act):
            act.wait_ge(abs_ready, 1)
            nc.scalar.activation(tmp, tmp, ACT.Exp, scale=-1.0).then_inc(exp_ready, 1)
            act.wait_ge(exp_ready, 1)
            nc.scalar.activation(tmp, tmp, ACT.Ln, bias=1.0).then_inc(ln_ready, 1)
            act.wait_ge(m_ready, 1)
            for i in range(2):
                for h in range(ML_HEADS):
                    w = W[:, i, h, 0:(i + 1) * P]
                    nc.scalar.activation(w, w, ACT.Exp, bias=nM[:, i, h:h + 1]).then_inc(w_ready, 1)
            act.wait_ge(b_ready, 1)
            nc.scalar.activation(em, B, ACT.Exp, scale=-1.0).then_inc(em_ready, 1)
            for g, b in enumerate((6, 0, 1)):
                act.wait_ge(turned, g + 1)
                nc.scalar.activation(St[:, g, :], ps[:, b, :], ACT.Copy).then_inc(t_out, 1)

        @pr.block.tensor
        def _(pe):
            pe.wait_ge(f_ready, 1)
            wide = lambda x: x.broadcast_to([P, P])
            for h in range(ML_HEADS):
                at = lambda j: ps[:, h // 2, (h % 2) * N + j * P:(h % 2) * N + (j + 1) * P]
                nc.tensor.matmul(at(0), wide(nlf[:, 0, h:h + 1]), c("tri_f"), start=True, stop=False)
                nc.tensor.matmul(at(0), wide(ig[:, 0, h:h + 1]), c("ident"), start=False, stop=True)
                nc.tensor.matmul(at(1), wide(nlf[:, 1, h:h + 1]), c("tri_f"), start=True, stop=False)
                nc.tensor.matmul(at(1), wide(nlf[:, 0, h:h + 1]), c("ones"), start=False, stop=False)
                nc.tensor.matmul(at(1), wide(ig[:, 1, h:h + 1]), c("ident"), start=False, stop=True)
            nc.tensor.matmul(ps[:, 7, 0:4], c("tri_f"), lf[:, 0], start=True, stop=True)
            nc.tensor.matmul(ps[:, 7, 4:8], c("tri_f"), lf[:, 1], start=True, stop=False)
            nc.tensor.matmul(ps[:, 7, 4:8], c("ones"), lf[:, 0], start=False, stop=True).then_inc(c_done, 1)
            pe.wait_ge(qk_act, 2)
            for i in range(2):
                w = (i + 1) * P
                for h in range(ML_HEADS):
                    last = nc.tensor.matmul(ps[:, 2 + 2 * i + h // 2, (h % 2) * N:(h % 2) * N + w],
                                            pj[:, QM + h, i * P:(i + 1) * P], pj[:, QM + 4 + h, 0:w],
                                            start=True, stop=True)
                last.then_inc(s_done, 1)
            pe.wait_ge(b_ready, 1)
            turns = [(6, 0, 0), (0, 1, 0), (1, 1, 1)]
            for g, (b, i, j) in enumerate(turns):
                pe.wait_ge(smat, 4 * i + 4)
                for h in range(ML_HEADS):
                    last = nc.tensor.transpose(ps[:, b, h * P:(h + 1) * P], S[:, i, h, j * P:(j + 1) * P], c("ident"))
                last.then_inc(turned, 1)
            pe.wait_ge(t_out, 3)
            for i in range(2):
                for h in range(ML_HEADS):
                    dst = ps[:, i, h * P:(h + 1) * P]
                    for j in range(i + 1):
                        last = nc.tensor.matmul(dst, St[:, i + j, h * P:(h + 1) * P], vm[:, j, h * P:(h + 1) * P],
                                                start=(j == 0), stop=(j == i))
                last.then_inc(n_done, 1)

    y_turned, y_out = pr.sem("mix_out_turned"), pr.sem("mix_out_copied")

    @pr.block.tensor
    def _(pe):
        pe.wait_ge(hm_ready, 2)
        for g, src in enumerate((att, hm)):
            for b in range(4):
                for i in range(2):
                    last = nc.tensor.transpose(ps[:, 2 + 2 * g + b // 2, (b % 2) * N + i * P:(b % 2) * N + (i + 1) * P],
                                               src[:, i, b * P:(b + 1) * P], c("ident"))
            last.then_inc(y_turned, 1)

    @pr.block.scalar
    def _(act):
        for g in range(2):
            act.wait_ge(y_turned, g + 1)
            nc.scalar.activation(y[:, 4 * g:4 * g + 4, :],
                                 ps[:, 2 + 2 * g:4 + 2 * g, :].rearrange("p b (h n) -> p (b h) n", n=N),
                                 ACT.Copy).then_inc(y_out, 1)
    t.close()

    done = pr.sem("mix_normed")
    one = [[0], [1], [2], [3]]
    with ExitStack() as t:
        r1, _, r1_ready = pr.rstd(t, "att_norm", y[:, 0:4, :], [(y_out, 2)], one, N, ATT_D, c("block64"))
        r2, _, r2_ready = pr.rstd(t, "ml_norm", y[:, 4:8, :], r1_ready, one, N, ML_D, c("ones"), bank=2)

        @pr.block.vector
        def _(dve):
            for w in r1_ready + r2_ready:
                dve.wait_ge(*w)
            for b in range(4):
                nc.vector.scalar_tensor_tensor(y[:, b, :], y[:, b, :], c("attn_out")[:, 4 * l + b:4 * l + b + 1],
                                               r1[:, b, :], ALU.mult, ALU.mult)
                last = nc.vector.scalar_tensor_tensor(y[:, 4 + b, :], y[:, 4 + b, :],
                                                      c("mlstm_out")[:, 4 * l + b:4 * l + b + 1],
                                                      r2[:, b, :], ALU.mult, ALU.mult)
            ch.then(dve, last)
            nc.vector.tensor_tensor(y[:, 4:8, :], y[:, 4:8, :], pj[:, OM:OM + 4, :], ALU.mult).then_inc(done, 1)
    inner.close()
    return [(done, 1)]


def build(nc, panels, small, xin, pos, out, until=None):
    with ExitStack() as ctx:
        pr = Program(nc, ctx, panels, small, xin, pos, out)
        const_in, x_in, silu_ready = (pr.sem(n) for n in ("constants_landed", "x_landed", "silu_c_ready"))
        cs = pr.sb("silu_c", [P, 3 * KD])
        vec1 = cs[:, 0:2 * KD].rearrange("p (k v) -> p k v", v=2)
        vec2 = cs[:, 2 * KD:3 * KD].rearrange("p (k v) -> p k v", v=1)
        ada_b = [pr.c("ada_b")[:, l * N_MOD:(l + 1) * N_MOD] for l in range(2)]
        b_mod = [pr.c("b_mod")[:, l * N_MOD:(l + 1) * N_MOD] for l in range(2)]
        norm = lambda name, l: pr.c(name)[:, l * KD:(l + 1) * KD]

        def mixer_out(name, y, ready, mod, nv, n, scope):
            with ExitStack() as t:
                high, low, y_split = whole_split(pr, t, name, y[:, :, 0:n], ready, n)
                got = pr.linear(name, 4, 2, 8, pr.features(high, low, n, KD, tall_offset),
                                pr.add_gated(mod, 16, nv, n), y_split, engines=("dve",))
            scope.close()
            return got

        def mlp(l, mod, nv, n, ready):
            with ExitStack() as t:
                y = pr.sb(f"mlp{l}_y", [P, KD, n], ctx=t)
                high = pr.sb(f"mlp{l}_a_h", [P, KD, n], F32R, ctx=t)
                low = pr.sb(f"mlp{l}_a_l", [P, KD, n], F32R, ctx=t)
                a_ready = pr.norm_modulate(f"norm2_{l}", norm("norm2", l), mod, nv, 24, 32, n, high, low, ready)
                y_ready = pr.feed_forward(f"mlp{l}", D_FF // 256, False, n, high, low, a_ready, y, [])
                return pr.add_feed_forward(f"mlp{l}", y, y_ready, mod, 40, nv, n)

        def store(ready, src):
            stored = pr.sem("out_stored")

            @pr.block.sync
            def _(sp):
                for w in ready:
                    sp.wait_ge(*w)
                sp.dma_start(out, src).then_inc(stored, 16)
                sp.wait_ge(stored, 16)

        def layer0():
            @pr.block.sync
            def _(sp):
                sp.dma_start(pr.cst[:], small).then_inc(const_in, 16)
                sp.dma_start(pr.xT[:], xin).then_inc(x_in, 16)

            pr.stream(24 + 17 + 32)

            @pr.block.scalar
            def _(act):
                act.wait_ge(const_in, 16)
                at = SMALL["cc"][0]
                nc.scalar.activation(cs[:], pr.cst[:, at:at + 3 * KD], ACT.Silu).then_inc(silu_ready, 1)

            mod = pr.mod1[0]
            mod_ready = pr.modulation("mod1_0", vec1, [(silu_ready, 1)], 2, mod, ada_b[0])
            ab = ExitStack()
            pr.y = pr.sb("even_y", [P, KD, TA], ctx=ab)
            pr.pa = pr.sb("even_pa", [P, 6, TA], ctx=ab)
            pr.pb_scope = ExitStack()
            pr.pb = pr.sb("even_pb", [P, 8, TA], ctx=pr.pb_scope)
            pr.gv = pr.sb("even_gv", [P, 4, 512], ctx=pr.pb_scope)
            tmp_a = ExitStack()
            high = pr.sb("a0_h", [P, KD, TA], F32R, ctx=tmp_a)
            low = pr.sb("a0_l", [P, KD, TA], F32R, ctx=tmp_a)
            a_ready = pr.norm_modulate("norm1_0", norm("norm1", 0), mod, 2, 0, 8, TA, high, low,
                                       mod_ready + [(x_in, 16)])
            ready = even_mixer(pr, high, low, a_ready, mod, tmp_a)
            ready = mixer_out("even_out", pr.y, ready, mod, 2, TA, ab)
            if until == "even":
                return store(ready, pr.xT[:, :, :])
            ready = mlp(0, pr.mod1[0], 2, TA, ready)
            if until == "mlp0":
                return store(ready, pr.xT[:, :, :])

        def layer1():
            pr.stream(2 * (24 + 17 + 32))
            mod = pr.mod1[1]
            mod_ready = pr.modulation("mod1_1", vec1, [], 2, mod, ada_b[1])
            scope = ExitStack()
            y, ready = odd_mixer(pr, mod, scope, norm("norm1", 1), mod_ready)
            ready = mixer_out("odd_out", y, ready, mod, 1, TL, scope)
            if until == "odd":
                return store(ready, pr.xT[:, :, 0:TL])
            ready = mlp(1, mod, 1, TL, ready)
            done = pr.sem("final_normed")
            with ExitStack() as t:
                x = pr.xT[:, :, 0:TL]
                r, a, r_ready = pr.rstd(t, "final", x, ready, [list(range(KD))], TL, D, pr.c("ones"))

                @pr.block.vector
                def _(dve):
                    for w in r_ready:
                        dve.wait_ge(*w)
                    pr.dve_chain.then(dve, nc.vector.tensor_tensor(x, x, r[:].broadcast_to([P, KD, TL]), ALU.mult))
                    nc.vector.tensor_tensor(x, x, spread(norm("final", 0), 2, TL), ALU.mult).then_inc(done, 1)
            if until == "mlp1":
                return store([(done, 1)], pr.xT[:, :, 0:TL])

        pr.pos_sb = pr.sb("positions", [P, TL], I32)
        cos, sin = pr.sb("rope_cos", [P, TL]), pr.sb("rope_sin", [P, TL])

        def second(l):
            pr.suffix = f"_{l}"
            pr.stream(2 * (24 + 17 + 32) + (l + 1) * (24 + 20 + 33))
            mod = pr.mod2[l]
            ready = pr.modulation(f"mod2_{l}", vec2, [], 1, mod, b_mod[l])
            if l == 0:
                pos_in = pr.sem("positions_landed")

                @pr.block.scalar
                def _(act):
                    act.dma_start(pr.pos_sb[:], pos).then_inc(pos_in, 16)
                ready += rope_tables(pr, pos_in, cos, sin)
            with ExitStack() as t:
                y = pr.sb("mix_y", [P, KD, TL], ctx=t)
                y_ready = hybrid_mixer(pr, l, mod, y, cos, sin, norm("mix_pre", l), ready)
                high, low, y_split = whole_split(pr, t, "mix_y", y[:], y_ready, TL)
                out_y = pr.sb("mix_out", [P, KD, TL], ctx=t)
                ready = pr.linear("mix_out", 4, 2, 8, pr.features(high, low, TL, KD, tall_offset),
                                  pr.copy_out(lambda q: out_y[:, q, :]), y_split)
                ready = post_add(pr, "mix_post", out_y[:], ready, mod, 16, norm("mix_post", l))
            if until == "b0m":
                return store(ready, pr.xT[:, :, 0:TL])
            with ExitStack() as t:
                y = pr.sb("ffn_y", [P, KD, TL], ctx=t)
                high = pr.sb("ffn_a_h", [P, KD, TL], F32R, ctx=t)
                low = pr.sb("ffn_a_l", [P, KD, TL], F32R, ctx=t)
                a_ready = pr.norm_modulate("ffn_pre", norm("ffn_pre", l), mod, 1, 24, 32, TL, high, low, ready)
                y_ready = pr.feed_forward("ffn", FFN // 256, True, TL, high, low, a_ready, y, [])
                ready = post_add(pr, "ffn_post", y[:], y_ready, mod, 40, norm("ffn_post", l))
            if until == "b0" or l == 1:
                store(ready, pr.xT[:, :, 0:TL])

        layers = [layer0, layer1, lambda: second(0), lambda: second(1)]
        if until in ("b0m", "b0"):
            layers = layers[:3]
        if until in ("even", "mlp0"):
            layers = layers[:1]
        if until in ("odd", "mlp1"):
            layers = layers[:2]
        for layer in layers:
            with nc.cleanup_on_exit():
                with nc.Block() as pr.block:
                    pr.layer_m = pr.m
                    layer()


def kernel(**inputs):
    from concourse import bacc
    from concourse.bass_utils import run_bass_kernel_spmd

    x = {name: np.asarray(value) for name, value in inputs.items()}
    residual = np.concatenate([x["x"][0], x["ctx"][0]]).reshape(TA, KD, P).transpose(2, 1, 0)
    arrays = {
        "panels": layout_panels(x),
        "small": layout_small(x),
        "x_features": np.ascontiguousarray(residual),
        "positions": np.ascontiguousarray(np.broadcast_to(x["positions_2"], (P, TL))),
    }
    nc = bacc.Bacc("TRN2", target_bir_lowering=False, num_devices=1)
    args = [nc.dram_tensor(f"{n}_dram", a.shape, mybir.dt.from_np(a.dtype), kind="ExternalInput").ap()
            for n, a in arrays.items()]
    out = nc.dram_tensor("out_dram", (P, KD, TL), F32, kind="ExternalOutput").ap()
    build(nc, *args, out)
    got = run_bass_kernel_spmd(nc, [{f"{n}_dram": a for n, a in arrays.items()}], core_ids=[0])
    return got.results[0]["out_dram"].transpose(2, 1, 0).reshape(1, TL, D)
```

```python
import math
from contextlib import ExitStack

import numpy as np

import concourse.bass as bass
from concourse import mybir

F32 = mybir.dt.float32
F32R = mybir.dt.float32r
I32 = mybir.dt.int32
U32 = mybir.dt.uint32
ALU = mybir.AluOpType
ACT = mybir.ActivationFunctionType
AX = mybir.AxisListType
ds = bass.ds

P = 128
D = 1024
KD = D // P
TL = 256
TC = 256
TA = TL + TC
EPS = 1e-6
PANEL = 2048
PC = PANEL // KD
RAW = 3
NEG = -1e30
TAKEN = -3e38

MLA_HEADS, NOPE, ROPE, MV = 8, 64, 32, 64
QK = NOPE + ROPE
GLA_HEADS, GLA_DK, GLA_DV, CH = 4, 64, 128, 64
GDN_HEADS, GDN_DK, GDN_DV = 8, 64, 128
ATT_HEADS, ATT_D = 8, 64
ML_HEADS, ML_D = 4, 128
TOPK = 64
FFN = 2816
D_FF = 4096
N_MOD = 48
FIRST = 16
GROUP = 4
ROWS = 2
GDN_ORDER = [0, 2, 4, 6, 1, 3, 5, 7]
LEVELS = 7


def small_layout():
    common = [
        ("eps", 1), ("ident", P), ("ones", P), ("block64", P), ("tri_f", P), ("tri_b", P),
        ("ada_b", 2 * N_MOD), ("b_mod", 2 * N_MOD), ("norm1", 2 * KD), ("norm2", 2 * KD),
        ("q_norm", 3), ("kv_norm", 2), ("gla_o", 1), ("gdn_conv", 3 * 16), ("gdn_o", 1),
        ("final", KD), ("mix_pre", 2 * KD), ("mix_post", 2 * KD), ("q_lat", 4),
        ("conv_w", 2 * 4 * 8), ("conv_b", 2 * 8), ("attn_out", 8), ("mlstm_out", 8),
        ("ffn_pre", 2 * KD), ("ffn_post", 2 * KD),
        ("a_log", 16), ("dt_bias", 16), ("b_ig", 8), ("b_fg", 8),
    ]
    early = [
        ("gla_f", P), ("gla_b", P), ("kpe_swap", P), ("chunk_start", TA),
        ("mla_q", TL), ("mla_qc", 1), ("kr_cos", TL), ("kr_sin", TL), ("gate_up", 4 * P), ("gate_bias", 4),
    ]
    late = [("rot", P), ("lev_f", LEVELS * P), ("lev_b", LEVELS * P), ("causal", 2 * TL), ("invf", 1)]
    out, dram, shared = {}, 0, sum(w for _, w in common)
    for group, chip in ((common, 0), (early, shared), (late, shared)):
        for name, width in group:
            out[name] = (dram, chip, width)
            dram, chip = dram + width, chip + width
    first = shared + sum(w for _, w in early)
    return out, dram, shared, first, max(at + width for _, at, width in out.values())


SMALL, SMALL_W, SMALL_SHARED, SMALL_FIRST, SMALL_CHIP = small_layout()


def panel_plan():
    first = [PANEL] * 9 + [1536] * 2 + [PANEL, 1024] + [PANEL] * 4
    delta = [PANEL] * 4 + [256] + [PANEL] * 12
    hybrid = [PANEL] * 14 + [256] + [PANEL] * 5
    mlp = [PANEL] * (2 * D_FF // PC)
    ffn = [PANEL] * (3 * FFN // PC)
    return [first + mlp, delta + mlp, hybrid + ffn, hybrid + ffn]


PLANS = panel_plan()
PLAN = sum(PLANS, [])


def shape_constants():
    c = {}
    j = np.arange(P)[:, None]
    i = np.arange(P)[None, :]
    c["eps"] = np.full((P, 1), EPS)
    c["ident"] = (j == i)
    c["ones"] = np.ones((P, P))
    c["block64"] = (j // 64 == i // 64)
    c["tri_f"] = (j <= i)
    c["tri_b"] = (j >= i)
    c["gla_f"] = (j <= i) & (j // CH == i // CH)
    c["gla_b"] = (j >= i) & (j // CH == i // CH)
    c["chunk_start"] = np.broadcast_to((np.arange(TA) % CH != 0)[None, :], (P, TA))
    swap = np.zeros((P, P))
    for half in (64, 96):
        for r in range(ROPE):
            axis, part, n = r // 16, (r // 8) % 2, r % 8
            swap[64 + axis * 16 + (1 - part) * 8 + n, half + r] = 1.0
    c["kpe_swap"] = swap
    rot = np.zeros((P, P))
    for h in (0, 64):
        for r in range(32):
            rot[h + 32 + r, h + r] = -1.0
            rot[h + r, h + 32 + r] = 1.0
    c["rot"] = rot
    f32 = np.float32
    row = np.repeat(np.arange(TL // 64), 64).astype(f32)
    col = np.tile(np.arange(64), TL // 64).astype(f32)
    inv = (10000.0 ** (-np.arange(0, 16, 2) / 16.0)).astype(f32)
    ang = np.stack([row[None, :] * inv[:, None], col[None, :] * inv[:, None]])
    cos = np.zeros((ROPE, TL))
    sin = np.zeros((ROPE, TL))
    for r in range(ROPE):
        axis, part, n = r // 16, (r // 8) % 2, r % 8
        cos[r] = np.cos(ang[axis, n].astype(f32))
        sin[r] = np.sin(ang[axis, n].astype(f32)) * (-1.0 if part == 0 else 1.0)
    c["mla_q"] = np.concatenate([np.ones((64, TL)), cos, sin])
    c["mla_qc"] = (np.arange(P) < 96).astype(f32)[:, None]
    c["kr_cos"] = np.concatenate([np.zeros((64, TL)), cos, cos])
    c["kr_sin"] = np.concatenate([np.zeros((64, TL)), sin, sin])
    lev = []
    for n in range(LEVELS):
        s = 1 << n
        lev.append((j // (2 * s) == i // (2 * s)) & (j // s % 2 == 0) & (i // s % 2 == 1))
    c["lev_f"] = np.concatenate(lev, axis=1)
    c["lev_b"] = np.concatenate([m.T for m in lev], axis=1)
    s = np.arange(TL)[None, :]
    c["causal"] = np.concatenate([np.where(s <= j + t * P, 0.0, NEG) for t in range(2)], axis=1)
    c["invf"] = np.tile((10000.0 ** (-np.arange(0, 64, 2) / 64.0)).astype(f32), 4)[:, None]
    return {n: np.asarray(v, f32) for n, v in c.items()}


def columns(v):
    v = np.asarray(v)
    return v.reshape(-1, P).T


def layout_small(x):
    out = np.zeros((P, SMALL_W), np.float32)

    def put(name, value):
        at, _, width = SMALL[name]
        assert value.shape[1] == width, (name, value.shape, width)
        out[:value.shape[0], at:at + width] = value

    for name, value in shape_constants().items():
        put(name, value)
    gate = np.zeros((64, 2, 256), np.float32)
    gate[32:48, 0] = x["gla_gate_up"][0, 0]
    gate[48:64, 1] = x["gla_gate_up"][0, 1]
    put("gate_up", gate.reshape(64, 512))
    put("gate_bias", columns(x["gla_gate_bias"][0]))
    for name, key in (("ada_b", "ada_b"), ("b_mod", "b_mod_2"), ("norm1", "norm1_w"), ("norm2", "norm2_w"),
                      ("q_norm", "mla_q_norm"), ("kv_norm", "mla_kv_norm"), ("gla_o", "gla_o_norm"),
                      ("gdn_conv", "gdn_conv_w"), ("gdn_o", "gdn_o_norm"), ("final", "final_norm"),
                      ("mix_pre", "mix_norm_pre_2"), ("mix_post", "mix_norm_post_2"), ("q_lat", "q_latent_norm_2"),
                      ("conv_w", "conv_w_2"), ("conv_b", "conv_b_2"), ("attn_out", "attn_out_norm_2"),
                      ("mlstm_out", "mlstm_out_norm_2"), ("ffn_pre", "ffn_norm_pre_2"),
                      ("ffn_post", "ffn_norm_post_2")):
        put(name, columns(x[key]))
    for name, row in (("a_log", x["gdn_a_log"][0][:, GDN_ORDER]), ("dt_bias", x["gdn_dt_bias"][0][:, GDN_ORDER]),
                      ("b_ig", x["b_igate_2"]), ("b_fg", x["b_fgate_2"])):
        put(name, np.broadcast_to(row.reshape(1, -1), (P, SMALL[name][2])))
    return out


def tall(w):
    n = w.shape[1] // PC
    return list(w.reshape(KD, P, n, PC).transpose(2, 1, 0, 3).reshape(n, P, PANEL))


def blocks_of(w, cols):
    k = w.shape[0] // P
    return w.reshape(k, P, cols // P, P).transpose(1, 2, 0, 3).reshape(P, -1)


def padded(a, width=PANEL):
    out = np.zeros((P, width), np.float32)
    out[:, :a.shape[1]] = a
    return out


def down_panels(w):
    n = w.shape[0] // PC
    return list(w.reshape(n, 2, P, D).transpose(0, 2, 1, 3).reshape(n, P, PANEL))


def layout_panels(x):
    out = []
    w = x["even_w_in"][0]
    cq, ckv, kpe = w[:, :384], w[:, 384:640], w[:, 640:672]
    gq, gk, gv, gg, glow = w[:, 672:928], w[:, 928:1184], w[:, 1184:1696], w[:, 1696:2208], w[:, 2208:2240]
    feat = np.concatenate([cq, ckv, np.zeros((D, 32), np.float32), glow, kpe, kpe, gq, gk, gg], axis=1)
    out += tall(feat) + tall(gv)
    uq = x["mla_w_uq"][0].reshape(384, MLA_HEADS, QK)
    order = [NOPE + (r // 16) * 16 + (1 - (r // 8) % 2) * 8 + r % 8 for r in range(ROPE)]
    uq = np.concatenate([uq, uq[:, :, order]], axis=2).reshape(384, MLA_HEADS * P)
    out += [padded(blocks_of(uq[:, :512], 512)), padded(blocks_of(uq[:, 512:], 512))]
    ukv = x["mla_w_ukv"][0].reshape(256, MLA_HEADS, NOPE + MV)
    kk = np.concatenate([ukv[:, :, :NOPE], np.zeros((256, MLA_HEADS, 64), np.float32)], axis=2)
    vv = ukv[:, :, NOPE:].reshape(2, P, 512).transpose(1, 0, 2).reshape(P, 1024)
    out += [blocks_of(kk.reshape(256, 1024), 1024), padded(vv)]
    out += tall(x["even_w_out"][0])

    def mlp(w1, w2):
        ups, downs = tall(w1), down_panels(w2)
        order = [ups[0]]
        for n in range(len(downs)):
            order += ups[n + 1:n + 2] + [downs[n]]
        return order

    out += mlp(x["mlp_w1"][0], x["mlp_w2"][0])
    w = x["gdn_w_in"][0]
    ab = w[:, 3072:].reshape(D, 4, GDN_HEADS)[:, :, GDN_ORDER].reshape(KD, P, 32)
    out += tall(w[:, 2048:3072]) + [padded(ab.transpose(1, 0, 2).reshape(P, 256))]
    out += tall(w[:, 1024:2048]) + tall(w[:, :1024])
    out += tall(x["gdn_w_out"][0]) + mlp(x["mlp_w1"][1], x["mlp_w2"][1])
    for l in range(2):
        w = x["w_in_2"][l]
        cut = np.cumsum([0, 256, 512, 512, 64, 8, 512, 512, 512, 512, 4, 4])
        cq, ka, va, ki, wi, qm, km, vm, om, im, fm = (w[:, a:b] for a, b in zip(cut[:-1], cut[1:]))
        out += tall(np.concatenate([cq, ka, qm, km, om, ki, ki, np.zeros((D, P), np.float32)], axis=1))
        out += tall(va) + tall(vm)
        small = np.concatenate([wi, im, fm, np.zeros((D, 16), np.float32)], axis=1)
        out += [padded(small.reshape(KD, P, 32).transpose(1, 0, 2).reshape(P, 256))]
        out += [np.concatenate([blocks_of(x["w_q_up_2"][l], 512), blocks_of(x["w_qidx_up_2"][l], 512)], axis=1)]
        out += tall(x["w_out_2"][l])
        gate = tall(x["w_gate_up_2"][l][:, :FFN])
        up = tall(x["w_gate_up_2"][l][:, FFN:])
        downs = down_panels(x["w_down_2"][l])
        out += [gate[0], up[0]]
        for n in range(len(downs)):
            out += gate[n + 1:n + 2] + up[n + 1:n + 2] + [downs[n]]
    assert len(out) == len(PLAN), (len(out), len(PLAN))
    return np.stack(out)


def layout_rows(x):
    return np.concatenate([w.T.reshape(N_MOD, P, D) for w in (*x["ada_w"], *x["w_mod_2"])])


def layout_conditions(x):
    c = np.stack([x["c"][0], x["c_ctx"].reshape(D), x["c_2"][0]])
    return np.ascontiguousarray(np.broadcast_to(c, (P, 3, D)))


PER_LOOP = 6


class Chain:

    def __init__(self, sem):
        self.sem, self.n = sem, 0

    def then(self, eng, ins):
        self.n += 1
        ins.then_inc(self.sem, 1)
        eng.wait_ge(self.sem, self.n)


class Program:

    def __init__(self, nc, ctx, panels, rows, conditions, small, xin, pos, out):
        self.nc, self.ctx = nc, ctx
        self.suffix = ""
        self.panels, self.rows, self.conditions = panels, rows, conditions
        self.small, self.xin, self.pos, self.out = small, xin, pos, out
        self.raw = self.sb("raw", [P, RAW, PANEL])
        self.wh = self.sb("w_high", [P, 2, PANEL], F32R)
        self.wl = self.sb("w_low", [P, 2, PANEL], F32R)
        self.cst = self.sb("constants", [P, SMALL_CHIP])
        self.xT = self.sb("x_features", [P, KD, TA])
        self.mod1 = [self.sb(f"mod1_{l}", [P, N_MOD, 2]) for l in range(2)]
        self.mod2 = [self.sb(f"mod2_{l}", [P, N_MOD, 1]) for l in range(2)]
        self.ps = ctx.enter_context(nc.psum_tensor("banks", [P, 8, 512], F32))
        self.landed = [self.sem(f"panel_landed_{s}") for s in range(RAW)]
        self.w_high = self.sem("weights_high_ready")
        self.w_split = self.sem("weights_split")
        self.dve_chain = Chain(self.sem("vector_step"))
        self.act_chain = Chain(self.sem("scalar_step"))
        self.pool_chain = Chain(self.sem("gpsimd_step"))
        self.slots = self.sb("mod_rows", [P, ROWS, D])
        self.cond = [self.sb(f"silu_condition_{v}", [P, D]) for v in range(2)]
        self.dots = self.sb("mod_dots", [P, ROWS, 2])
        self.touched = self.sb("mod_step_mark", [P, 1])
        self.ends = [None] * len(PLAN)
        self.m = 0
        self.split_next = {"act": 0, "dve": 0}
        self.block = None
        self.operand_wait = None
        self.layer_m = 0
        self.streamed = 0

    def sb(self, name, shape, dt=F32, ctx=None):
        return (ctx or self.ctx).enter_context(self.nc.sbuf_tensor(name + self.suffix, shape, dt))

    def sem(self, name):
        return self.nc.alloc_semaphore(name=name + self.suffix)

    def c(self, name):
        _, at, width = SMALL[name]
        return self.cst[:, at:at + width]

    def take(self, count, sem, per_panel, first=0):
        ms = list(range(self.m, self.m + count))
        self.m += count
        for j, m in enumerate(ms):
            self.ends[m] = (sem, first + per_panel * (j + 1))
        return ms

    def landed_count(self, m):
        return 16 * (m // RAW + 1)

    def in_loop(self, value, m, q):
        if q is None:
            return value(m)
        return q * (value(m + PER_LOOP) - value(m)) + value(m)

    def split_act(self, act, m, q=None):
        slot, width = m % RAW, PLAN[m]
        act.wait_ge(self.landed[slot], self.in_loop(self.landed_count, m, q))
        if m - 2 >= self.layer_m:
            sem = self.ends[m - 2][0]
            act.wait_ge(sem, self.in_loop(lambda x: self.ends[x][1], m - 2, q))
        self.nc.scalar.activation(self.wh[:, m % 2, 0:width], self.raw[:, slot, 0:width],
                                  ACT.Copy).then_inc(self.w_high, 1)

    def split_dve(self, dve, m, q=None):
        slot, width = m % RAW, PLAN[m]
        dve.wait_ge(self.w_high, self.in_loop(lambda x: x + 1, m, q))
        self.nc.vector.tensor_tensor(self.wl[:, m % 2, 0:width], self.raw[:, slot, 0:width],
                                     self.wh[:, m % 2, 0:width].bitcast(F32),
                                     ALU.subtract).then_inc(self.w_split, 1)

    def split_upto(self, which, eng, m):
        while self.split_next[which] <= m:
            (self.split_act if which == "act" else self.split_dve)(eng, self.split_next[which])
            self.split_next[which] += 1

    def presplit(self, count=2):
        @self.block.scalar
        def _(act):
            self.split_upto("act", act, self.m + count - 1)

        @self.block.vector
        def _(dve):
            self.split_upto("dve", dve, self.m + count - 1)

    def wait_split(self, pe, m, q=None):
        pe.wait_ge(self.w_split, self.in_loop(lambda x: x + 1, m, q))

    def product3(self, out, sh, sl, mh, ml, nk):
        for k in range(nk):
            if self.operand_wait is not None:
                self.operand_wait(k)
            self.nc.tensor.matmul(out, sh(k), ml(k), start=(k == 0), stop=False)
            self.nc.tensor.matmul(out, sh(k), mh(k), start=False, stop=False)
            last = self.nc.tensor.matmul(out, sl(k), mh(k), start=False, stop=(k == nk - 1))
        return last

    def stream(self, end):
        total = min(end + RAW, len(PLAN))

        @self.block.sync
        def _(sp):
            n = self.streamed
            while n < RAW:
                sp.dma_start(self.raw[:, n, :], self.panels[n, :, :]).then_inc(self.landed[n], 16)
                n += 1
            turns = (total - n) // RAW
            with sp.Fori(0, turns) as q:
                for s in range(n, n + RAW):
                    sp.wait_ge(self.w_split, q * RAW + (s - RAW + 1))
                    sp.dma_start(self.raw[:, s % RAW, :],
                                 self.panels[ds(q * RAW + s, 1), :, :].rearrange("a p n -> p (a n)")
                                 ).then_inc(self.landed[s % RAW], 16)
            for n in range(n + turns * RAW, total):
                sp.wait_ge(self.w_split, n - RAW + 1)
                sp.dma_start(self.raw[:, n % RAW, :], self.panels[n, :, :]).then_inc(self.landed[n % RAW], 16)
        self.streamed = total

    def silu(self, name, source, cond):
        landed, ready = self.sem(f"{name}_landed"), self.sem(f"{name}_ready")

        @self.block.scalar
        def _(act):
            for v, row in enumerate(cond):
                act.dma_start(row[:], source[:, v, :]).then_inc(landed, 16)
            act.wait_ge(landed, 16 * len(cond))
            for row in cond:
                last = self.nc.scalar.activation(row[:], row[:], ACT.Silu)
            last.then_inc(ready, 1)
        return [(ready, 1)]

    def first_modulation(self, name, ready, mod, bias, scope):
        nc, groups = self.nc, FIRST // GROUP
        buf = self.sb(f"{name}_rows", [P, FIRST, D], ctx=scope)
        junk = self.sb(f"{name}_junk", [P, 2, D], ctx=scope)
        landed = [self.sem(f"{name}_rows_landed_{g}") for g in range(groups)]
        done, out = self.sem(f"{name}_dots"), self.sem(f"{name}_ready")

        def load(sp, g):
            sp.dma_start(buf[:, g * GROUP:(g + 1) * GROUP, :],
                         self.rows[g * GROUP:(g + 1) * GROUP, :, :].rearrange("j p i -> p j i")
                         ).then_inc(landed[g], 16)

        @self.block.vector
        def _(dve):
            for w in ready:
                dve.wait_ge(*w)
            for i in range(FIRST):
                if i % GROUP == 0:
                    dve.wait_ge(landed[i // GROUP], 16)
                for v in range(2):
                    if i:
                        dve.wait_ge(done, 2 * i + v - 1)
                    nc.vector.scalar_tensor_tensor(
                        junk[:, v, :], buf[:, i, :], 1.0, self.cond[v][:], ALU.mult, ALU.mult,
                        accum_out=mod[:, i, v:v + 1]).then_inc(done, 1)
            dve.wait_ge(done, 2 * FIRST)
            part = mod[:, 0:FIRST, :]
            nc.vector.tensor_tensor(part, part, spread(bias[:, 0:FIRST], 2, 2), ALU.add).then_inc(out, 1)

        return load, [(out, 1)]

    def beside_modulation(self, name, layer, first, count, per_panel, ready, mod, bias):
        nc = self.nc
        landed = [self.sem(f"{name}_rows_landed_{s}") for s in range(ROWS)]
        done, out = self.sem(f"{name}_dots"), self.sem(f"{name}_ready")

        @self.block.gpsimd
        def _(pool):
            for i in range(count):
                if i >= ROWS:
                    pool.wait_ge(done, 2 * (i - ROWS) + 2)
                pool.dma_start(self.slots[:, i % ROWS, :], self.rows[layer * N_MOD + first + i, :, :]
                               ).then_inc(landed[i % ROWS], 16)

        def step(which, eng, p):
            if which != "dve":
                return
            if p == 0:
                for w in ready:
                    eng.wait_ge(*w)
            for i in range(p * per_panel, min((p + 1) * per_panel, count)):
                eng.wait_ge(landed[i % ROWS], 16 * (i // ROWS + 1))
                for v in range(2):
                    if i or v:
                        eng.wait_ge(done, 2 * i + v)
                    nc.vector.scalar_tensor_tensor(
                        self.slots[:, i % ROWS, :] if v else self.scratch[:], self.slots[:, i % ROWS, :], 1.0,
                        self.cond[v][:], ALU.mult, ALU.mult,
                        accum_out=mod[:, first + i, v:v + 1]).then_inc(done, 1)
                if i == count - 1:
                    eng.wait_ge(done, 2 * count)
                    part = mod[:, first:first + count, :]
                    nc.vector.tensor_tensor(part, part, spread(bias[:, first:first + count], 2, 2),
                                            ALU.add).then_inc(out, 1)
        return step, [(out, 1)]

    def modulation(self, name, layer, first, count, ready, nv, mod, bias):
        nc, n0, width = self.nc, layer * N_MOD + first, mod.shape[2]
        landed = [self.sem(f"{name}_rows_landed_{s}") for s in range(ROWS)]
        done, out = self.sem(f"{name}_steps"), self.sem(f"{name}_ready")
        halvings = D.bit_length() - 1
        sums = nv * (halvings + 1)
        steps = sums + 2

        @self.block.gpsimd
        def _(pool):
            def load(s, source):
                pool.dma_start(self.slots[:, s, :], source).then_inc(landed[s], 16)

            def mark():
                nc.gpsimd.tensor_tensor(self.touched[:], self.cond[0][:, 0:1], self.cond[0][:, 0:1],
                                        ALU.mult).then_inc(done, 1)

            def block(q, s, target, again):
                wait = lambda n: pool.wait_ge(done, q * (ROWS * steps) + (s * steps + n + 1))
                rows = self.slots[:, s, :]
                work = [rows if v == nv - 1 else self.scratch[:] for v in range(nv)]
                pool.wait_ge(landed[s], q * 16 + 16)
                for v in range(nv):
                    wait(v)
                    nc.gpsimd.tensor_tensor(work[v], rows, self.cond[v][:], ALU.mult).then_inc(done, 1)
                for n in range(1, halvings + 1):
                    half = D >> n
                    for v in range(nv):
                        wait((n - 1) * nv + v + 1)
                        dst = work[v][:, 0:half] if half > 1 else self.dots[:, s, v:v + 1]
                        nc.gpsimd.tensor_tensor(dst, work[v][:, 0:half], work[v][:, half:2 * half],
                                                ALU.add).then_inc(done, 1)
                wait(sums)
                mark()
                if again:
                    load(s, self.rows[ds(q * ROWS + (n0 + ROWS + s), 1), :, :].rearrange("a p i -> p (a i)"))
                nc.gpsimd.tensor_copy(target, self.dots[:, s, 0:nv]).then_inc(done, 1)

            for w in ready:
                pool.wait_ge(*w)
            for s in range(ROWS):
                load(s, self.rows[n0 + s, :, :])
            mark()
            flat = mod.rearrange("p j v -> p (j v)")
            turns = count // ROWS - 1
            with pool.Fori(0, turns) as q:
                for s in range(ROWS):
                    block(q, s, flat[:, ds(q * (ROWS * width) + (first + s) * width, nv)], True)
            for s in range(ROWS):
                block(turns, s, mod[:, first + turns * ROWS + s, 0:nv], False)
            pool.wait_ge(done, count * steps + 1)
            part = mod[:, first:first + count, 0:nv]
            nc.gpsimd.tensor_tensor(part, part, spread(bias[:, first:first + count], 2, nv),
                                    ALU.add).then_inc(out, 1)
        return [(out, 1)]

    def rstd(self, tmp, name, src, src_ready, groups, n, dim, matrix, bank=0, squares=None,
             meanwhile=None):
        nc, g = self.nc, len(groups)
        nb = src.shape[1]
        per_bank = 512 // n
        if squares is None:
            squares = self.sb(f"{name}_squares", [P, nb, n], ctx=tmp)
        r = self.sb(f"{name}_rstd", [P, g, n], ctx=tmp)
        root = self.sb(f"{name}_root", [P, g, n], ctx=tmp)
        sq_ready, summed, root_ready, ready = (
            self.sem(f"{name}_{s}") for s in ("squares_ready", "summed", "root_ready", "rstd_ready"))
        nbanks = (g + per_bank - 1) // per_bank
        sums = self.ps[:, bank:bank + nbanks, :].rearrange("p b n -> p (b n)")[:, 0:g * n]\
            .rearrange("p (g n) -> p g n", n=n)

        @self.block.scalar
        def _(act):
            for b in range(nb):
                if callable(src_ready):
                    for w in src_ready(b):
                        act.wait_ge(*w)
                elif b == 0:
                    for w in src_ready:
                        act.wait_ge(*w)
                nc.scalar.activation(squares[:, b, :], src[:, b, :], ACT.Square).then_inc(sq_ready, 1)
            act.wait_ge(summed, 1)
            first = ACT.Sqrt if g == 1 else ACT.Ln
            nc.scalar.activation(root[:], sums, first, bias=self.c("eps"), scale=1.0 / dim).then_inc(root_ready, 1)
            if g > 1:
                act.wait_ge(root_ready, 1)
                nc.scalar.activation(r[:], root[:], ACT.Exp, scale=-0.5).then_inc(ready, 1)

        @self.block.tensor
        def _(pe):
            for i, blocks in enumerate(groups):
                for b in blocks:
                    pe.wait_ge(sq_ready, b + 1)
                    last = nc.tensor.matmul(sums[:, i, :], matrix, squares[:, b, :],
                                            start=(b == blocks[0]), stop=(b == blocks[-1]))
            last.then_inc(summed, 1)

        @self.block.vector
        def _(dve):
            if meanwhile is not None:
                meanwhile(dve, sq_ready)
            if g == 1:
                dve.wait_ge(root_ready, 1)
                nc.vector.reciprocal(r[:], root[:]).then_inc(ready, 1)
        return r, squares, [(ready, 1)]

    def split_blocks(self, name, a, a_ready, high, low, counts=None):
        nc = self.nc
        nb = a.shape[1]
        h_ready, ready = self.sem(f"{name}_high_ready"), self.sem(f"{name}_split_ready")

        @self.block.scalar
        def _(act):
            for k in range(nb):
                act.wait_ge(a_ready, k + 1 if counts is None else counts[k])
                nc.scalar.activation(high[:, k, :], a[:, k, :], ACT.Copy).then_inc(h_ready, 1)

        @self.block.vector
        def _(dve):
            for k in range(nb):
                dve.wait_ge(h_ready, k + 1)
                nc.vector.tensor_tensor(low[:, k, :], a[:, k, :], high[:, k, :].bitcast(F32),
                                        ALU.subtract).then_inc(ready, 1)
        return [(ready, nb)]

    def norm_modulate(self, name, weight, mod, nv, shift, scale, n, high, low, ready, bank=0, work=None,
                      scaled_x=None):
        nc = self.nc
        self.presplit()
        with ExitStack() as tmp:
            x = self.xT[:, :, 0:n]
            gain = self.sb(f"{name}_gain", [P, KD, nv], ctx=tmp)
            scaled, normed, high_ready, split = (self.sem(f"{name}_{s}") for s in (
                "scaled", "normed", "high_ready", "split_ready"))
            half = n // nv
            part = lambda buf, k, v: buf[:, k, v * half:(v + 1) * half]
            t = (scaled_x if scaled_x is not None else self.sb(f"{name}_scaled_x", [P, KD, n], ctx=tmp))

            def scale_x(dve, _):
                for w in ready(0) if callable(ready) else ready:
                    dve.wait_ge(*w)
                self.dve_chain.then(dve, nc.vector.scalar_tensor_tensor(
                    gain[:], mod[:, scale:scale + KD, 0:nv], 1.0, spread(weight, 2, nv), ALU.add, ALU.mult))
                for k in range(KD):
                    if callable(ready):
                        for w in ready(k):
                            dve.wait_ge(*w)
                    for v in range(nv):
                        last = nc.vector.tensor_scalar(part(t, k, v), part(x, k, v), gain[:, k, v:v + 1],
                                                       None, ALU.mult)
                    last.then_inc(scaled, 1)

            r, _, r_ready = self.rstd(tmp, name, x, ready, [list(range(KD))], n, D, self.c("ones"), bank, work,
                                      meanwhile=scale_x)

            @self.block.vector
            def _(dve):
                for w in r_ready:
                    dve.wait_ge(*w)
                for step in range(KD + 1):
                    k = step
                    if k < KD:
                        dve.wait_ge(scaled, k + 1)
                        nc.vector.tensor_tensor(t[:, k, :], t[:, k, :], r[:, 0, :],
                                                ALU.mult).then_inc(normed, 1)
                    k = step - 1
                    if k >= 0:
                        dve.wait_ge(high_ready, k + 1)
                        for v in range(nv):
                            last = nc.vector.scalar_tensor_tensor(
                                part(low, k, v), part(t, k, v), mod[:, shift + k, v:v + 1],
                                part(high, k, v).bitcast(F32), ALU.add, ALU.subtract)
                        last.then_inc(split, 1)

            @self.block.scalar
            def _(act):
                for k in range(KD):
                    act.wait_ge(normed, k + 1)
                    for v in range(nv):
                        last = nc.scalar.activation(part(high, k, v), part(t, k, v), ACT.Identity,
                                                    bias=mod[:, shift + k, v:v + 1])
                    last.then_inc(high_ready, 1)
        return [(split, KD)]

    def linear(self, name, panels, per_panel, nblocks, product, evac, x_ready, engines=("dve", "act"),
               banks=(0, 1, 2, 3), after=(), beside=None, rising=False):
        nc, nb = self.nc, len(banks)
        done = self.sem(f"{name}_products")
        out = {e: self.sem(f"{name}_out_{e}") for e in sorted(set(engines))}
        ms = self.take(panels, done, per_panel)
        self.ends[ms[-1]] = (done, nblocks)
        who = [engines[q % len(engines)] for q in range(nblocks)]
        rank = [sum(w == who[q] for w in who[:q + 1]) for q in range(nblocks)]

        @self.block.tensor
        def _(pe):
            for w in x_ready if not rising else []:
                pe.wait_ge(*w)
            for q in range(nblocks):
                m = ms[q // per_panel]
                if q % per_panel == 0:
                    self.wait_split(pe, m)
                if q >= nb:
                    pe.wait_ge(out[who[q - nb]], rank[q - nb])
                if rising and q == 0:
                    self.operand_wait = lambda k: pe.wait_ge(x_ready[0][0], k + 1)
                product(q, m, self.ps[:, banks[q % nb], :]).then_inc(done, 1)
                self.operand_wait = None

        def take_out(which, eng):
            for w in after:
                eng.wait_ge(*w)
            for p, m in enumerate(ms):
                self.split_upto(which, eng, min(m + 1, ms[-1]))
                if beside is not None:
                    beside(which, eng, p)
                for q in range(p * per_panel, min((p + 1) * per_panel, nblocks)):
                    if who[q] == which:
                        eng.wait_ge(done, q + 1)
                        evac(q, which, eng, self.ps[:, banks[q % nb], :]).then_inc(out[which], 1)

        @self.block.scalar
        def _(act):
            take_out("act", act)

        @self.block.vector
        def _(dve):
            take_out("dve", dve)
        return [(out[e], sum(w == e for w in who)) for e in out]

    def features(self, high, low, n, nk, offset):
        def product(q, m, bank):
            return self.product3(bank[:, 0:n],
                                 lambda k: self.wh[:, m % 2, offset(q, k):offset(q, k) + P],
                                 lambda k: self.wl[:, m % 2, offset(q, k):offset(q, k) + P],
                                 lambda k: high[:, k, 0:n], lambda k: low[:, k, 0:n], nk)
        return product

    def tokens(self, high, low, tiles, width, nk):
        def product(q, m, bank):
            t = q % tiles
            return self.product3(bank[:, 0:width],
                                 lambda k: high[:, k, t * P:(t + 1) * P], lambda k: low[:, k, t * P:(t + 1) * P],
                                 lambda k: self.wh[:, m % 2, k * width:(k + 1) * width],
                                 lambda k: self.wl[:, m % 2, k * width:(k + 1) * width], nk)
        return product

    def copy_out(self, target):
        def evac(q, which, eng, bank):
            dst = target(q)
            src = bank[:, 0:dst.shape[-1]]
            if which == "act":
                return self.nc.scalar.activation(dst, src, ACT.Copy)
            return self.nc.vector.tensor_copy(dst, src)
        return evac

    def add_gated(self, mod, gate, nv, n):
        half = n // nv

        def evac(q, which, eng, bank):
            for v in range(nv):
                x = self.xT[:, q, v * half:(v + 1) * half]
                last = self.nc.vector.scalar_tensor_tensor(
                    x, bank[:, v * half:(v + 1) * half], mod[:, gate + q, v:v + 1], x, ALU.mult, ALU.add)
            return last
        return evac

    def feed_forward(self, name, chunks, gated, n, high, low, a_ready, y, y_free):
        nc = self.nc
        ups = 2 if gated else 1
        per = PER_LOOP // (ups + 1)
        up_done, down_done, r_ready, h_ready, hh_ready, hid_ready, y_ready = (
            self.sem(f"{name}_{s}") for s in ("up_products", "down_products", "activated", "hidden_ready",
                                              "hidden_high", "hidden_split", "added"))
        first = self.m
        kinds = [("up", 0, u) for u in range(ups)]
        for c in range(chunks):
            if c + 1 < chunks:
                kinds += [("up", c + 1, u) for u in range(ups)]
            kinds += [("down", c, 0)]
        m_of = {}
        for kind, c, u in kinds:
            if kind == "up":
                m_of[kind, c, u] = self.take(1, up_done, 1, c * ups + u)[0]
            else:
                m_of[kind, c, u] = self.take(1, down_done, 4, 4 * c)[0]
        last_m = self.m - 1
        tmp = ExitStack()
        act_buf = self.sb(f"{name}_activated", [P, 2, n], ctx=tmp)
        hid = self.sb(f"{name}_hidden", [P, 2, n], ctx=tmp)
        hh = self.sb(f"{name}_hidden_h", [P, per, 2, n], F32R, ctx=tmp)
        hl = self.sb(f"{name}_hidden_l", [P, per, 2, n], F32R, ctx=tmp)
        ps = self.ps

        def pe_up(pe, cs, q=None):
            c = cs if q is None else q * per + cs
            for u in range(ups):
                self.wait_split(pe, m_of["up", cs, u], q)
                m = m_of["up", cs, u]
                if u == 0 and cs >= 1:
                    pe.wait_ge(h_ready, c)
                for b in range(2):
                    if cs == 0 and u == 0 and b == 0:
                        self.operand_wait = lambda k: pe.wait_ge(a_ready[0][0], k + 1)
                    last = self.product3(ps[:, 2 * u + b, 0:n],
                                         lambda k: self.wh[:, m % 2, k * PC + b * P:k * PC + (b + 1) * P],
                                         lambda k: self.wl[:, m % 2, k * PC + b * P:k * PC + (b + 1) * P],
                                         lambda k: high[:, k, 0:n], lambda k: low[:, k, 0:n], KD)
                    self.operand_wait = None
                last.then_inc(up_done, 1)

        def pe_down(pe, cs, q=None):
            c = cs if q is None else q * per + cs
            m = m_of["down", cs, 0]
            self.wait_split(pe, m, q)
            pe.wait_ge(hid_ready, c + 1)
            for g in range(4):
                if cs > 0 or g >= 2:
                    pe.wait_ge(y_ready, c * 4 + (g - 1))
                for o in (2 * g, 2 * g + 1):
                    last = self.product3(ps[:, 4 + o % 4, 0:n],
                                         lambda k: self.wh[:, m % 2, k * D + o * P:k * D + (o + 1) * P],
                                         lambda k: self.wl[:, m % 2, k * D + o * P:k * D + (o + 1) * P],
                                         lambda k: hh[:, cs % per, k, :], lambda k: hl[:, cs % per, k, :], 2)
                last.then_inc(down_done, 1)

        def act_up(act, cs, q=None):
            c = cs if q is None else q * per + cs
            if cs >= 1:
                act.wait_ge(h_ready, c)
            act.wait_ge(up_done, c * ups + 1)
            nc.scalar.activation(act_buf[:], ps[:, 0:2, 0:n], ACT.Silu if gated else ACT.Relu).then_inc(r_ready, 1)

        def act_high(act, cs, q=None):
            c = cs if q is None else q * per + cs
            act.wait_ge(h_ready, c + 1)
            if cs >= per:
                act.wait_ge(down_done, c * 4 + 4 * (1 - per))
            nc.scalar.activation(hh[:, cs % per], hid[:], ACT.Copy).then_inc(hh_ready, 1)

        def dve_up(dve, cs, q=None):
            c = cs if q is None else q * per + cs
            dve.wait_ge(r_ready, c + 1)
            dve.wait_ge(up_done, (c + 1) * ups)
            if cs >= 1:
                dve.wait_ge(hid_ready, c)
            if gated:
                ins = nc.vector.tensor_tensor(hid[:], act_buf[:], ps[:, 2:4, 0:n], ALU.mult)
            else:
                ins = nc.vector.scalar_tensor_tensor(hid[:], ps[:, 0:2, 0:n], 0.0, act_buf[:], ALU.max, ALU.mult)
            ins.then_inc(h_ready, 1)

        def dve_low(dve, cs, q=None):
            c = cs if q is None else q * per + cs
            dve.wait_ge(hh_ready, c + 1)
            nc.vector.tensor_tensor(hl[:, cs % per], hid[:], hh[:, cs % per].bitcast(F32),
                                    ALU.subtract).then_inc(hid_ready, 1)

        def dve_add(dve, cs, q=None, groups=range(4)):
            c = cs if q is None else q * per + cs
            for g in groups:
                dve.wait_ge(down_done, c * 4 + (g + 1))
                src, dst = ps[:, 4 + 2 * (g % 2):6 + 2 * (g % 2), 0:n], y[:, 2 * g:2 * g + 2, 0:n]
                if cs == 0:
                    ins = nc.vector.tensor_copy(dst, src)
                else:
                    dve.wait_ge(y_ready, c * 4 + (g - 3))
                    ins = nc.vector.tensor_tensor(dst, src, dst, ALU.add)
                ins.then_inc(y_ready, 1)

        def turn(body, eng):
            for j in range(per):
                body(eng, j, None)
            with eng.Fori(0, (chunks - 1) // per - 1) as q:
                for j in range(per):
                    body(eng, per + j, q)

        assert (chunks - 1) % per == 0

        def split(which, m, q):
            def go(eng):
                (self.split_act if which == "act" else self.split_dve)(eng, m, q)
            return go

        def step(which, up, high_or_low, add):
            def body(eng, cs, q):
                for u in range(1, ups):
                    split(which, m_of["up", cs + 1, u], q)(eng)
                split(which, m_of["down", cs, 0], q)(eng)
                up(eng, cs + 1, q)
                if add:
                    add(eng, cs, q, range(0, 1))
                high_or_low(eng, cs + 1, q)
                if add:
                    add(eng, cs, q, range(1, 2))
                split(which, m_of["down", cs, 0] + 1, q)(eng)
                if add:
                    add(eng, cs, q, range(2, 4))
            return body

        @self.block.tensor
        def _(pe):
            pe_up(pe, 0)

            def body(pe, cs, q):
                pe_up(pe, cs + 1, q)
                pe_down(pe, cs, q)
            turn(body, pe)
            pe_down(pe, chunks - 1)

        @self.block.scalar
        def _(act):
            self.split_upto("act", act, first + ups)
            act_up(act, 0)
            act_high(act, 0)
            turn(step("act", act_up, act_high, None), act)
            self.split_next["act"] = last_m + 1

        @self.block.vector
        def _(dve):
            for w in y_free:
                dve.wait_ge(*w)
            self.split_upto("dve", dve, first + ups)
            dve_up(dve, 0)
            dve_low(dve, 0)
            turn(step("dve", dve_up, dve_low, dve_add), dve)
            dve_add(dve, chunks - 1)
            self.split_next["dve"] = last_m + 1
        tmp.close()
        return [(y_ready, 4 * chunks)]

    def add_feed_forward(self, name, y, y_ready, mod, gate, nv, n):
        nc, ready, half = self.nc, self.sem(f"{name}_added_to_x"), n // nv

        @self.block.vector
        def _(dve):
            for w in y_ready:
                dve.wait_ge(*w)
            for k in range(KD):
                for v in range(nv):
                    x = self.xT[:, k, v * half:(v + 1) * half]
                    last = nc.vector.scalar_tensor_tensor(
                        x, y[:, k, v * half:(v + 1) * half], mod[:, gate + k, v:v + 1], x, ALU.mult, ALU.add)
                last.then_inc(ready, 1)
        return [(ready, KD)]


def tall_offset(q, k):
    return k * PC + (q % 2) * P


def whole_split(pr, scope, name, a, ready, n):
    nc = pr.nc
    pr.presplit()
    high = pr.sb(f"{name}_h", [P, KD, n], F32R, ctx=scope)
    low = pr.sb(f"{name}_l", [P, KD, n], F32R, ctx=scope)
    h_ready, l_ready = pr.sem(f"{name}_high_ready"), pr.sem(f"{name}_split_ready")

    @pr.block.scalar
    def _(act):
        for k in range(KD):
            for w in ready(k) if callable(ready) else ready if k == 0 else []:
                act.wait_ge(*w)
            nc.scalar.activation(high[:, k, :], a[:, k, :], ACT.Copy).then_inc(h_ready, 1)

    @pr.block.vector
    def _(dve):
        for k in range(KD):
            dve.wait_ge(h_ready, k + 1)
            nc.vector.tensor_tensor(low[:, k, :], a[:, k, :], high[:, k, :].bitcast(F32),
                                    ALU.subtract).then_inc(l_ready, 1)
    return high, low, [(l_ready, KD)]


def spread(ap, axis, n):
    shape = list(ap.shape)
    shape.insert(axis, n)
    return ap.unsqueeze(axis).broadcast_to(shape)


def even_mixer(pr, high, low, a_ready, mod, tmp_a, beside):
    nc, ps, c = pr.nc, pr.ps, pr.c
    N = TA
    pa = pr.pa
    pb = pr.pb
    gv = pr.gv
    y = pr.y

    def target(q):
        return (pa[:, q, :] if q < 6 else pb[:, q - 6, :])

    proj = pr.linear("even_in", 7, 2, 14, pr.features(high, low, N, KD, tall_offset),
                     pr.copy_out(target), a_ready, beside=beside, rising=True)
    vals = pr.linear("even_v", 2, 4, 8, pr.tokens(high, low, 4, PC, KD),
                     pr.copy_out(lambda q: gv[:, q % 4, (q // 4) * PC:(q // 4 + 1) * PC]), proj,
                     beside=lambda which, eng, p: beside(which, eng, p + 7))
    tmp_a.close()
    ready = proj + vals

    out_ready = pr.sem("gla_out_ready")
    for d in range(2):
        with ExitStack() as t:
            n = f"gla{d}"
            z = pr.sb(f"{n}_z", [P, 2, N], ctx=t)
            e = pr.sb(f"{n}_e", [P, 2, N], ctx=t)
            cum = pr.sb(f"{n}_cum", [P, 2, N], ctx=t)
            q_dec = pr.sb(f"{n}_q_dec", [P, 2, N], ctx=t)
            k_inv = pr.sb(f"{n}_k_inv", [P, 2, N], ctx=t)
            k_tok = pr.sb(f"{n}_k_tok", [P, 2, 4, P], ctx=t)
            att = pr.sb(f"{n}_att", [P, GLA_HEADS, N], ctx=t)
            states = pr.sb(f"{n}_states", [P, 2, 8, 2 * P], ctx=t)
            g_end = pr.sb(f"{n}_g_end", [P, 2, 8], ctx=t)
            (z_ready, abs_ready, e_ready, l_ready, b_ready, exp_ready, dec_ready, turned, k_ready, u_ready,
             s_ready, a_done, a_out, o_done, zeroed) = (pr.sem(f"{n}_{x}") for x in (
                 "gate_products", "abs_ready", "exp_ready", "log_ready", "cumsum_ready", "decays_ready",
                 "decayed", "turned", "k_tokens_ready", "updates_ready", "states_ready", "scores_done",
                 "scores_out", "outputs_done", "zeroed"))
            k_end = e

            def update(b, ch):
                at = (ch // 2 % 2) * 256
                return ps[:, 4 * b + 2 * (ch % 2) + ch // 4, at:at + 256]

            @pr.block.gpsimd
            def _(pool):
                for w in ready:
                    pool.wait_ge(*w)
                if d:
                    pool.wait_ge(out_ready, GLA_HEADS)
                nc.gpsimd.memset(att[:], 0.0).then_inc(zeroed, 1)
                nc.gpsimd.memset(states[:], 0.0).then_inc(zeroed, 1)

            @pr.block.tensor
            def _(pe):
                for w in ready:
                    pe.wait_ge(*w)
                if d:
                    pe.wait_ge(out_ready, GLA_HEADS)
                for b in range(2):
                    at = d * 256 + b * P
                    last = nc.tensor.matmul(ps[:, b, :], c("gate_up")[32:64, at:at + P], pa[32:64, 5, :],
                                            start=True, stop=True)
                last.then_inc(z_ready, 1)
                pe.wait_ge(dec_ready, 3)
                for h in range(GLA_HEADS):
                    rows = slice(64 * (h % 2), 64 * (h % 2) + 64)
                    for i in range(4):
                        cols = slice(i * P, (i + 1) * P)
                        last = nc.tensor.matmul(ps[:, h, cols], k_inv[rows, h // 2, cols],
                                                q_dec[rows, h // 2, cols], start=True, stop=True)
                    last.then_inc(a_done, 1)
                for b in range(2):
                    for i in range(4):
                        last = nc.tensor.transpose(ps[:, 4 + b, i * P:(i + 1) * P],
                                                   k_end[:, b, i * P:(i + 1) * P], c("ident"))
                    last.then_inc(turned, 1)
                pe.wait_ge(k_ready, 2)
                pe.wait_ge(a_out, GLA_HEADS)
                for b in range(2):
                    for ch in range(8):
                        rows = slice(64 * (ch % 2), 64 * (ch % 2) + 64)
                        last = nc.tensor.matmul(
                            update(b, ch),
                            k_tok[rows, b, ch // 2, :], gv[rows, ch // 2, b * 256:(b + 1) * 256],
                            start=True, stop=True)
                    last.then_inc(u_ready, 1)
                pe.wait_ge(s_ready, 14)
                for h in range(GLA_HEADS):
                    rows = slice(64 * (h % 2), 64 * (h % 2) + 64)
                    for i in range(4):
                        cols = slice(i * P, (i + 1) * P)
                        nc.tensor.matmul(ps[:, h, cols], gv[:, i, h * P:(h + 1) * P], att[:, h, cols],
                                         start=True, stop=False)
                        for ch in (2 * i, 2 * i + 1):
                            cc = slice(ch * CH, (ch + 1) * CH)
                            last = nc.tensor.matmul(ps[:, h, cc],
                                                    states[rows, h // 2, ch, (h % 2) * P:(h % 2 + 1) * P],
                                                    q_dec[rows, h // 2, cc], start=False, stop=(ch == 2 * i + 1))
                    last.then_inc(o_done, 1)

            @pr.block.scalar
            def _(act):
                act.wait_ge(abs_ready, 1)
                nc.scalar.activation(e[:], e[:], ACT.Exp, scale=-1.0).then_inc(e_ready, 1)
                act.wait_ge(e_ready, 1)
                nc.scalar.activation(e[:], e[:], ACT.Ln, bias=1.0).then_inc(l_ready, 1)
                act.wait_ge(b_ready, 2)
                nc.scalar.activation(q_dec[:], z[:] if d else cum[:], ACT.Exp, scale=1.0 / 16).then_inc(exp_ready, 1)
                nc.scalar.activation(k_inv[:], z[:] if d else cum[:], ACT.Exp, scale=-1.0 / 16).then_inc(exp_ready, 1)
                nc.scalar.activation(k_end[:], e[:], ACT.Exp, scale=1.0 / 16).then_inc(exp_ready, 1)
                tot = cum[:].rearrange("p b (c t) -> p b c t", t=CH)[:, :, :, CH - 1]
                nc.scalar.activation(g_end[:], tot, ACT.Exp, scale=1.0 / 16).then_inc(exp_ready, 1)
                for b in range(2):
                    act.wait_ge(turned, b + 1)
                    nc.scalar.activation(k_tok[:, b].rearrange("p i n -> p (i n)"), ps[:, 4 + b, :],
                                         ACT.Copy).then_inc(k_ready, 1)

            @pr.block.vector
            def _(dve):
                ch = pr.dve_chain
                dve.wait_ge(z_ready, 1)
                for b in range(2):
                    bias = c("gate_bias")[:, 2 * d + b:2 * d + b + 1]
                    last = nc.vector.tensor_scalar(z[:, b, :], ps[:, b, :], bias, None, ALU.add)
                ch.then(dve, last)
                nc.vector.scalar_tensor_tensor(e[:], z[:], -1.0, z[:], ALU.mult, ALU.max).then_inc(abs_ready, 1)
                dve.wait_ge(l_ready, 1)
                ch.then(dve, nc.vector.scalar_tensor_tensor(z[:], z[:], 0.0, e[:], ALU.min, ALU.subtract))
                for b in range(2):
                    last = nc.vector.tensor_tensor_scan(cum[:, b, :], c("chunk_start"), z[:, b, :], 0.0,
                                                        ALU.mult, ALU.add)
                ch.then(dve, last)
                blocks = [x.rearrange("p b (c t) -> p (b c) t", t=CH) for x in (cum[:], z[:], e[:])]
                cum_c, z_c, e_c = blocks
                tot = cum_c[:, :, CH - 1:CH].broadcast_to([P, 16, CH])
                if d == 0:
                    nc.vector.tensor_tensor(e_c, tot, cum_c, ALU.subtract).then_inc(b_ready, 2)
                else:
                    ch.then(dve, nc.vector.tensor_tensor(e[:], cum[:], z[:], ALU.subtract))
                    nc.vector.tensor_tensor(z_c, tot, e_c, ALU.subtract).then_inc(b_ready, 2)
                dve.wait_ge(exp_ready, 4)
                nc.vector.scalar_tensor_tensor(q_dec[:], pb[:, 0:2, :], GLA_DK ** -0.5, q_dec[:],
                                               ALU.mult, ALU.mult).then_inc(dec_ready, 1)
                nc.vector.tensor_tensor(k_inv[:], pb[:, 2:4, :], k_inv[:], ALU.mult).then_inc(dec_ready, 1)
                nc.vector.tensor_tensor(k_end[:], pb[:, 2:4, :], k_end[:], ALU.mult).then_inc(dec_ready, 1)
                dve.wait_ge(zeroed, 2)
                mask = c("gla_b" if d else "gla_f").bitcast(U32)
                for h in range(GLA_HEADS):
                    dve.wait_ge(a_done, h + 1)
                    nc.vector.copy_predicated(att[:, h, :].rearrange("p (i n) -> p i n", n=P),
                                              spread(mask, 1, 4),
                                              ps[:, h, :].rearrange("p (i n) -> p i n", n=P)).then_inc(a_out, 1)
                order = [7, 6, 5, 4, 3, 2, 1, 0] if d else [4, 5, 6, 7, 0, 1, 2, 3]
                for b in range(2):
                    dve.wait_ge(u_ready, b + 1)
                    for i in range(7):
                        a, z1 = order[i], order[i + 1]
                        if i:
                            dve.wait_ge(s_ready, 7 * b + i)
                        nc.vector.scalar_tensor_tensor(
                            states[:, b, z1, :], states[:, b, a, :], g_end[:, b, a:a + 1],
                            update(b, a),
                            ALU.mult, ALU.add).then_inc(s_ready, 1)
                for h in range(GLA_HEADS):
                    dve.wait_ge(o_done, h + 1)
                    if d == 0:
                        ins = nc.vector.tensor_copy(y[:, 4 + h, :], ps[:, h, :])
                    else:
                        ins = nc.vector.tensor_tensor(y[:, 4 + h, :], ps[:, h, :], y[:, 4 + h, :], ALU.add)
                    ins.then_inc(out_ready, 1)

    with ExitStack() as t:
        gla = y[:, 4:8, :]
        gla_ready = [(out_ready, 2 * GLA_HEADS)]
        gate_ready, done = pr.sem("gla_gate_ready"), pr.sem("gla_gated")
        r, _, r_ready = pr.rstd(t, "gla_norm", gla, gla_ready, [[0], [1], [2], [3]], N, GLA_DV, c("ones"))

        @pr.block.scalar
        def _(act):
            nc.scalar.activation(pb[:, 4:8, :], pb[:, 4:8, :], ACT.Silu).then_inc(gate_ready, 1)

        @pr.block.vector
        def _(dve):
            for w in r_ready:
                dve.wait_ge(*w)
            pr.dve_chain.then(dve, nc.vector.tensor_tensor(gla, gla, r[:], ALU.mult))
            dve.wait_ge(gate_ready, 1)
            nc.vector.scalar_tensor_tensor(gla, gla, c("gla_o"), pb[:, 4:8, :], ALU.mult, ALU.mult)\
                .then_inc(done, 1)
    pr.pb_scope.close()
    att_ready = mla(pr, pa, y, [(done, 1)])
    return att_ready


def mla(pr, pa, y, ready):
    nc, ps, c = pr.nc, pr.ps, pr.c
    N = TA
    scope = ExitStack()
    qT = pr.sb("mla_q", [P, MLA_HEADS, N], ctx=scope)
    kT = pr.sb("mla_k", [P, MLA_HEADS, N], ctx=scope)
    v = pr.sb("mla_v", [P, 4, 512], ctx=scope)
    kr = pr.sb("mla_k_rope", [P, N], ctx=scope)
    with ExitStack() as t:
        parts = {}
        for name, blocks, norm in (("cq", (0, 3), "q_norm"), ("ckv", (3, 5), "kv_norm")):
            nb = blocks[1] - blocks[0]
            src = pa[:, blocks[0]:blocks[1], :]
            hi = pr.sb(f"{name}_h", [P, nb, N], F32R, ctx=t)
            lo = pr.sb(f"{name}_l", [P, nb, N], F32R, ctx=t)
            with ExitStack() as t2:
                r, a, r_ready = pr.rstd(t2, name, src, ready, [list(range(nb))], N, nb * P, c("ones"))
                a_ready = pr.sem(f"{name}_normed")

                @pr.block.vector
                def _(dve):
                    for w in r_ready:
                        dve.wait_ge(*w)
                    for k in range(nb):
                        nc.vector.scalar_tensor_tensor(a[:, k, :], src[:, k, :], c(norm)[:, k:k + 1], r[:, 0, :],
                                                       ALU.mult, ALU.mult).then_inc(a_ready, 1)
                parts[name] = (hi, lo, pr.split_blocks(name, a, a_ready, hi, lo))
                ready = parts[name][2]
        swapped, kr_ready, k_full = pr.sem("kpe_swapped"), pr.sem("k_rope_ready"), pr.sem("k_rope_in_place")

        @pr.block.tensor
        def _(pe):
            for w in ready:
                pe.wait_ge(*w)
            nc.tensor.matmul(ps[:, 4, 0:TL], c("kpe_swap"), pa[:, 5, 0:TL], start=True, stop=True)\
                .then_inc(swapped, 1)

        @pr.block.vector
        def _(dve):
            r = slice(64, P)
            nc.vector.tensor_copy(kr[r, TL:TA], pa[r, 5, TL:TA])
            pr.dve_chain.then(dve, nc.vector.tensor_tensor(kr[r, 0:TL], pa[r, 5, 0:TL], c("kr_cos")[r, :], ALU.mult))
            dve.wait_ge(swapped, 1)
            pr.dve_chain.then(dve, nc.vector.tensor_tensor(pa[r, 5, 0:TL], ps[r, 4, 0:TL], c("kr_sin")[r, :], ALU.mult))
            nc.vector.tensor_tensor(kr[r, 0:TL], kr[r, 0:TL], pa[r, 5, 0:TL], ALU.add).then_inc(kr_ready, 1)

        @pr.block.gpsimd
        def _(pool):
            pool.wait_ge(kr_ready, 1)
            nc.gpsimd.tensor_copy(kT[64:P, :, :], spread(kr[64:P, :], 1, MLA_HEADS)).then_inc(k_full, 1)
        pr.after_mla = (k_full, 1)

        def q_out(q, which, eng, bank):
            nc.vector.tensor_tensor(qT[:, q, 0:TL], bank[:, 0:TL], c("mla_q"), ALU.mult)
            return nc.vector.tensor_scalar(qT[:, q, TL:TA], bank[:, TL:TA], c("mla_qc"), None, ALU.mult)

        def k_out(q, which, eng, bank):
            if which == "act":
                return nc.scalar.activation(kT[0:64, q, :], bank[0:64, :], ACT.Copy)
            return nc.vector.tensor_copy(kT[0:64, q, :], bank[0:64, :])

        cqh, cql, cq_ready = parts["cq"]
        ckh, ckl, ck_ready = parts["ckv"]
        q_ready = pr.linear("mla_uq", 2, 4, 8, pr.features(cqh, cql, N, 3, lambda q, k: ((q % 4) * 3 + k) * P),
                            q_out, cq_ready, engines=("dve",))
        k_ready = pr.linear("mla_uk", 1, 8, 8, pr.features(ckh, ckl, N, 2, lambda q, k: (q * 2 + k) * P),
                            k_out, ck_ready + q_ready)
        v_ready = pr.linear("mla_uv", 1, 4, 4, pr.tokens(ckh, ckl, 4, 512, 2),
                            pr.copy_out(lambda q: v[:, q, :]), k_ready)
        ready = q_ready + k_ready + v_ready + [(k_full, 1)]

    tasks = [(i, h) for i in range(4) for h in range(MLA_HEADS)]
    with ExitStack() as t:
        att = pr.sb("mla_att", [P, 4, 512], ctx=t)

        def spec(n):
            i, h = tasks[n]
            lo = 0 if i < 2 else TL
            return dict(q=lambda: qT[:, h, i * P:(i + 1) * P], k=lambda: kT[:, h, lo:TA], keys=TA - lo,
                        v=lambda j: v[:, lo // P + j, h * MV:(h + 1) * MV],
                        out=att[:, i, h * MV:(h + 1) * MV])

        done = attention(pr, t, "mla", len(tasks), spec, QK ** -0.5, MV, ready)
        turned, out = pr.sem("mla_out_turned"), pr.sem("mla_out_ready")

        @pr.block.tensor
        def _(pe):
            pe.wait_ge(*done[0])
            for b in range(4):
                for i in range(4):
                    last = nc.tensor.transpose(ps[:, b, i * P:(i + 1) * P], att[:, i, b * P:(b + 1) * P], c("ident"))
                last.then_inc(turned, 1)

        @pr.block.scalar
        def _(act):
            for b in range(4):
                act.wait_ge(turned, b + 1)
                nc.scalar.activation(y[:, b, :], ps[:, b, :], ACT.Copy).then_inc(out, 1)
    scope.close()
    return [(out, 4)]


def attention(pr, scope, name, ntasks, spec, scale, width, ready, mask=None):
    nc, ps, c = pr.nc, pr.ps, pr.c
    keys = max(spec(n)["keys"] for n in range(ntasks))
    prob = pr.sb(f"{name}_prob", [P, 2, keys], ctx=scope)
    prob_t = pr.sb(f"{name}_prob_t", [P, 2, keys], ctx=scope)
    stat = pr.sb(f"{name}_stat", [P, 4, ntasks], ctx=scope)
    logit = pr.sb(f"{name}_logits", [P, 2, keys], ctx=scope) if mask else None
    s_done, m_ready, p_ready, t_done, t_out, o_done, o_out = (pr.sem(f"{name}_{x}") for x in (
        "scores_done", "max_ready", "probs_ready", "turned", "turned_out", "values_done", "values_out"))
    mx, nmx, total, inv = (stat[:, i, :] for i in range(4))

    @pr.block.tensor
    def _(pe):
        for w in ready:
            pe.wait_ge(*w)

        def scores(n):
            s = spec(n)
            if n >= 2:
                pe.wait_ge(p_ready, n - 1)
            nc.tensor.matmul(ps[:, n % 2, 0:s["keys"]], s["q"](), s["k"](), start=True, stop=True)\
                .then_inc(s_done, 1)

        for n in range(min(2, ntasks)):
            scores(n)
        for n in range(ntasks):
            s = spec(n)
            pe.wait_ge(p_ready, n + 1)
            if n >= 2:
                pe.wait_ge(t_out, n - 1)
            for j in range(s["keys"] // P):
                last = nc.tensor.transpose(ps[:, 2 + n % 2, j * P:(j + 1) * P], prob[:, n % 2, j * P:(j + 1) * P],
                                           c("ident"))
            last.then_inc(t_done, 1)
            if n + 2 < ntasks:
                scores(n + 2)
            pe.wait_ge(t_out, n + 1)
            if n >= 2:
                pe.wait_ge(o_out, n - 1)
            for j in range(s["keys"] // P):
                last = nc.tensor.matmul(ps[:, 4 + n % 2, 0:width], prob_t[:, n % 2, j * P:(j + 1) * P], s["v"](j),
                                        start=(j == 0), stop=(j == s["keys"] // P - 1))
            last.then_inc(o_done, 1)

    @pr.block.vector
    def _(dve):
        ch = pr.dve_chain
        for n in range(ntasks + 2):
            if n < ntasks:
                s = spec(n)
                w = s["keys"]
                dve.wait_ge(s_done, n + 1)
                src = ps[:, n % 2, 0:w]
                if mask:
                    if n >= 2:
                        dve.wait_ge(p_ready, n - 1)
                    src = logit[:, n % 2, 0:w]
                    ch.then(dve, nc.vector.scalar_tensor_tensor(src, ps[:, n % 2, 0:w], 1.0, mask(n), ALU.mult,
                                                                ALU.add))
                ch.then(dve, nc.vector.tensor_reduce(mx[:, n:n + 1], src, AX.X, ALU.max))
                nc.vector.tensor_scalar(nmx[:, n:n + 1], mx[:, n:n + 1], -scale, None, ALU.mult).then_inc(m_ready, 1)
            if n >= 2:
                k = n - 2
                dve.wait_ge(p_ready, k + 1)
                ch.then(dve, nc.vector.reciprocal(inv[:, k:k + 1], total[:, k:k + 1]))
                dve.wait_ge(o_done, k + 1)
                nc.vector.tensor_scalar(spec(k)["out"], ps[:, 4 + k % 2, 0:width], inv[:, k:k + 1], None,
                                        ALU.mult).then_inc(o_out, 1)

    @pr.block.scalar
    def _(act):
        for n in range(ntasks + 1):
            if n < ntasks:
                w = spec(n)["keys"]
                act.wait_ge(m_ready, n + 1)
                if n >= 2:
                    act.wait_ge(t_done, n - 1)
                src = logit[:, n % 2, 0:w] if mask else ps[:, n % 2, 0:w]
                nc.scalar.activation(prob[:, n % 2, 0:w], src, ACT.Exp, bias=nmx[:, n:n + 1], scale=scale,
                                     accum_out=total[:, n:n + 1]).then_inc(p_ready, 1)
            if n >= 1:
                k = n - 1
                w = spec(k)["keys"]
                act.wait_ge(t_done, k + 1)
                if k >= 2:
                    act.wait_ge(o_done, k - 1)
                nc.scalar.activation(prob_t[:, k % 2, 0:w], ps[:, 2 + k % 2, 0:w], ACT.Copy).then_inc(t_out, 1)

    return [(o_out, ntasks)]


def odd_mixer(pr, mod, scope, norm_w, ready):
    nc, ps, c = pr.nc, pr.ps, pr.c
    N, H = TA, GDN_HEADS
    ch = pr.dve_chain
    y = pr.sb("odd_y", [P, H, TL], ctx=scope)
    inner = ExitStack()
    gate = pr.sb("odd_gate", [P, H, TL], ctx=inner)
    kT = pr.sb("odd_kT", [P, 4, N], ctx=inner)
    qT = pr.sb("odd_qT", [P, 4, TL], ctx=inner)
    k_tok = pr.sb("odd_k_tok", [P, 4, 512], ctx=inner)
    v_tok = pr.sb("odd_v_tok", [P, 4, 1024], ctx=inner)
    ab = pr.sb("odd_ab", [P, 4, 32], ctx=inner)
    pre_scope = ExitStack()
    pre = pr.sb("odd_conv", [P, 8, N], ctx=pre_scope)
    tmp_a = ExitStack()
    high = pr.sb("a1_h", [P, KD, N], F32R, ctx=tmp_a)
    low = pr.sb("a1_l", [P, KD, N], F32R, ctx=tmp_a)
    a_ready = pr.norm_modulate("norm1_1", norm_w, mod, 2, 0, 8, N, high, low, ready, work=pre,
                               scaled_x=v_tok.rearrange("p i (k n) -> p (i k) n", n=N))

    g_ready = pr.linear("odd_g", 4, 2, 8, pr.features(high, low, TL, KD, tall_offset),
                        pr.copy_out(lambda q: gate[:, q, :]), a_ready)
    ab_ready = pr.linear("odd_ab_in", 1, 4, 4, pr.tokens(high, low, 4, 32, KD),
                         pr.copy_out(lambda q: ab[:, q, :]), g_ready)

    def conv_out(first):
        def evac(q, which, eng, bank):
            tap = lambda n: c("gdn_conv")[:, n * 16 + first + q:n * 16 + first + q + 1]
            src = bank[:, 0:N].rearrange("p (s t) -> p s t", s=2)
            dst = pre[:, q, :].rearrange("p (s t) -> p s t", s=2)
            ch.then(eng, nc.vector.tensor_scalar(dst, src, tap(1), None, ALU.mult))
            ch.then(eng, nc.vector.scalar_tensor_tensor(dst[:, :, 1:TL], src[:, :, 0:TL - 1], tap(0),
                                                        dst[:, :, 1:TL], ALU.mult, ALU.add))
            return nc.vector.scalar_tensor_tensor(dst[:, :, 0:TL - 1], src[:, :, 1:TL], tap(2),
                                                  dst[:, :, 0:TL - 1], ALU.mult, ALU.add)
        return evac

    v_conv = pr.linear("odd_v", 4, 2, 8, pr.features(high, low, N, KD, tall_offset), conv_out(8),
                       ab_ready, engines=("dve",))
    v_act, v_turned, v_ready = pr.sem("odd_v_activated"), pr.sem("odd_v_turned"), pr.sem("odd_v_tokens")

    @pr.block.scalar
    def _(act):
        for q in range(8):
            act.wait_ge(v_conv[0][0], q + 1)
            nc.scalar.activation(pre[:, q, :], pre[:, q, :], ACT.Silu).then_inc(v_act, 1)

    @pr.block.tensor
    def _(pe):
        for q in range(8):
            pe.wait_ge(v_act, q + 1)
            if q >= 2:
                pe.wait_ge(v_ready, q - 1)
            for i in range(4):
                last = nc.tensor.transpose(ps[:, 4 + q % 2, i * P:(i + 1) * P], pre[:, q, i * P:(i + 1) * P],
                                           c("ident"))
            last.then_inc(v_turned, 1)

    @pr.block.vector
    def _(dve):
        for q in range(8):
            dve.wait_ge(v_turned, q + 1)
            nc.vector.tensor_copy(v_tok[:, :, q * P:(q + 1) * P],
                                  ps[:, 4 + q % 2, :].rearrange("p (i n) -> p i n", n=P)).then_inc(v_ready, 1)

    qk_conv = pr.linear("odd_qk", 4, 2, 8, pr.features(high, low, N, KD, tall_offset), conv_out(0),
                        [(v_ready, 8)], engines=("dve",))
    tmp_a.close()
    qk_act = pr.sem("odd_qk_activated")

    @pr.block.scalar
    def _(act):
        act.wait_ge(*qk_conv[0])
        nc.scalar.activation(pre[:], pre[:], ACT.Silu).then_inc(qk_act, 1)

    normed = pr.sem("odd_qk_normed")
    k_turned, kt_ready = pr.sem("odd_k_turned"), pr.sem("odd_k_tokens")
    with ExitStack() as t:
        r, _, r_ready = pr.rstd(t, "odd_k", pre[:, 4:8, :], [(qk_act, 1)], [[0], [1], [2], [3]], N, 1, c("block64"))

        @pr.block.vector
        def _(dve):
            for w in r_ready:
                dve.wait_ge(*w)
            nc.vector.tensor_tensor(kT[:], pre[:, 4:8, :], r[:], ALU.mult).then_inc(normed, 1)

    with ExitStack() as t:
        r, _, r_ready = pr.rstd(t, "odd_q", pre[:, 0:4, 0:TL], [(normed, 1)], [[0], [1], [2], [3]], TL, 1,
                                c("block64"), bank=4)

        @pr.block.vector
        def _(dve):
            for w in r_ready:
                dve.wait_ge(*w)
            nc.vector.scalar_tensor_tensor(qT[:], pre[:, 0:4, 0:TL], GDN_DK ** -0.5, r[:], ALU.mult, ALU.mult)\
                .then_inc(normed, 1)

    @pr.block.tensor
    def _(pe):
        pe.wait_ge(normed, 2)
        for b in range(4):
            for i in range(4):
                last = nc.tensor.transpose(ps[:, b, i * P:(i + 1) * P], kT[:, b, i * P:(i + 1) * P], c("ident"))
            last.then_inc(k_turned, 1)

    @pr.block.vector
    def _(dve):
        for b in range(4):
            dve.wait_ge(k_turned, b + 1)
            nc.vector.tensor_copy(k_tok[:, :, b * P:(b + 1) * P],
                                  ps[:, b, :].rearrange("p (i n) -> p i n", n=P)).then_inc(kt_ready, 1)
    pre_scope.close()

    t = ExitStack()
    la = pr.sb("odd_log_a", [P, 4, 16], ctx=t)
    tmp = pr.sb("odd_gate_tmp", [P, 4, 16], ctx=t)
    beta = pr.sb("odd_beta", [P, 4, 16], ctx=t)
    rate = pr.sb("odd_rate", [P, 16], ctx=t)
    G = pr.sb("odd_g_sum", [P, 4, 16], ctx=t)
    e_g = pr.sb("odd_exp_g", [P, 4, 16], ctx=t)
    e_end = pr.sb("odd_exp_end", [P, 4, 16], ctx=t)
    e_tot = pr.sb("odd_exp_total", [P, 4, 16], ctx=t)
    decay = pr.sb("odd_state_decay", [P, 4, 2, 4], ctx=t)
    abs_ready, exp_ready, ln_ready, la_ready, g_done, g_out, eg_ready, gates = (pr.sem(f"odd_{x}") for x in (
        "abs_ready", "gate_exp", "gate_log", "log_a_ready", "decay_sums", "g_sums_out", "exp_g_ready",
        "gates_ready"))

    @pr.block.vector
    def _(dve):
        for w in ab_ready:
            dve.wait_ge(*w)
        ch.then(dve, nc.vector.tensor_tensor(la[:], ab[:, :, 0:16], spread(c("dt_bias"), 1, 4), ALU.add))
        nc.vector.scalar_tensor_tensor(tmp[:], la[:], -1.0, la[:], ALU.mult, ALU.max).then_inc(abs_ready, 1)
        dve.wait_ge(ln_ready, 1)
        ch.then(dve, nc.vector.scalar_tensor_tensor(la[:], la[:], 0.0, tmp[:], ALU.max, ALU.add))
        nc.vector.scalar_tensor_tensor(la[:], la[:], -1.0, spread(rate[:], 1, 4), ALU.mult, ALU.mult)\
            .then_inc(la_ready, 1)
        dve.wait_ge(g_done, 1)
        g = ps[:, 4, 0:64].rearrange("p (i n) -> p i n", i=4)
        total = ps[:, 4, 64:128].rearrange("p (i n) -> p i n", i=4)
        for d in range(2):
            last = nc.vector.tensor_copy(G[:, :, 8 * d:8 * d + 8],
                                         ps[:, 4, 32 * d:32 * d + 32].rearrange("p (i n) -> p i n", i=4))
        ch.then(dve, last)
        nc.vector.tensor_tensor(e_end[:], total, G[:], ALU.subtract).then_inc(g_out, 1)
        dve.wait_ge(eg_ready, 3)
        tot_v = e_tot[:].rearrange("p i (d r b) -> p i d r b", d=2, r=2)
        for r in range(2):
            rows = slice(64 * r, 64 * r + 64)
            for d in range(2):
                last = nc.vector.tensor_copy(decay[rows, :, d, :], tot_v[rows, :, d, r, :])
        last.then_inc(gates, 1)

    @pr.block.scalar
    def _(act):
        act.wait_ge(normed, 2)
        nc.scalar.activation(rate[:], c("a_log"), ACT.Exp)
        act.wait_ge(abs_ready, 1)
        nc.scalar.activation(tmp[:], tmp[:], ACT.Exp, scale=-1.0).then_inc(exp_ready, 1)
        act.wait_ge(exp_ready, 1)
        nc.scalar.activation(tmp[:], tmp[:], ACT.Ln, bias=1.0).then_inc(ln_ready, 1)
        act.wait_ge(g_out, 1)
        nc.scalar.activation(e_tot[:], ps[:, 4, 64:128].rearrange("p (i n) -> p i n", i=4), ACT.Exp)\
            .then_inc(eg_ready, 1)
        nc.scalar.activation(e_g[:], G[:], ACT.Exp).then_inc(eg_ready, 1)
        nc.scalar.activation(e_end[:], e_end[:], ACT.Exp).then_inc(eg_ready, 1)
        nc.scalar.activation(beta[:], ab[:, :, 16:32], ACT.Sigmoid).then_inc(gates, 1)

    @pr.block.tensor
    def _(pe):
        pe.wait_ge(la_ready, 1)
        for d, tri in enumerate(("tri_f", "tri_b")):
            nc.tensor.matmul(ps[:, 4, 32 * d:32 * d + 32].rearrange("p (i n) -> p i n", i=4), c(tri),
                             la[:, :, 8 * d:8 * d + 8], start=True, stop=True)
        nc.tensor.matmul(ps[:, 4, 64:128].rearrange("p (i n) -> p i n", i=4), c("ones"), la[:],
                         start=True, stop=True).then_inc(g_done, 1)

    big = lambda name: pr.sb(f"odd_{name}", [P, H, P], ctx=t)
    Dt, E, X, Y, T, Dm, QKt, e_row, v_new = (big(x) for x in ("D", "E", "X", "Y", "T", "Dm", "QKt", "e_row", "v_new"))
    q_dec = pr.sb("odd_q_dec", [P, 4, P], ctx=t)
    w_t = pr.sb("odd_w", [P, 4, P], ctx=t)
    keg = pr.sb("odd_keg", [P, H, 64], ctx=t)
    kend = pr.sb("odd_kend", [P, H, 64], ctx=t)
    S = pr.sb("odd_S", [P, 4, P], ctx=t)
    names = ("row_sums", "kk_products", "scores_products", "diffs_ready", "decay_ready", "d_ready", "level_masked",
             "t_products", "t_out", "x_products", "y_products", "x_out", "y_out", "qk_ready", "q_dec_ready",
             "keg_ready", "kend_ready", "w_products", "w_out", "u_products", "v_new_ready", "o_products", "o_out",
             "s_products", "s_ready")
    (row_done, kk_done, qk_done, diff_ready, e_ready, d_ready, dm, t_done, t_out, x_done, y_done, xo, yo,
     qk_ready, qd_ready, keg_ready, kend_ready, w_done, w_out, u_done, vn_ready, o_done, o_out, s_done,
     s_ready) = (pr.sem(f"rule_{x}") for x in names)
    half = lambda buf, a: buf[:, 4 * a:4 * a + 4, :]
    bank = lambda b, n=2: ps[:, b:b + n, :].rearrange("p b (s n) -> p (b s) n", n=P)
    steps = [(0, i) for i in (2, 3, 0, 1)] + [(1, i) for i in (3, 2, 1, 0)]
    lats = 0

    def row_sums(pe, idx):
        d, i = steps[idx]
        for s in range(H):
            last = nc.tensor.matmul(ps[:, s // 4, (s % 4) * P:(s % 4 + 1) * P],
                                    la[:, i, 8 * d + s:8 * d + s + 1].broadcast_to([P, P]),
                                    c("tri_b" if d else "tri_f"), start=True, stop=True)
        last.then_inc(row_done, 1)

    def differences(dve, idx):
        d, i = steps[idx]
        dve.wait_ge(row_done, idx + 1)
        for s in range(H):
            last = nc.vector.tensor_scalar(E[:, s, :], ps[:, s // 4, (s % 4) * P:(s % 4 + 1) * P],
                                           G[:, i, 8 * d + s:8 * d + s + 1], 0.0, ALU.subtract, ALU.min)
        last.then_inc(diff_ready, 1)

    def decays(act, idx):
        before = sum(i < 2 for _, i in steps[:idx])
        act.wait_ge(diff_ready, idx + 1)
        if steps[idx][1] < 2:
            if before:
                act.wait_ge(qd_ready, before)
            nc.scalar.activation(e_row[:], bank(0), ACT.Exp)
        nc.scalar.activation(E[:], E[:], ACT.Exp).then_inc(e_ready, 1)

    for idx, (d, i) in enumerate(steps):
        lat, fresh = i < 2, idx % 4 == 0
        cols = slice(i * P, (i + 1) * P)
        tri = c("tri_b" if d else "tri_f")
        lev = c("lev_b" if d else "lev_f").rearrange("p (l n) -> p l n", n=P)
        gs = slice(8 * d, 8 * d + 8)

        @pr.block.tensor
        def _(pe):
            if idx == 0:
                pe.wait_ge(gates, 2)
                pe.wait_ge(kt_ready, 4)
                row_sums(pe, 0)
            if lats:
                pe.wait_ge(o_out, lats)
            for s in range(H):
                rows, b = slice(64 * (s // 4), 64 * (s // 4) + 64), s % 4
                last = nc.tensor.matmul(ps[:, 2 + s // 4, b * P:(b + 1) * P], kT[rows, b, cols], kT[rows, b, cols],
                                        start=True, stop=True)
            last.then_inc(kk_done, 1)
            if lat:
                for s in range(H):
                    rows, b = slice(64 * (s // 4), 64 * (s // 4) + 64), s % 4
                    last = nc.tensor.matmul(ps[:, 4 + s // 4, b * P:(b + 1) * P], kT[rows, b, cols],
                                            qT[rows, b, cols], start=True, stop=True)
                last.then_inc(qk_done, 1)

            def t_products(n, a):
                pe.wait_ge(dm, n * 2 + (14 * idx + a + 1))
                if not isinstance(n, int) or n:
                    pe.wait_ge(xo, n * 2 + (12 * idx + a - 1))
                    for s in range(4 * a, 4 * a + 4):
                        last = nc.tensor.matmul(ps[:, a, (s % 4) * P:(s % 4 + 1) * P], Dm[:, s, :], X[:, s, :],
                                                start=True, stop=True)
                else:
                    for s in range(4 * a, 4 * a + 4):
                        last = nc.tensor.matmul(ps[:, a, (s % 4) * P:(s % 4 + 1) * P], Dm[:, s, :], c("ident"),
                                                start=True, stop=True)
                last.then_inc(t_done, 1)

            def xy_products(n, a, want_x):
                pe.wait_ge(t_out, n * 2 + (12 * idx + a - 1))
                pe.wait_ge(yo, n * 2 + (14 * idx + a - 1))
                at = lambda s: slice((s % 4) * P, (s % 4 + 1) * P)
                if want_x:
                    for s in range(4 * a, 4 * a + 4):
                        last = nc.tensor.matmul(ps[:, 2 + a, at(s)], Y[:, s, :], T[:, s, :], start=True, stop=True)
                    last.then_inc(x_done, 1)
                for s in range(4 * a, 4 * a + 4):
                    last = nc.tensor.matmul(ps[:, 4 + a, at(s)], T[:, s, :], Y[:, s, :], start=True, stop=True)
                last.then_inc(y_done, 1)

            for a in range(2):
                t_products(0, a)
            with pe.Fori(1, LEVELS - 1) as n:
                for a in range(2):
                    t_products(n, a)
                for a in range(2):
                    xy_products(n, a, True)
            for a in range(2):
                t_products(LEVELS - 1, a)
            for a in range(2):
                xy_products(LEVELS - 1, a, False)
            pe.wait_ge(yo, 14 * idx + 14)
            pe.wait_ge(keg_ready, idx + 1)
            for s in range(H):
                r, b = s // 4, s % 4
                last = nc.tensor.matmul(ps[64 * r:64 * r + 64, 6, b * P:(b + 1) * P], keg[:, s, :], Y[:, s, :],
                                        start=True, stop=True)
            last.then_inc(w_done, 1)
            pe.wait_ge(w_out, idx + 1)
            pe.wait_ge(s_ready, idx + 1)
            for s in range(H):
                r, b = s // 4, s % 4
                h = GDN_ORDER[s]
                dst = ps[:, r, b * P:(b + 1) * P]
                nc.tensor.matmul(dst, Y[:, s, :], v_tok[:, i, h * P:(h + 1) * P], start=True, stop=False)
                last = nc.tensor.matmul(dst, w_t[64 * r:64 * r + 64, b, :], S[64 * r:64 * r + 64, b, :],
                                        start=False, stop=True)
            last.then_inc(u_done, 1)
            pe.wait_ge(vn_ready, idx + 1)
            if idx + 1 < len(steps):
                row_sums(pe, idx + 1)
            if lat:
                pe.wait_ge(qk_ready, lats + 1)
                pe.wait_ge(qd_ready, lats + 1)
                for s in range(H):
                    r, b = s // 4, s % 4
                    rows = slice(64 * r, 64 * r + 64)
                    dst = ps[:, 2 + r, b * P:(b + 1) * P]
                    nc.tensor.matmul(dst, v_new[:, s, :], QKt[:, s, :], start=True, stop=False)
                    last = nc.tensor.matmul(dst, S[rows, b, :], q_dec[rows, b, :], start=False, stop=True)
                last.then_inc(o_done, 1)
            pe.wait_ge(kend_ready, idx + 1)
            for s in range(H):
                r, b = s // 4, s % 4
                last = nc.tensor.matmul(ps[64 * r:64 * r + 64, 7, b * P:(b + 1) * P], kend[:, s, :], v_new[:, s, :],
                                        start=True, stop=True)
            last.then_inc(s_done, 1)

        @pr.block.scalar
        def _(act):
            if idx == 0:
                decays(act, 0)

            def t_copy(n, a):
                act.wait_ge(t_done, n * 2 + (14 * idx + a + 1))
                nc.scalar.activation(half(T, a), bank(a, 1), ACT.Copy).then_inc(t_out, 1)

            with act.Fori(1, LEVELS) as n:
                for a in range(2):
                    t_copy(n, a)
            act.wait_ge(w_done, idx + 1)
            nc.scalar.activation(w_t[:], bank(6, 1), ACT.Copy, scale=-1.0).then_inc(w_out, 1)
            if idx + 1 < len(steps):
                decays(act, idx + 1)

        @pr.block.gpsimd
        def _(pool):
            pool.wait_ge(d_ready, idx + 1)

            def mask(n, a):
                if n:
                    pool.wait_ge(t_done, 14 * idx + 2 * n + a - 1)
                    if n == 1:
                        pool.wait_ge(yo, 14 * idx + a + 1)
                elif idx:
                    pool.wait_ge(t_done, 14 * idx)
                m = lev[:, n:n + 1, :].broadcast_to([P, 4, P])
                nc.gpsimd.tensor_tensor(half(Dm, a), half(Dt, a), m, ALU.mult).then_inc(dm, 1)

            for n in range(LEVELS):
                for a in range(2):
                    mask(n, a)
            kv = k_tok[:, i, :].rearrange("p (b r n) -> p r b n", r=2, n=64)
            for r in range(2):
                if idx:
                    pool.wait_ge(w_done, idx)
                last = nc.gpsimd.tensor_tensor(keg[:, 4 * r:4 * r + 4, :], kv[:, r], spread(
                    e_g[:, i, 8 * d + 4 * r:8 * d + 4 * r + 4], 2, 64), ALU.mult)
            last.then_inc(keg_ready, 1)
            for r in range(2):
                if idx:
                    pool.wait_ge(s_done, idx)
                last = nc.gpsimd.tensor_tensor(kend[:, 4 * r:4 * r + 4, :], kv[:, r], spread(
                    e_end[:, i, 8 * d + 4 * r:8 * d + 4 * r + 4], 2, 64), ALU.mult)
            last.then_inc(kend_ready, 1)

        @pr.block.vector
        def _(dve):
            if fresh:
                if idx:
                    dve.wait_ge(s_ready, idx)
                    dve.wait_ge(s_done, idx)
                nc.vector.memset(S[:], 0.0).then_inc(s_ready, 1)
            if idx == 0:
                differences(dve, 0)
            dve.wait_ge(kk_done, idx + 1)
            dve.wait_ge(e_ready, idx + 1)
            for s in range(H):
                last = nc.vector.scalar_tensor_tensor(Dt[:, s, :], E[:, s, :], beta[:, i, 8 * d + s:8 * d + s + 1],
                                                      ps[:, 2 + s // 4, (s % 4) * P:(s % 4 + 1) * P],
                                                      ALU.mult, ALU.mult)
            last.then_inc(d_ready, 1)
            if lat:
                dve.wait_ge(qk_done, lats + 1)
                ch.then(dve, nc.vector.tensor_tensor(QKt[:], bank(4), E[:], ALU.mult))
                nc.vector.tensor_tensor(QKt[:], QKt[:], spread(tri, 1, H), ALU.mult).then_inc(qk_ready, 1)
                for r in range(2):
                    rows = slice(64 * r, 64 * r + 64)
                    last = nc.vector.tensor_tensor(q_dec[rows, :, :], qT[rows, :, cols],
                                                   e_row[rows, 4 * r:4 * r + 4, :], ALU.mult)
                last.then_inc(qd_ready, 1)
            eye = spread(c("ident"), 1, 4)
            for a in range(2):
                dve.wait_ge(t_done, 14 * idx + a + 1)
                nc.vector.tensor_tensor(half(X, a), eye, bank(a, 1), ALU.subtract).then_inc(xo, 1)
                nc.vector.tensor_tensor(half(Y, a), eye, half(Dm, a), ALU.subtract).then_inc(yo, 1)

            def update(n, a, want_x):
                if want_x:
                    dve.wait_ge(x_done, n * 2 + (10 * idx + a - 1))
                    dve.wait_ge(xo, n * 2 + (12 * idx + a - 1))
                    nc.vector.tensor_tensor(half(X, a), half(X, a), bank(2 + a, 1), ALU.subtract).then_inc(xo, 1)
                dve.wait_ge(y_done, n * 2 + (12 * idx + a - 1))
                dve.wait_ge(yo, n * 2 + (14 * idx + a - 1))
                nc.vector.tensor_tensor(half(Y, a), half(Y, a), bank(4 + a, 1), ALU.subtract).then_inc(yo, 1)

            with dve.Fori(1, LEVELS - 1) as n:
                for a in range(2):
                    update(n, a, True)
            for a in range(2):
                update(LEVELS - 1, a, False)
            dve.wait_ge(u_done, idx + 1)
            b_row = spread(beta[:, i, gs], 2, P)
            nc.vector.tensor_tensor(v_new[:], bank(0), b_row, ALU.mult).then_inc(vn_ready, 1)
            if idx + 1 < len(steps):
                differences(dve, idx + 1)
            if lat:
                dve.wait_ge(o_done, lats + 1)
                for r in range(2):
                    dst = y[:, r::2, cols]
                    if d == 0:
                        last = nc.vector.tensor_copy(dst, bank(2 + r, 1))
                    else:
                        last = nc.vector.tensor_tensor(dst, bank(2 + r, 1), dst, ALU.add)
                last.then_inc(o_out, 1)
            dve.wait_ge(s_done, idx + 1)
            if idx % 4 != 3:
                for b in range(4):
                    last = nc.vector.scalar_tensor_tensor(S[:, b, :], S[:, b, :], decay[:, i, d, b:b + 1],
                                                          ps[:, 7, b * P:(b + 1) * P], ALU.mult, ALU.add)
                last.then_inc(s_ready, 1)
        lats += lat
    pr.after_rule = (kend_ready, len(steps))
    t.close()

    gate_ready, done = pr.sem("odd_gate_ready"), pr.sem("odd_gated")
    with ExitStack() as t:
        @pr.block.scalar
        def _(act):
            nc.scalar.activation(gate[:], gate[:], ACT.Silu).then_inc(gate_ready, 1)

        def gated(dve, _):
            dve.wait_ge(gate_ready, 1)
            dve.wait_ge(o_out, lats)
            ch.then(dve, nc.vector.scalar_tensor_tensor(gate[:], gate[:], c("gdn_o"), y[:], ALU.mult, ALU.mult))

        r, _, r_ready = pr.rstd(t, "odd_norm", y[:], [(o_out, lats), (s_done, len(steps))], [[h] for h in range(H)],
                                TL, GDN_DV, c("ones"), meanwhile=gated)

        @pr.block.vector
        def _(dve):
            for w in r_ready:
                dve.wait_ge(*w)
            for h in range(H):
                nc.vector.tensor_tensor(y[:, h, :], gate[:, h, :], r[:, h, :], ALU.mult).then_inc(done, 1)
    inner.close()
    return y, lambda k: [(done, k + 1)]


def rope_tables(pr, pos_in, cos, sin):
    nc, c, ch = pr.nc, pr.c, pr.dve_chain
    turn = 2.0 * math.pi
    c1 = 6.28125
    c2 = float(np.float32(np.round((turn - c1) * 2.0 ** 20) / 2.0 ** 20))
    c3 = turn - c1 - c2
    magic = 1.5 * 2.0 ** 23
    limit = 3.1415925
    angles_ready, ready = pr.sem("angles_ready"), pr.sem("rope_tables_ready")
    with ExitStack() as t:
        ang = pr.sb("rope_angle", [P, TL], ctx=t)
        k = pr.sb("rope_turns", [P, TL], ctx=t)

        @pr.block.vector
        def _(dve):
            dve.wait_ge(pos_in, 16)
            ch.then(dve, nc.vector.tensor_copy(k[:], pr.pos_sb[:]))
            ch.then(dve, nc.vector.tensor_scalar(ang[:], k[:], c("invf"), None, ALU.mult))
            for dst, quarter in ((sin, 0.0), (cos, 0.25)):
                ch.then(dve, nc.vector.tensor_scalar(k[:], ang[:], 1.0 / turn, quarter, ALU.mult, ALU.add))
                ch.then(dve, nc.vector.tensor_scalar(k[:], k[:], magic, None, ALU.add))
                ch.then(dve, nc.vector.tensor_scalar(k[:], k[:], magic, None, ALU.subtract))
                ch.then(dve, nc.vector.scalar_tensor_tensor(dst[:], k[:], -c1, ang[:], ALU.mult, ALU.add))
                ch.then(dve, nc.vector.scalar_tensor_tensor(dst[:], k[:], -c2, dst[:], ALU.mult, ALU.add))
                ch.then(dve, nc.vector.scalar_tensor_tensor(dst[:], k[:], -c3, dst[:], ALU.mult, ALU.add))
                ch.then(dve, nc.vector.tensor_scalar(dst[:], dst[:], quarter * turn, limit, ALU.add, ALU.min))
                last = nc.vector.tensor_scalar(dst[:], dst[:], -limit, None, ALU.max)
                last.then_inc(angles_ready, 1)

        @pr.block.scalar
        def _(act):
            act.wait_ge(angles_ready, 2)
            nc.scalar.activation(sin[:], sin[:], ACT.Sin).then_inc(ready, 1)
            nc.scalar.activation(cos[:], cos[:], ACT.Sin).then_inc(ready, 1)
    return [(ready, 2)]


def post_add(pr, name, y, y_ready, mod, gate, weight, bank, squares=None):
    nc, ready, normed = pr.nc, pr.sem(f"{name}_added_to_x"), pr.sem(f"{name}_normed")
    with ExitStack() as t:
        r, _, r_ready = pr.rstd(t, name, y, y_ready, [list(range(KD))], TL, D, pr.c("ones"), bank, squares)
        gain = pr.sb(f"{name}_gain", [P, KD], ctx=t)

        @pr.block.vector
        def _(dve):
            nc.vector.tensor_tensor(gain[:], mod[:, gate:gate + KD, 0], weight, ALU.mult)
            for w in r_ready:
                dve.wait_ge(*w)
            for step in range(KD + 1):
                if step < KD:
                    nc.vector.tensor_tensor(y[:, step, :], y[:, step, :], r[:, 0, :], ALU.mult).then_inc(normed, 1)
                if step:
                    k, x = step - 1, pr.xT[:, step - 1, 0:TL]
                    dve.wait_ge(normed, step)
                    nc.vector.scalar_tensor_tensor(x, y[:, k, :], gain[:, k:k + 1], x, ALU.mult,
                                                   ALU.add).then_inc(ready, 1)
    return [(ready, KD)]


def hybrid_mixer(pr, l, mod, y, cos, sin, pre_w, ready):
    nc, ps, c, ch = pr.nc, pr.ps, pr.c, pr.dve_chain
    N = TL
    CQ, KA, QM, OM, KI = 0, 2, 6, 14, 18
    inner = ExitStack()
    pj = pr.sb("mix_proj", [P, 19, N], ctx=inner)
    vt = pr.sb("mix_v", [P, 2, 512], ctx=inner)
    vm = pr.sb("mix_vm", [P, 2, 512], ctx=inner)
    sm = pr.sb("mix_small", [P, 2, 32], ctx=inner)
    qr = pr.sb("mix_q", [P, 8, N], ctx=inner)
    tmp_a = ExitStack()
    high = pr.sb("mix_a_h", [P, KD, N], F32R, ctx=tmp_a)
    low = pr.sb("mix_a_l", [P, KD, N], F32R, ctx=tmp_a)
    a_ready = pr.norm_modulate("mix_pre", pre_w, mod, 1, 0, 8, N, high, low, ready)

    def in_out(q, which, eng, bank):
        dst, src = pj[:, q, :], bank[:, 0:N]
        if which == "act":
            return nc.scalar.activation(dst, src, ACT.Copy)
        b = q - QM
        tap = lambda n: c("conv_w")[:, l * 32 + n * 8 + b:l * 32 + n * 8 + b + 1]
        bias = c("conv_b")[:, l * 8 + b:l * 8 + b + 1]
        ch.then(eng, nc.vector.tensor_scalar(dst, src, tap(3), bias, ALU.mult, ALU.add))
        for back in (1, 2, 3):
            last = nc.vector.scalar_tensor_tensor(dst[:, back:N], src[:, 0:N - back], tap(3 - back),
                                                  dst[:, back:N], ALU.mult, ALU.add)
            if back < 3:
                ch.then(eng, last)
        return last

    who = ["dve" if QM <= q < QM + 8 else "act" for q in range(19)]
    in_ready = pr.linear("mix_in", 10, 2, 19, pr.features(high, low, N, KD, tall_offset), in_out, a_ready,
                         engines=who, rising=True)
    vals = lambda dst: pr.copy_out(lambda q: dst[:, q % 2, (q // 2) * PC:(q // 2 + 1) * PC])
    vt_ready = pr.linear("mix_v_in", 2, 2, 4, pr.tokens(high, low, 2, PC, KD), vals(vt), in_ready)
    vm_ready = pr.linear("mix_vm_in", 2, 2, 4, pr.tokens(high, low, 2, PC, KD), vals(vm), vt_ready)
    sm_ready = pr.linear("mix_small_in", 1, 2, 2, pr.tokens(high, low, 2, 32, KD),
                         pr.copy_out(lambda q: sm[:, q, :]), vm_ready)
    tmp_a.close()
    proj_ready = in_ready + vt_ready + vm_ready + sm_ready

    with ExitStack() as t:
        src = pj[:, CQ:CQ + 2, :]
        r, a, r_ready = pr.rstd(t, "mix_cq", src, proj_ready, [[0, 1]], N, 2 * P, c("ones"))
        hi = pr.sb("mix_cq_h", [P, 2, N], F32R, ctx=t)
        lo = pr.sb("mix_cq_l", [P, 2, N], F32R, ctx=t)
        a_ready = pr.sem("mix_cq_normed")

        @pr.block.vector
        def _(dve):
            for w in r_ready:
                dve.wait_ge(*w)
            for k in range(2):
                nc.vector.scalar_tensor_tensor(a[:, k, :], src[:, k, :], c("q_lat")[:, 2 * l + k:2 * l + k + 1],
                                               r[:, 0, :], ALU.mult, ALU.mult).then_inc(a_ready, 1)
        cq_ready = pr.split_blocks("mix_cq", a, a_ready, hi, lo)
        q_ready = pr.linear("mix_q_up", 1, 8, 8, pr.features(hi, lo, N, 2, lambda q, k: (q * 2 + k) * P),
                            pr.copy_out(lambda q: qr[:, q, :]), cq_ready)

    rotated, rope_ready, qk_act = pr.sem("mix_rotated"), pr.sem("mix_rope_ready"), pr.sem("mix_qk_activated")
    flat = lambda x: x.rearrange("p b n -> p (b n)")
    with ExitStack() as t:
        rot = pr.sb("mix_rot", [P, 13, N], ctx=t)

        @pr.block.tensor
        def _(pe):
            for w in q_ready:
                pe.wait_ge(*w)
            srcs = [pj[:, KA:KA + 2, :], pj[:, KA + 2:KA + 4, :]] + [qr[:, 2 * i:2 * i + 2, :] for i in range(4)]
            for i, src in enumerate(srcs):
                nc.tensor.matmul(ps[:, i, :], c("rot"), flat(src), start=True, stop=True)
            nc.tensor.matmul(ps[:, 6, 0:N], c("rot"), pj[:, KI, :], start=True, stop=True).then_inc(rotated, 1)

        @pr.block.vector
        def _(dve):
            dve.wait_ge(rotated, 1)
            for w in proj_ready:
                dve.wait_ge(*w)
            for w in q_ready:
                dve.wait_ge(*w)
            allb = ps[:, 0:7, :].rearrange("p b n -> p (b n)")[:, 0:13 * N].rearrange("p (b n) -> p b n", n=N)
            ch.then(dve, nc.vector.tensor_tensor(rot[:], allb, spread(sin[:], 1, 13), ALU.mult))
            parts = ((pj[:, KA:KA + 4, :], 0, 4), (qr[:], 4, 8), (pj[:, KI:KI + 1, :], 12, 1))
            for x, at, n in parts:
                ch.then(dve, nc.vector.tensor_tensor(x, x, spread(cos[:], 1, n), ALU.mult))
                nc.vector.tensor_tensor(x, x, rot[:, at:at + n, :], ALU.add).then_inc(rope_ready, 1)

        @pr.block.scalar
        def _(act):
            for w in proj_ready:
                act.wait_ge(*w)
            nc.scalar.activation(pj[:, QM:QM + 8, :], pj[:, QM:QM + 8, :], ACT.Silu).then_inc(qk_act, 1)
            nc.scalar.activation(pj[:, OM:OM + 4, :], pj[:, OM:OM + 4, :], ACT.Sigmoid).then_inc(qk_act, 1)

    t = ExitStack()
    att = pr.sb("mix_att", [P, 2, 512], ctx=t)
    hm = pr.sb("mix_hm", [P, 2, 512], ctx=t)
    amask = pr.sb("mix_mask", [P, 2, N], ctx=t)
    causal = c("causal").rearrange("p (i n) -> p i n", i=2)
    i_done, i_relu, i_added, mask_ready = (pr.sem(f"index_{x}") for x in (
        "products", "relu_out", "added", "mask_ready"))
    with ExitStack() as t2:
        relu = pr.sb("index_relu", [P, 2, N], ctx=t2)
        score = pr.sb("index_score", [P, 2, N], ctx=t2)
        work = pr.sb("index_work", [P, 2, N], ctx=t2)
        top = pr.sb("index_top", [P, 8], ctx=t2)
        w_idx = pr.sb("index_weight", [P, 2, 8], ctx=t2)
        tasks = [(i, h) for i in range(2) for h in range(8)]

        @pr.block.tensor
        def _(pe):
            pe.wait_ge(rope_ready, 3)
            for n, (i, h) in enumerate(tasks):
                rows = slice(64 * (h % 2), 64 * (h % 2) + 64)
                if n >= 4:
                    pe.wait_ge(i_relu, n - 3)
                nc.tensor.matmul(ps[:, n % 4, 0:(i + 1) * P], qr[rows, 4 + h // 2, i * P:(i + 1) * P],
                                 pj[rows, KI, 0:(i + 1) * P], start=True, stop=True).then_inc(i_done, 1)

        @pr.block.scalar
        def _(act):
            act.wait_ge(rope_ready, 3)
            for n, (i, h) in enumerate(tasks):
                w = (i + 1) * P
                act.wait_ge(i_done, n + 1)
                if n >= 2:
                    act.wait_ge(i_added, n - 1)
                nc.scalar.activation(relu[:, n % 2, 0:w], ps[:, n % 4, 0:w], ACT.Relu).then_inc(i_relu, 1)

        @pr.block.vector
        def _(dve):
            ch.then(dve, nc.vector.tensor_scalar(w_idx[:], sm[:, :, 0:8], (8 * 64) ** -0.5, None, ALU.mult))
            for n, (i, h) in enumerate(tasks):
                w = (i + 1) * P
                dve.wait_ge(i_relu, n + 1)
                if h:
                    dve.wait_ge(i_added, n)
                nc.vector.scalar_tensor_tensor(score[:, i, 0:w], relu[:, n % 2, 0:w], w_idx[:, i, h:h + 1],
                                               score[:, i, 0:w] if h else causal[:, i, 0:w],
                                               ALU.mult, ALU.add).then_inc(i_added, 1)
            dve.wait_ge(i_added, len(tasks))
            for i in range(2):
                w = (i + 1) * P
                src = score
                for _ in range(TOPK // 8):
                    ch.then(dve, nc.vector.max(top[:], src[:, i, 0:w]))
                    ch.then(dve, nc.vector.match_replace(work[:, i, 0:w], top[:], src[:, i, 0:w], TAKEN))
                    src = work
                ch.then(dve, nc.vector.tensor_scalar(work[:, i, 0:w], work[:, i, 0:w], -2e38, -NEG, ALU.is_lt,
                                                     ALU.mult))
                nc.vector.scalar_tensor_tensor(amask[:, i, 0:w], work[:, i, 0:w], NEG, causal[:, i, 0:w],
                                               ALU.add, ALU.min).then_inc(mask_ready, 1)

    with ExitStack() as t2:
        def spec(n):
            i, h = n // 8, n % 8
            rows = slice(64 * (h % 2), 64 * (h % 2) + 64)
            return dict(q=lambda: qr[rows, h // 2, i * P:(i + 1) * P], k=lambda: pj[rows, KA + h // 2, 0:(i + 1) * P],
                        keys=(i + 1) * P, v=lambda j: vt[:, j, h * 64:(h + 1) * 64],
                        out=att[:, i, h * 64:(h + 1) * 64])

        def mask(n):
            return amask[:, n // 8, 0:(n // 8 + 1) * P]

        att_done = attention(pr, t2, "mix_att", 16, spec, ATT_D ** -0.5, 64, [(mask_ready, 2)], mask=mask)

    with ExitStack() as t2:
        gates = pr.sb("ml_gates", [P, 6, 2, 4], ctx=t2)
        ig, lf, nlf, tmp, M, B = (gates[:, k] for k in range(6))
        stats = pr.sb("ml_stats", [P, 4, 2, 4], ctx=t2)
        nM, den, em, inv = (stats[:, k] for k in range(4))
        W = pr.sb("ml_weights", [P, 2, 4, N], ctx=t2)
        S = pr.sb("ml_scores", [P, 2, 4, N], ctx=t2)
        St = pr.sb("ml_scores_t", [P, 3, 512], ctx=t2)
        (abs_ready, exp_ready, ln_ready, f_ready, c_done, m_ready, w_ready, s_done, smat, turned, t_out, b_ready,
         em_ready, inv_ready, n_done, hm_ready) = (pr.sem(f"ml_{x}") for x in (
             "abs_ready", "exp_ready", "log_ready", "gates_ready", "row_sums", "max_ready", "weights_ready",
             "scores_done", "weighted", "turned", "turned_out", "m_ready", "floor_ready", "inverse_ready",
             "numerators", "h_ready"))
        free = att_done

        @pr.block.vector
        def _(dve):
            for w in free:
                dve.wait_ge(*w)
            b = lambda name: spread(c(name)[:, 4 * l:4 * l + 4], 1, 2)
            nc.vector.tensor_tensor(ig, sm[:, :, 8:12], b("b_ig"), ALU.add)
            ch.then(dve, nc.vector.tensor_tensor(lf, sm[:, :, 12:16], b("b_fg"), ALU.add))
            nc.vector.scalar_tensor_tensor(tmp, lf, -1.0, lf, ALU.mult, ALU.max).then_inc(abs_ready, 1)
            dve.wait_ge(ln_ready, 1)
            ch.then(dve, nc.vector.scalar_tensor_tensor(lf, lf, 0.0, tmp, ALU.min, ALU.subtract))
            nc.vector.tensor_scalar(nlf, lf, -1.0, None, ALU.mult).then_inc(f_ready, 1)
            dve.wait_ge(c_done, 1)
            row = ps[:, 0:2, :].rearrange("p b (h n) -> p (b h) n", n=N)
            for i in range(2):
                w = (i + 1) * P
                ch.then(dve, nc.vector.tensor_tensor(W[:, i, :, 0:w], row[:, :, 0:w], spread(causal[:, i, 0:w], 1, 4),
                                                     ALU.add))
                ch.then(dve, nc.vector.tensor_reduce(M[:, i], W[:, i, :, 0:w], AX.X, ALU.max))
            ch.then(dve, nc.vector.tensor_scalar(M, M, 0.0, None, ALU.max))
            nc.vector.tensor_scalar(nM, M, -1.0, None, ALU.mult).then_inc(m_ready, 1)
            nc.vector.tensor_tensor(B, M, ps[:, 7, 0:8].rearrange("p (i h) -> p i h", i=2), ALU.add)\
                .then_inc(b_ready, 1)
            for i in range(2):
                w = (i + 1) * P
                dve.wait_ge(s_done, i + 1)
                for h in range(ML_HEADS):
                    dve.wait_ge(w_ready, 4 * i + h + 1)
                    nc.vector.scalar_tensor_tensor(
                        S[:, i, h, 0:w], ps[:, 2 + 2 * i + h // 2, (h % 2) * N:(h % 2) * N + w], ML_D ** -0.5,
                        W[:, i, h, 0:w], ALU.mult, ALU.mult, accum_out=den[:, i, h:h + 1]).then_inc(smat, 1)
            dve.wait_ge(smat, 8)
            ch.then(dve, nc.vector.scalar_tensor_tensor(den, den, -1.0, den, ALU.mult, ALU.max))
            dve.wait_ge(em_ready, 1)
            ch.then(dve, nc.vector.tensor_tensor(den, den, em, ALU.max))
            ch.then(dve, nc.vector.reciprocal(inv, den))
            for i in range(2):
                dve.wait_ge(n_done, i + 1)
                nc.vector.tensor_tensor(hm[:, i, :].rearrange("p (h n) -> p h n", h=4),
                                        ps[:, i, :].rearrange("p (h n) -> p h n", h=4),
                                        spread(inv[:, i], 2, P), ALU.mult).then_inc(hm_ready, 1)

        @pr.block.scalar
        def _(act):
            act.wait_ge(abs_ready, 1)
            nc.scalar.activation(tmp, tmp, ACT.Exp, scale=-1.0).then_inc(exp_ready, 1)
            act.wait_ge(exp_ready, 1)
            nc.scalar.activation(tmp, tmp, ACT.Ln, bias=1.0).then_inc(ln_ready, 1)
            act.wait_ge(m_ready, 1)
            for i in range(2):
                for h in range(ML_HEADS):
                    w = W[:, i, h, 0:(i + 1) * P]
                    nc.scalar.activation(w, w, ACT.Exp, bias=nM[:, i, h:h + 1]).then_inc(w_ready, 1)
            act.wait_ge(b_ready, 1)
            nc.scalar.activation(em, B, ACT.Exp, scale=-1.0).then_inc(em_ready, 1)
            for g, b in enumerate((6, 0, 1)):
                act.wait_ge(turned, g + 1)
                nc.scalar.activation(St[:, g, :], ps[:, b, :], ACT.Copy).then_inc(t_out, 1)

        @pr.block.tensor
        def _(pe):
            pe.wait_ge(f_ready, 1)
            wide = lambda x: x.broadcast_to([P, P])
            for h in range(ML_HEADS):
                at = lambda j: ps[:, h // 2, (h % 2) * N + j * P:(h % 2) * N + (j + 1) * P]
                nc.tensor.matmul(at(0), wide(nlf[:, 0, h:h + 1]), c("tri_f"), start=True, stop=False)
                nc.tensor.matmul(at(0), wide(ig[:, 0, h:h + 1]), c("ident"), start=False, stop=True)
                nc.tensor.matmul(at(1), wide(nlf[:, 1, h:h + 1]), c("tri_f"), start=True, stop=False)
                nc.tensor.matmul(at(1), wide(nlf[:, 0, h:h + 1]), c("ones"), start=False, stop=False)
                nc.tensor.matmul(at(1), wide(ig[:, 1, h:h + 1]), c("ident"), start=False, stop=True)
            nc.tensor.matmul(ps[:, 7, 0:4], c("tri_f"), lf[:, 0], start=True, stop=True)
            nc.tensor.matmul(ps[:, 7, 4:8], c("tri_f"), lf[:, 1], start=True, stop=False)
            nc.tensor.matmul(ps[:, 7, 4:8], c("ones"), lf[:, 0], start=False, stop=True).then_inc(c_done, 1)
            pe.wait_ge(qk_act, 2)
            for i in range(2):
                w = (i + 1) * P
                for h in range(ML_HEADS):
                    last = nc.tensor.matmul(ps[:, 2 + 2 * i + h // 2, (h % 2) * N:(h % 2) * N + w],
                                            pj[:, QM + h, i * P:(i + 1) * P], pj[:, QM + 4 + h, 0:w],
                                            start=True, stop=True)
                last.then_inc(s_done, 1)
            pe.wait_ge(b_ready, 1)
            turns = [(6, 0, 0), (0, 1, 0), (1, 1, 1)]
            for g, (b, i, j) in enumerate(turns):
                pe.wait_ge(smat, 4 * i + 4)
                for h in range(ML_HEADS):
                    last = nc.tensor.transpose(ps[:, b, h * P:(h + 1) * P], S[:, i, h, j * P:(j + 1) * P], c("ident"))
                last.then_inc(turned, 1)
            pe.wait_ge(t_out, 3)
            for i in range(2):
                for h in range(ML_HEADS):
                    dst = ps[:, i, h * P:(h + 1) * P]
                    for j in range(i + 1):
                        last = nc.tensor.matmul(dst, St[:, i + j, h * P:(h + 1) * P], vm[:, j, h * P:(h + 1) * P],
                                                start=(j == 0), stop=(j == i))
                last.then_inc(n_done, 1)

    y_turned, y_out = pr.sem("mix_out_turned"), pr.sem("mix_out_copied")

    @pr.block.tensor
    def _(pe):
        pe.wait_ge(hm_ready, 2)
        for g, src in enumerate((att, hm)):
            for b in range(4):
                for i in range(2):
                    last = nc.tensor.transpose(ps[:, 2 + 2 * g + b // 2, (b % 2) * N + i * P:(b % 2) * N + (i + 1) * P],
                                               src[:, i, b * P:(b + 1) * P], c("ident"))
            last.then_inc(y_turned, 1)

    @pr.block.scalar
    def _(act):
        for g in range(2):
            act.wait_ge(y_turned, g + 1)
            nc.scalar.activation(y[:, 4 * g:4 * g + 4, :],
                                 ps[:, 2 + 2 * g:4 + 2 * g, :].rearrange("p b (h n) -> p (b h) n", n=N),
                                 ACT.Copy).then_inc(y_out, 1)
    t.close()

    done = pr.sem("mix_normed")
    one = [[0], [1], [2], [3]]
    with ExitStack() as t:
        r1, _, r1_ready = pr.rstd(t, "att_norm", y[:, 0:4, :], [(y_out, 2)], one, N, ATT_D, c("block64"))
        r2, _, r2_ready = pr.rstd(t, "ml_norm", y[:, 4:8, :], r1_ready, one, N, ML_D, c("ones"), bank=2)

        @pr.block.vector
        def _(dve):
            for w in r1_ready + r2_ready:
                dve.wait_ge(*w)
            for b in range(4):
                nc.vector.scalar_tensor_tensor(y[:, b, :], y[:, b, :], c("attn_out")[:, 4 * l + b:4 * l + b + 1],
                                               r1[:, b, :], ALU.mult, ALU.mult)
                last = nc.vector.scalar_tensor_tensor(y[:, 4 + b, :], y[:, 4 + b, :],
                                                      c("mlstm_out")[:, 4 * l + b:4 * l + b + 1],
                                                      r2[:, b, :], ALU.mult, ALU.mult)
            ch.then(dve, last)
            nc.vector.tensor_tensor(y[:, 4:8, :], y[:, 4:8, :], pj[:, OM:OM + 4, :], ALU.mult).then_inc(done, 1)
    inner.close()
    return [(done, 1)]


def build(nc, panels, rows, conditions, small, xin, pos, out):
    with ExitStack() as ctx:
        pr = Program(nc, ctx, panels, rows, conditions, small, xin, pos, out)
        const_in, late_in, x_in = (pr.sem(f"{n}_landed") for n in ("constants", "later_constants", "x"))
        ends = [sum(len(p) for p in PLANS[:i + 1]) for i in range(len(PLANS))]
        ada_b = [pr.c("ada_b")[:, l * N_MOD:(l + 1) * N_MOD] for l in range(2)]
        b_mod = [pr.c("b_mod")[:, l * N_MOD:(l + 1) * N_MOD] for l in range(2)]
        norm = lambda name, l: pr.c(name)[:, l * KD:(l + 1) * KD]

        def mixer_out(name, y, ready, mod, nv, n, scope, mod_ready=()):
            with ExitStack() as t:
                high, low, y_split = whole_split(pr, t, name, y[:, :, 0:n], ready, n)
                got = pr.linear(name, 4, 2, 8, pr.features(high, low, n, KD, tall_offset),
                                pr.add_gated(mod, 16, nv, n), y_split, engines=("dve",), after=mod_ready, rising=True)
            scope.close()
            return got

        def mlp(l, mod, nv, n, ready, mod_ready=()):
            with ExitStack() as t:
                y = pr.sb(f"mlp{l}_y", [P, KD, n], ctx=t)
                high = pr.sb(f"mlp{l}_a_h", [P, KD, n], F32R, ctx=t)
                low = pr.sb(f"mlp{l}_a_l", [P, KD, n], F32R, ctx=t)
                a_ready = pr.norm_modulate(f"norm2_{l}", norm("norm2", l), mod, nv, 24, 32, n, high, low,
                                           lambda k: [(ready[0][0], k + 1)], bank=4, scaled_x=y)
                y_ready = pr.feed_forward(f"mlp{l}", D_FF // 256, False, n, high, low, a_ready, y, [])
                return pr.add_feed_forward(f"mlp{l}", y, y_ready + list(mod_ready), mod, 40, nv, n)

        def store(ready, src):
            stored = pr.sem("out_stored")

            @pr.block.sync
            def _(sp):
                for w in ready:
                    sp.wait_ge(*w)
                sp.dma_start(out, src).then_inc(stored, 16)
                sp.wait_ge(stored, 16)

        pair = ExitStack()
        pr.scratch = pr.sb("mod_scratch", [P, D], ctx=pair)

        def layer0():
            mod = pr.mod1[0]
            silu_ready = pr.silu("c", pr.conditions[:, 0:2, :], pr.cond)
            first = ExitStack()
            load, mod_ready = pr.first_modulation("mod1_0a", silu_ready + [(const_in, 16)], mod, ada_b[0], first)

            @pr.block.sync
            def _(sp):
                load(sp, 0)
                sp.dma_start(pr.cst[:, 0:SMALL_FIRST], small[:, 0:SMALL_FIRST]).then_inc(const_in, 16)
                load(sp, 1)
                sp.dma_start(pr.xT[:], xin).then_inc(x_in, 16)
                load(sp, 2)
                load(sp, 3)

            first.close()
            pr.stream(ends[0])
            beside, rest_ready = pr.beside_modulation("mod1_0b", 0, FIRST, 24, 3, silu_ready, mod, ada_b[0])
            ab = ExitStack()
            pr.y = pr.sb("even_y", [P, KD, TA], ctx=ab)
            pr.pa = pr.sb("even_pa", [P, 6, TA], ctx=ab)
            pr.pb_scope = ExitStack()
            pr.pb = pr.sb("even_pb", [P, 8, TA], ctx=pr.pb_scope)
            pr.gv = pr.sb("even_gv", [P, 4, 512], ctx=pr.pb_scope)
            tmp_a = ExitStack()
            high = pr.sb("a0_h", [P, KD, TA], F32R, ctx=tmp_a)
            low = pr.sb("a0_l", [P, KD, TA], F32R, ctx=tmp_a)
            a_ready = pr.norm_modulate("norm1_0", norm("norm1", 0), mod, 2, 0, 8, TA, high, low,
                                       mod_ready + [(x_in, 16)], work=pr.y, scaled_x=pr.pb)
            ready = even_mixer(pr, high, low, a_ready, mod, tmp_a, beside)
            pool_ready = silu_ready + rest_ready + [(const_in, 16), pr.after_mla]
            last_ready = pr.modulation("mod1_0c", 0, FIRST + 24, N_MOD - FIRST - 24, pool_ready, 2, mod, ada_b[0])
            nxt = pr.modulation("mod1_1a", 1, 0, FIRST, last_ready, 2, pr.mod1[1], ada_b[1])
            pr.modulation("mod1_1b", 1, FIRST, 16, nxt, 1, pr.mod1[1], ada_b[1])
            ready = mixer_out("even_out", pr.y, ready, mod, 2, TA, ab, rest_ready)
            mlp(0, mod, 2, TA, ready, last_ready)

        def layer1():
            @pr.block.sync
            def _(sp):
                sp.dma_start(pr.cst[:, SMALL_SHARED:SMALL_SHARED + SMALL_W - SMALL_FIRST],
                             small[:, SMALL_FIRST:]).then_inc(late_in, 16)

            pr.stream(ends[1])
            mod = pr.mod1[1]
            last_ready = pr.modulation("mod1_1c", 1, FIRST + 16, N_MOD - FIRST - 16, [], 1, mod, ada_b[1])
            silu_ready = last_ready + pr.silu("c2", pr.conditions[:, 2:3, :], pr.cond[1:])
            pr.cond.reverse()
            sooner = pr.modulation("mod2_0a", 2, 0, 8, silu_ready, 1, pr.mod2[0], b_mod[0])
            scope = ExitStack()
            y, ready = odd_mixer(pr, mod, scope, norm("norm1", 1), [(late_in, 16)])
            pr.modulation("mod2_0b", 2, 8, FIRST, sooner + [pr.after_rule], 1, pr.mod2[0], b_mod[0])
            ready = mixer_out("odd_out", y, ready, mod, 1, TL, scope)
            ready = mlp(1, mod, 1, TL, ready, last_ready)
            done = pr.sem("final_normed")
            with ExitStack() as t:
                x = pr.xT[:, :, 0:TL]
                r, a, r_ready = pr.rstd(t, "final", x, lambda k: [(ready[0][0], k + 1)], [list(range(KD))], TL, D, pr.c("ones"))

                @pr.block.vector
                def _(dve):
                    for w in r_ready:
                        dve.wait_ge(*w)
                    pr.dve_chain.then(dve, nc.vector.tensor_tensor(x, x, r[:].broadcast_to([P, KD, TL]), ALU.mult))
                    nc.vector.tensor_tensor(x, x, spread(norm("final", 0), 2, TL), ALU.mult).then_inc(done, 1)

        def second(l):
            pr.suffix = f"_{l}"
            pr.stream(ends[2 + l])
            mod = pr.mod2[l]
            ready, half = [], FIRST + 8
            rest_ready = pr.modulation("mod2", 2 + l, half, N_MOD - half, [], 1, mod, b_mod[l])
            if l == 0:
                pr.modulation("mod2_next", 3, 0, half, rest_ready, 1, pr.mod2[1], b_mod[1])
                pos_in = pr.sem("positions_landed")

                @pr.block.scalar
                def _(act):
                    act.dma_start(pr.pos_sb[:], pos).then_inc(pos_in, 16)
                ready += rope_tables(pr, pos_in, pr.cos, pr.sin)
            with ExitStack() as t:
                out_y = pr.sb("mix_out", [P, KD, TL], ctx=t)
                y = pr.sb("mix_y", [P, KD, TL], ctx=t)
                y_ready = hybrid_mixer(pr, l, mod, y, pr.cos, pr.sin, norm("mix_pre", l), ready)
                high, low, y_split = whole_split(pr, t, "mix_y", y[:], y_ready, TL)
                ready = pr.linear("mix_out", 4, 2, 8, pr.features(high, low, TL, KD, tall_offset),
                                  pr.copy_out(lambda q: out_y[:, q, :]), y_split, rising=True)
                (act_out, _), (dve_out, _) = ready
                added = post_add(pr, "mix_post", out_y[:], lambda k: [(act_out if k % 2 else dve_out, k // 2 + 1)],
                                 mod, 16, norm("mix_post", l), 4)
            with ExitStack() as t:
                y = pr.sb("ffn_y", [P, KD, TL], ctx=t)
                high = pr.sb("ffn_a_h", [P, KD, TL], F32R, ctx=t)
                low = pr.sb("ffn_a_l", [P, KD, TL], F32R, ctx=t)
                a_ready = pr.norm_modulate("ffn_pre", norm("ffn_pre", l), mod, 1, 24, 32, TL, high, low,
                                           lambda k: [(added[0][0], k + 1)] + rest_ready, bank=4, scaled_x=y)
                y_ready = pr.feed_forward("ffn", FFN // 256, True, TL, high, low, a_ready, y, [])
                ready = post_add(pr, "ffn_post", y[:], lambda k: [(y_ready[0][0], y_ready[0][1] - 3 + k // 2)],
                                 mod, 40, norm("ffn_post", l), 0, pr.xT[:, :, TL:TA])
            if l == 1:
                store(ready, pr.xT[:, :, 0:TL])

        layers = [layer0, layer1, lambda: second(0), lambda: second(1)]
        for layer in layers:
            with nc.cleanup_on_exit():
                with nc.Block() as pr.block:
                    pr.layer_m = pr.m
                    layer()
            pair.close()
            if layer is layer1:
                pr.pos_sb = pr.sb("positions", [P, TL], I32)
                pr.cos, pr.sin = pr.sb("rope_cos", [P, TL]), pr.sb("rope_sin", [P, TL])


def kernel(**inputs):
    from concourse import bacc
    from concourse.bass_utils import run_bass_kernel_spmd

    x = {name: np.asarray(value) for name, value in inputs.items()}
    residual = np.concatenate([x["x"][0], x["ctx"][0]]).reshape(TA, KD, P).transpose(2, 1, 0)
    arrays = {
        "panels": layout_panels(x),
        "rows": layout_rows(x),
        "conditions": layout_conditions(x),
        "small": layout_small(x),
        "x_features": np.ascontiguousarray(residual),
        "positions": np.ascontiguousarray(np.broadcast_to(x["positions_2"], (P, TL))),
    }
    nc = bacc.Bacc("TRN2", target_bir_lowering=False, num_devices=1)
    args = [nc.dram_tensor(f"{n}_dram", a.shape, mybir.dt.from_np(a.dtype), kind="ExternalInput").ap()
            for n, a in arrays.items()]
    out = nc.dram_tensor("out_dram", (P, KD, TL), F32, kind="ExternalOutput").ap()
    build(nc, *args, out)
    got = run_bass_kernel_spmd(nc, [{f"{n}_dram": a for n, a in arrays.items()}], core_ids=[0])
    return got.results[0]["out_dram"].transpose(2, 1, 0).reshape(1, TL, D)
```
